# Optimizing a Trainium2 kernel written in Bass

```python
import math
import jax
import jax.numpy as jnp
from jax import lax
import numpy as np

D_MODEL = 1024
BATCH = 1
SEQ = 256
DEPTH = 2

GRID_W = 64
CTX_LEN = 256
HEAD_DIM = 64
BRANCH_WIDTH = D_MODEL // 2
N_BRANCH = 4
DIFF_HEADS = BRANCH_WIDTH // (2 * HEAD_DIM)
NA_HEADS = BRANCH_WIDTH // HEAD_DIM
NA_KH = 8
NA_KW = 16
GQA_Q_HEADS = BRANCH_WIDTH // HEAD_DIM
GQA_KV_HEADS = 2
SWA_Q_HEADS = BRANCH_WIDTH // HEAD_DIM
SWA_KV_HEADS = 2
SWA_WINDOW = 128
Q_BLOCK = 128
D_FF = ((8 * D_MODEL // 3 + 255) // 256) * 256
FFN_RES_WEIGHT = 0.5
ROPE_THETA = 10000.0
NORM_EPS = 1e-6
N_MOD = 9

kernel_name = "hybrid_gated_branch_dit_block"

def _segments():
    widths = [
        ("a_q", DIFF_HEADS * 2 * HEAD_DIM), ("a_k", DIFF_HEADS * 2 * HEAD_DIM), ("a_v", DIFF_HEADS * 2 * HEAD_DIM),
        ("b_q", NA_HEADS * HEAD_DIM), ("b_k", NA_HEADS * HEAD_DIM), ("b_v", NA_HEADS * HEAD_DIM),
        ("c_q", GQA_Q_HEADS * HEAD_DIM), ("c_k", GQA_KV_HEADS * HEAD_DIM), ("c_v", GQA_KV_HEADS * HEAD_DIM),
        ("d_q", SWA_Q_HEADS * HEAD_DIM), ("d_k", SWA_KV_HEADS * HEAD_DIM), ("d_v", SWA_KV_HEADS * HEAD_DIM),
    ] + [("gate%d" % i, D_MODEL) for i in range(N_BRANCH)]
    seg, off = {}, 0
    for name, w in widths:
        seg[name] = (off, off + w)
        off += w
    return seg, off

def rms_norm(x, g):
    xf = x.astype(jnp.float32)
    y = xf * lax.rsqrt(jnp.mean(jnp.square(xf), axis=-1, keepdims=True) + NORM_EPS)
    return (y * g.astype(jnp.float32)).astype(x.dtype)

def swiglu(u, wg, wu, wd):
    return (jax.nn.silu(u @ wg) * (u @ wu)) @ wd

def rope_2d_tables(n_tok):
    t = jnp.arange(n_tok, dtype=jnp.int32)
    row = (t // GRID_W).astype(jnp.float32)
    col = (t % GRID_W).astype(jnp.float32)
    n_freq = HEAD_DIM // 4
    inv_freq = ROPE_THETA ** (-jnp.arange(n_freq, dtype=jnp.float32) / n_freq)
    ang = jnp.stack([row[:, None] * inv_freq, col[:, None] * inv_freq], axis=1)
    return jnp.cos(ang), jnp.sin(ang)

def apply_rope_2d(x, cos, sin):
    xf = x.astype(jnp.float32).reshape(x.shape[:-1] + (2, 2, HEAD_DIM // 4))
    x1, x2 = xf[..., 0, :], xf[..., 1, :]
    out = jnp.stack([x1 * cos - x2 * sin, x2 * cos + x1 * sin], axis=-2)
    return out.reshape(x.shape).astype(x.dtype)

def _heads(t, n):
    b, s, _ = t.shape
    return t.reshape(b, s, n, -1).transpose(0, 2, 1, 3)

def _gqa_heads(t, n_kv):
    b, s, _ = t.shape
    return t.reshape(b, s, n_kv, -1, HEAD_DIM).transpose(0, 2, 3, 1, 4)

def _merge(t):
    b, h, s, d = t.shape
    return t.transpose(0, 2, 1, 3).reshape(b, s, h * d)

def _merge_gqa(t):
    b, n, g, s, d = t.shape
    return t.transpose(0, 3, 1, 2, 4).reshape(b, s, n * g * d)

def _diff_split(t):
    b, s, _ = t.shape
    t = t.reshape(b, s, DIFF_HEADS, 2, HEAD_DIM).transpose(3, 0, 2, 1, 4)
    return t[0], t[1]

def _to_blocks(t, axis):
    shp = t.shape
    t = t.reshape(shp[:axis] + (shp[axis] // Q_BLOCK, Q_BLOCK) + shp[axis + 1:])
    return jnp.moveaxis(t, axis, 0)

def _from_blocks(t, axis):
    t = jnp.moveaxis(t, 0, axis)
    shp = t.shape
    return t.reshape(shp[:axis] + (shp[axis] * shp[axis + 1],) + shp[axis + 2:])

def _diff_attend(q1, q2, k1, k2, v, lam):
    scale = HEAD_DIM ** -0.5
    s1 = jnp.einsum('bhqd,bhkd->bhqk', q1, k1).astype(jnp.float32) * scale
    s2 = jnp.einsum('bhqd,bhkd->bhqk', q2, k2).astype(jnp.float32) * scale
    a = jax.nn.softmax(s1, axis=-1) - lam * jax.nn.softmax(s2, axis=-1)
    return jnp.einsum('bhqk,bhkd->bhqd', a.astype(v.dtype), v)

def _mha(q, k, v):
    s = jnp.einsum('bhqd,bhkd->bhqk', q, k).astype(jnp.float32) * HEAD_DIM ** -0.5
    p = jax.nn.softmax(s, axis=-1).astype(v.dtype)
    return jnp.einsum('bhqk,bhkd->bhqd', p, v)

def _gqa_attend(q, k, v, sink_ng=None):
    s = jnp.einsum('bngqd,bnkd->bngqk', q, k).astype(jnp.float32) * HEAD_DIM ** -0.5
    if sink_ng is None:
        p = jax.nn.softmax(s, axis=-1)
    else:
        sk = jnp.broadcast_to(sink_ng[None, :, :, None, None], s.shape[:-1] + (1,))
        p = jax.nn.softmax(jnp.concatenate([s, sk], axis=-1), axis=-1)[..., :-1]
    return jnp.einsum('bngqk,bnkd->bngqd', p.astype(v.dtype), v)

def neighbourhood_attention(q, k, v, k_ctx, v_ctx, rel_bias):
    b, h, s, d = q.shape
    rows = s // GRID_W
    kh, kw = min(NA_KH, rows), min(NA_KW, GRID_W)
    scale = d ** -0.5
    qg = q.reshape(b, h, rows, GRID_W, d)
    kg = k.reshape(b, h, rows, GRID_W, d)
    vg = v.reshape(b, h, rows, GRID_W, d)
    r_idx = jnp.arange(rows, dtype=jnp.int32)
    row_start = jnp.clip(r_idx - kh // 2, 0, rows - kh)
    cq = jnp.arange(GRID_W, dtype=jnp.int32)
    col_idx = jnp.clip(cq - kw // 2, 0, GRID_W - kw)[:, None] + jnp.arange(kw, dtype=jnp.int32)
    col_bias_idx = col_idx - cq[:, None] + (NA_KW - 1)

    def one_row(args):
        q_row, r, r0 = args
        k_slab = lax.dynamic_slice_in_dim(kg, r0, kh, axis=2)
        v_slab = lax.dynamic_slice_in_dim(vg, r0, kh, axis=2)
        k_win = k_slab[:, :, :, col_idx]
        v_win = v_slab[:, :, :, col_idx]
        s_loc = jnp.einsum('bhqd,bhrqkd->bhqrk', q_row, k_win).astype(jnp.float32) * scale
        row_bias_idx = r0 + jnp.arange(kh, dtype=jnp.int32) - r + (NA_KH - 1)
        bias = rel_bias[:, row_bias_idx[None, :, None], col_bias_idx[:, None, :]]
        s_loc = (s_loc + bias.astype(jnp.float32)[None]).reshape(b, h, GRID_W, kh * kw)
        s_ctx = jnp.einsum('bhqd,bhcd->bhqc', q_row, k_ctx).astype(jnp.float32) * scale
        p = jax.nn.softmax(jnp.concatenate([s_loc, s_ctx], axis=-1), axis=-1).astype(v.dtype)
        p_loc = p[..., :kh * kw].reshape(b, h, GRID_W, kh, kw)
        return (jnp.einsum('bhqrk,bhrqkd->bhqd', p_loc, v_win)
                + jnp.einsum('bhqc,bhcd->bhqd', p[..., kh * kw:], v_ctx))

    out = lax.map(one_row, (jnp.moveaxis(qg, 2, 0), r_idx, row_start))
    return jnp.moveaxis(out, 0, 2).reshape(b, h, s, d)

def sliding_window_attention(q, k, v, k_ctx, v_ctx, sink_ng):
    b, n, g, s, d = q.shape
    nb = s // Q_BLOCK
    scale = d ** -0.5
    qb = q.reshape(b, n, g, nb, Q_BLOCK, d)

    def band(t):
        tp = jnp.pad(t.reshape(b, n, nb, Q_BLOCK, d), ((0, 0), (0, 0), (1, 1), (0, 0), (0, 0)))
        return jnp.concatenate([tp[:, :, :-2], tp[:, :, 1:-1], tp[:, :, 2:]], axis=3)

    kb, vb = band(k), band(v)
    qi = jnp.arange(Q_BLOCK, dtype=jnp.int32)
    kj = jnp.arange(3 * Q_BLOCK, dtype=jnp.int32)
    in_window = jnp.abs(kj[None, :] - Q_BLOCK - qi[:, None]) <= SWA_WINDOW
    kpos = (jnp.arange(nb, dtype=jnp.int32)[:, None] - 1) * Q_BLOCK + kj[None, :]
    mask = in_window[None] & ((kpos >= 0) & (kpos < s))[:, None, :]
    s_band = jnp.einsum('bngxqd,bnxkd->bngxqk', qb, kb).astype(jnp.float32) * scale
    s_band = jnp.where(mask, s_band, -jnp.inf)
    s_ctx = jnp.einsum('bngxqd,bncd->bngxqc', qb, k_ctx).astype(jnp.float32) * scale
    s_sink = jnp.broadcast_to(sink_ng[None, :, :, None, None, None], s_ctx.shape[:-1] + (1,))
    p = jax.nn.softmax(jnp.concatenate([s_band, s_ctx, s_sink], axis=-1), axis=-1).astype(v.dtype)
    nk, nc = 3 * Q_BLOCK, k_ctx.shape[2]
    o = (jnp.einsum('bngxqk,bnxkd->bngxqd', p[..., :nk], vb)
         + jnp.einsum('bngxqc,bncd->bngxqd', p[..., nk:nk + nc], v_ctx))
    return o.reshape(b, n, g, s, d)

def token_mixer(u_x, u_c, w_in, w_branch, w_out, diff_lambda, diff_subln, na_bias, qk_gain, sink,
                lam_init, cos, sin, need_ctx):
    seg, _ = _segments()

    def proj(u, name):
        a, bnd = seg[name]
        return u @ w_in[:, a:bnd]

    ys_x, ys_c = [], []

    dl = diff_lambda.astype(jnp.float32)
    lam = jnp.exp(jnp.sum(dl[0] * dl[1])) - jnp.exp(jnp.sum(dl[2] * dl[3])) + lam_init
    q1, q2 = _diff_split(proj(u_x, 'a_q'))
    k1, k2 = _diff_split(proj(u_x, 'a_k'))
    k1c, k2c = _diff_split(proj(u_c, 'a_k'))
    vac = _heads(proj(u_c, 'a_v'), DIFF_HEADS)
    q1, q2 = apply_rope_2d(q1, cos, sin), apply_rope_2d(q2, cos, sin)
    k1_all = jnp.concatenate([apply_rope_2d(k1, cos, sin), k1c], axis=2)
    k2_all = jnp.concatenate([apply_rope_2d(k2, cos, sin), k2c], axis=2)
    va_all = jnp.concatenate([_heads(proj(u_x, 'a_v'), DIFF_HEADS), vac], axis=2)
    o = lax.map(lambda qq: _diff_attend(qq[0], qq[1], k1_all, k2_all, va_all, lam),
                (_to_blocks(q1, 2), _to_blocks(q2, 2)))
    ys_x.append(_merge(rms_norm(_from_blocks(o, 2), diff_subln) * (1.0 - lam_init)))
    if need_ctx:
        q1c, q2c = _diff_split(proj(u_c, 'a_q'))
        oc = _diff_attend(q1c, q2c, k1c, k2c, vac, lam)
        ys_c.append(_merge(rms_norm(oc, diff_subln) * (1.0 - lam_init)))

    kbc = _heads(proj(u_c, 'b_k'), NA_HEADS)
    vbc = _heads(proj(u_c, 'b_v'), NA_HEADS)
    ob = neighbourhood_attention(_heads(proj(u_x, 'b_q'), NA_HEADS), _heads(proj(u_x, 'b_k'), NA_HEADS),
                                 _heads(proj(u_x, 'b_v'), NA_HEADS), kbc, vbc, na_bias)
    ys_x.append(_merge(ob))
    if need_ctx:
        ys_c.append(_merge(_mha(_heads(proj(u_c, 'b_q'), NA_HEADS), kbc, vbc)))

    qc_ = apply_rope_2d(rms_norm(_gqa_heads(proj(u_x, 'c_q'), GQA_KV_HEADS), qk_gain[0]), cos, sin)
    kc_ = apply_rope_2d(rms_norm(_heads(proj(u_x, 'c_k'), GQA_KV_HEADS), qk_gain[1]), cos, sin)
    kcc = rms_norm(_heads(proj(u_c, 'c_k'), GQA_KV_HEADS), qk_gain[1])
    vcc = _heads(proj(u_c, 'c_v'), GQA_KV_HEADS)
    kc_all = jnp.concatenate([kc_, kcc], axis=2)
    vc_all = jnp.concatenate([_heads(proj(u_x, 'c_v'), GQA_KV_HEADS), vcc], axis=2)
    oc_ = lax.map(lambda qb: _gqa_attend(qb, kc_all, vc_all), _to_blocks(qc_, 3))
    ys_x.append(_merge_gqa(_from_blocks(oc_, 3)))
    if need_ctx:
        qcc = rms_norm(_gqa_heads(proj(u_c, 'c_q'), GQA_KV_HEADS), qk_gain[0])
        ys_c.append(_merge_gqa(_gqa_attend(qcc, kcc, vcc)))

    sink_ng = sink.astype(jnp.float32).reshape(SWA_KV_HEADS, SWA_Q_HEADS // SWA_KV_HEADS)
    kdc = _heads(proj(u_c, 'd_k'), SWA_KV_HEADS)
    vdc = _heads(proj(u_c, 'd_v'), SWA_KV_HEADS)
    od = sliding_window_attention(
        apply_rope_2d(_gqa_heads(proj(u_x, 'd_q'), SWA_KV_HEADS), cos, sin),
        apply_rope_2d(_heads(proj(u_x, 'd_k'), SWA_KV_HEADS), cos, sin),
        _heads(proj(u_x, 'd_v'), SWA_KV_HEADS), kdc, vdc, sink_ng)
    ys_x.append(_merge_gqa(od))
    if need_ctx:
        ys_c.append(_merge_gqa(_gqa_attend(_gqa_heads(proj(u_c, 'd_q'), SWA_KV_HEADS), kdc, vdc, sink_ng)))

    def merge_branches(u, ys):
        acc = jax.nn.sigmoid(proj(u, 'gate0')) * (ys[0] @ w_branch[0])
        for i in range(1, N_BRANCH):
            acc = acc + jax.nn.sigmoid(proj(u, 'gate%d' % i)) * (ys[i] @ w_branch[i])
        return acc @ w_out

    y_x = merge_branches(u_x, ys_x)
    y_c = merge_branches(u_c, ys_c) if need_ctx else None
    return y_x, y_c

def _ffn_sublayer(h, mod, k, g_pre, g_post, wg, wu, wd):
    u = rms_norm(h, g_pre) * (1.0 + mod[:, :, 3 * k + 1]) + mod[:, :, 3 * k]
    return h + FFN_RES_WEIGHT * mod[:, :, 3 * k + 2] * rms_norm(swiglu(u, wg, wu, wd), g_post)

def setup_inputs(seed: int = 0) -> dict:
    key = jax.random.key(seed)
    ks = jax.random.split(key, 20)
    _, in_width = _segments()
    f32 = jnp.float32

    def w(k, shape, fan_in, mult=1.0):
        return jax.random.normal(k, shape, f32) * (mult * fan_in ** -0.5)

    def gain(k, shape):
        return 1.0 + 0.05 * jax.random.normal(k, shape, f32)

    return {
        "x": jax.random.normal(ks[0], (BATCH, SEQ, D_MODEL), f32),
        "c": jax.random.normal(ks[1], (BATCH, D_MODEL), f32),
        "ctx": jax.random.normal(ks[2], (BATCH, CTX_LEN, D_MODEL), f32),
        "c_ctx": jax.random.normal(ks[3], (D_MODEL,), f32),
        "w_mod": w(ks[4], (DEPTH, D_MODEL, N_MOD * D_MODEL), D_MODEL, 0.5),
        "b_mod": 0.02 * jax.random.normal(ks[5], (DEPTH, N_MOD * D_MODEL), f32),
        "norm_gain": gain(ks[6], (DEPTH, 6, D_MODEL)),
        "ffn_w_gate": w(ks[7], (DEPTH, 2, D_MODEL, D_FF), D_MODEL),
        "ffn_w_up": w(ks[8], (DEPTH, 2, D_MODEL, D_FF), D_MODEL),
        "ffn_w_down": w(ks[9], (DEPTH, 2, D_FF, D_MODEL), D_FF),
        "w_in": w(ks[10], (DEPTH, D_MODEL, in_width), D_MODEL),
        "w_branch": w(ks[11], (DEPTH, N_BRANCH, BRANCH_WIDTH, D_MODEL), BRANCH_WIDTH),
        "w_out": w(ks[12], (DEPTH, D_MODEL, D_MODEL), D_MODEL),
        "diff_lambda": 0.1 * jax.random.normal(ks[13], (DEPTH, 4, HEAD_DIM), f32),
        "diff_subln": gain(ks[14], (DEPTH, 2 * HEAD_DIM)),
        "na_bias": 0.1 * jax.random.normal(ks[15], (DEPTH, NA_HEADS, 2 * NA_KH - 1, 2 * NA_KW - 1), f32),
        "qk_norm": gain(ks[16], (DEPTH, 2, HEAD_DIM)),
        "sink": 0.5 * jax.random.normal(ks[17], (DEPTH, SWA_Q_HEADS), f32),
    }

def reference(x, c, ctx, c_ctx, w_mod, b_mod, norm_gain, ffn_w_gate, ffn_w_up, ffn_w_down, w_in, w_branch,
              w_out, diff_lambda, diff_subln, na_bias, qk_norm, sink):
    bsz, n_tok, d = x.shape
    cos, sin = rope_2d_tables(n_tok)
    h_x, h_c = x, ctx
    sc, scc = jax.nn.silu(c), jax.nn.silu(c_ctx)
    for l in range(DEPTH):
        last = l == DEPTH - 1
        lam_init = 0.8 - 0.6 * math.exp(-0.3 * l)
        mod_x = (sc @ w_mod[l] + b_mod[l]).reshape(bsz, 1, N_MOD, d)
        mod_c = (scc @ w_mod[l] + b_mod[l]).reshape(1, 1, N_MOD, d)
        g = norm_gain[l]
        h_x = _ffn_sublayer(h_x, mod_x, 0, g[0], g[1], ffn_w_gate[l, 0], ffn_w_up[l, 0], ffn_w_down[l, 0])
        h_c = _ffn_sublayer(h_c, mod_c, 0, g[0], g[1], ffn_w_gate[l, 0], ffn_w_up[l, 0], ffn_w_down[l, 0])
        u_x = rms_norm(h_x, g[2]) * (1.0 + mod_x[:, :, 4]) + mod_x[:, :, 3]
        u_c = rms_norm(h_c, g[2]) * (1.0 + mod_c[:, :, 4]) + mod_c[:, :, 3]
        y_x, y_c = token_mixer(u_x, u_c, w_in[l], w_branch[l], w_out[l], diff_lambda[l], diff_subln[l],
                               na_bias[l], qk_norm[l], sink[l], lam_init, cos, sin, not last)
        h_x = h_x + mod_x[:, :, 5] * rms_norm(y_x, g[3])
        h_x = _ffn_sublayer(h_x, mod_x, 2, g[4], g[5], ffn_w_gate[l, 1], ffn_w_up[l, 1], ffn_w_down[l, 1])
        if not last:
            h_c = h_c + mod_c[:, :, 5] * rms_norm(y_c, g[3])
            h_c = _ffn_sublayer(h_c, mod_c, 2, g[4], g[5], ffn_w_gate[l, 1], ffn_w_up[l, 1], ffn_w_down[l, 1])
    return h_x


_drawn_inputs = setup_inputs


def setup_inputs(seed=0):
    import zlib

    import numpy as np

    out = dict(_drawn_inputs(seed))
    spreads = {}
    factors = {'diff_lambda': 4.549,
     'diff_subln': 2.866,
     'na_bias': 32.311,
     'qk_norm': 8.0,
     'sink': 63.607}
    for name, (base, spread) in spreads.items():
        noise = np.random.default_rng([zlib.crc32(name.encode()), seed]).standard_normal(out[name].shape)
        drawn = base * np.exp(spread * noise) if base else spread * noise
        out[name] = jnp.asarray(drawn.astype(out[name].dtype))
    for name, factor in factors.items():
        out[name] = (out[name] * factor).astype(out[name].dtype)
    return out
```

```python
import math
from contextlib import ExitStack

import numpy as np
import concourse.bass as bass
from concourse import mybir

F32 = mybir.dt.float32
F32R = mybir.dt.float32r
ALU = mybir.AluOpType
ACT = mybir.ActivationFunctionType
AX = mybir.AxisListType

P = 128
D = 1024
DEPTH = 2
S_X = 256
S_C = 256
S_ALL = S_X + S_C
GRID_W = 64
HD = 64
KT = D // P
BW = D // 2
BT = BW // P
FF = ((8 * D // 3 + 255) // 256) * 256
FT = FF // P
N_MOD = 9
MODT = N_MOD * KT
NA_KH, NA_KW = 8, 16
SWA_WINDOW = 128
EPS = 1e-6
SCALE = HD ** -0.5
MASKED = -1e30

UNIT = 8 * P
RAW_SLOTS = 4
SPLIT_SLOTS = 2
DOWN_K = (6, 5, 6, 5)
DOWN_WIDTH = max(DOWN_K) * P
MOD_GROUP = 512

BRANCHES = "ABCD"
N_K = {"A": BT, "B": BT, "C": 1, "D": 1}

SMALL = {}
_at = 0
for _name, _w in (("c", KT * 2), ("b_mod", DEPTH * MODT), ("gain", DEPTH * 6 * KT), ("lam", DEPTH * 4 * HD),
                  ("subln", DEPTH), ("qk_gain", DEPTH * 2), ("sink", DEPTH * 8), ("cos", S_X), ("sin", S_X),
                  ("ident", P), ("pairs", P), ("pick", 2), ("mask", 2 * 2 * P)):
    SMALL[_name] = (_at, _w)
    _at += _w
SMALL_W = _at


def layer_units():
    out = [("mod", MODT // 4 * 4 * P * KT * 4 // (P * UNIT))]
    out = [("mod", N_MOD * D // MOD_GROUP * 4)]
    out += [("up0", 2 * FT), ("down0", 4 * KT)]
    for b in BRANCHES:
        out += [(b + "q", BT), (b + "kv", 2 * N_K[b]), (b + "gate", KT), (b + "mix", BT)]
    out += [("out", KT), ("up2", 2 * FT), ("down2", 4 * KT)]
    return out


def unit_starts():
    at, starts = 0, {}
    for layer in range(DEPTH):
        for name, n in layer_units():
            starts[layer, name] = at
            at += n
    return starts, at


class Signal:

    def __init__(self, sem, base):
        self.sem, self.base = sem, base

    def at(self, k):
        return self.base + k


class Signals:

    def __init__(self, nc, ctx):
        self.nc, self.ctx, self.sems, self.counts = nc, ctx, {}, {}

    def new(self, name, total):
        if name not in self.sems:
            self.sems[name] = self.ctx.enter_context(self.nc.semaphore(name))
            self.counts[name] = 0
        s = Signal(self.sems[name], self.counts[name])
        self.counts[name] += total
        return s


def past(k):
    return not isinstance(k, int) or k > 0


def repeat(eng, count, body):
    body(0)
    if count == 2:
        body(1)
    elif count > 2:
        with eng.Fori(1, count) as i:
            body(i)


def build(nc, tokens, small, weights, na_rows, out, stop=None):
    STARTS, N_UNITS = unit_starts()
    with ExitStack() as ctx:
        start = (nc.sbuf_base + 31) // 32 * 32
        slab = ctx.enter_context(nc.sbuf_tensor("slab", [P, 207 * 256 - 40], F32))
        del slab

        def place(name, shape, dt, at):
            return nc.alloc_sbuf_tensor_at(name, [P] + shape, dt, offset=start + at)

        KB = 1024
        at = 0
        raw = place("raw", [RAW_SLOTS, UNIT], F32, at); at += 16 * KB
        w_high = place("w_high", [SPLIT_SLOTS, 8, P], F32R, at); at += 8 * KB
        w_low = place("w_low", [SPLIT_SLOTS, 8, P], F32R, at); at += 8 * KB
        h = place("h", [KT, S_ALL], F32, at); at += 16 * KB
        u_high = place("u_high", [KT, S_ALL], F32R, at)
        u_low = place("u_low", [KT, S_ALL], F32R, at + 16 * KB)
        y = place("y", [KT, S_ALL], F32, at); at += 32 * KB
        big = at; at += 88 * KB
        acc_at = at; at += 16 * KB
        smalls = place("smalls", [SMALL_W], F32, at); at += (SMALL_W * 4 + 31) // 32 * 32
        mod = place("mod", [MODT, 2], F32, at); at += MODT * 8
        pre = place("pre", [3, KT, 2], F32, at); at += 3 * KT * 8
        post = place("post", [3, KT, 2], F32, at); at += 3 * KT * 8
        sq = place("sq", [2, S_ALL], F32, at); at += 4 * KB
        rstd = place("rstd", [2, S_ALL], F32, at); at += 4 * KB
        tmp = place("tmp", [2, S_ALL], F32, at); at += 4 * KB
        ones = place("ones", [P], F32, at); at += 512
        stat = place("stat", [2, 6, 2], F32, at); at += 96
        lam = place("lam", [8], F32, at); at += 32
        eps = place("eps", [2], F32, at); at += 32
        assert start + at <= nc.sbuf_usable_end, (start + at, nc.sbuf_usable_end)
        hid_high = place("hid_high", [FT, S_ALL], F32R, big)
        hid_low = place("hid_low", [FT, S_ALL], F32R, big + 44 * KB)
        q_high = place("q_high", [BT, S_ALL], F32R, big)
        q_low = place("q_low", [BT, S_ALL], F32R, big + 8 * KB)
        k_high = place("k_high", [BT, S_ALL], F32R, big + 16 * KB)
        k_low = place("k_low", [BT, S_ALL], F32R, big + 24 * KB)
        v_high = place("v_high", [4, BW], F32R, big + 32 * KB)
        v_low = place("v_low", [4, BW], F32R, big + 40 * KB)
        a_high = place("a_high", [KT, S_ALL], F32R, big + 16 * KB)
        a_low = place("a_low", [KT, S_ALL], F32R, big + 32 * KB)
        pt_high = place("pt_high", [2, 4 * P], F32R, big + 48 * KB)
        pt_low = place("pt_low", [2, 4 * P], F32R, big + 52 * KB)
        proj = place("proj", [12, S_ALL], F32, big + 56 * KB)
        prob = place("prob", [2, 2, S_ALL], F32, big + 56 * KB)
        gate = place("gate", [KT, S_ALL], F32, big + 64 * KB)
        diff_out = place("diff_out", [BT, S_ALL], F32, big + 80 * KB)
        rot = place("rot", [4, S_X], F32, big + 80 * KB)
        na_bias = place("na_bias", [2, 2, S_X], F32, big + 84 * KB)
        acc = place("acc", [KT, S_ALL], F32, acc_at)
        silu_g = place("silu_g", [2, S_ALL], F32, acc_at)
        hid = place("hid", [2, S_ALL], F32, acc_at + 4 * KB)
        ssq = place("ssq", [S_ALL], F32, acc_at + 8 * KB)
        mod_row = place("mod_row", [2, MOD_GROUP], F32, acc_at + 8 * KB)
        c_split = place("c_split", [KT, P], F32R, acc_at + 12 * KB)
        silu_c = place("silu_c", [KT, 2], F32, acc_at)

        ps = ctx.enter_context(nc.psum_tensor("ps", [P, 8, 512], F32))

        def sm(name, layer=0, n=1):
            a, w = SMALL[name]
            w //= n
            return smalls[:, a + layer * w:a + (layer + 1) * w]

        def smv(name, layer=0, n=1, pattern=None, **k):
            v = sm(name, layer, n)
            return v.rearrange(pattern, **k) if pattern else v

        ident = sm("ident")
        pairs = sm("pairs")
        gain_of = [smv("gain", l, DEPTH, "p (a k) -> p a k", a=6) for l in range(DEPTH)]
        b_mod_of = [sm("b_mod", l, DEPTH) for l in range(DEPTH)]

        signals = Signals(nc, ctx)
        loaded = signals.new("inputs_loaded", 32)
        landed = [signals.new(f"weights_landed{i}", 0) for i in range(RAW_SLOTS)]
        high_made = signals.new("weights_high_made", 0)
        low_made = signals.new("weights_low_made", 0)
        used = signals.new("weights_used", 0)
        ones_set = signals.new("ones_set", 3)
        stored = signals.new("stored", 0)
        bias_landed = [signals.new(f"bias_landed{i}", 0) for i in range(2)]
        bias_steps = signals.new("scores_biased", 0)

        def fetch(sp, n, width, j):
            if not isinstance(n, int) or n >= RAW_SLOTS:
                sp.wait_ge(low_made.sem, n - RAW_SLOTS + 1)
            src = weights[n, :, 0:width] if isinstance(n, int) else weights[bass.ds(n, 1), :, 0:width].rearrange("a p w -> (a p) w")
            sp.dma_start(raw[:, j, 0:width], src).then_inc(landed[j].sem, 16)

        def split_high(act, n, n0):
            act.wait_ge(landed[n0 % RAW_SLOTS].sem, (n0 // RAW_SLOTS + 1) * 16 + (n - n0) * (16 // RAW_SLOTS))
            if n0 >= SPLIT_SLOTS:
                act.wait_ge(used.sem, n - SPLIT_SLOTS + 1)
            s = n0 % SPLIT_SLOTS
            act.activation(w_high[:, s].rearrange("p a b -> p (a b)"), raw[:, n0 % RAW_SLOTS], ACT.Copy).then_inc(high_made.sem, 1)

        def split_low(dve, n, n0):
            dve.wait_ge(high_made.sem, n + 1)
            s = n0 % SPLIT_SLOTS
            dve.tensor_tensor(w_low[:, s].rearrange("p a b -> p (a b)"), raw[:, n0 % RAW_SLOTS],
                              w_high[:, s].rearrange("p a b -> p (a b)"), ALU.subtract).then_inc(low_made.sem, 1)

        def product(pe, n, n0, outs, x_high, x_low, first=True, last=True, before=None):
            s = n0 % SPLIT_SLOTS
            pe.wait_ge(high_made.sem, n + 1)
            for o, terms in outs:
                for a, (w, x) in enumerate(terms):
                    if before:
                        before(x)
                    pe.matmul(o, w_high[:, s, w], x_high(x), start=first and a == 0, stop=False)
                    pe.matmul(o, w_high[:, s, w], x_low(x), start=False, stop=False)
            pe.wait_ge(low_made.sem, n + 1)
            for o, terms in outs:
                for a, (w, x) in enumerate(terms):
                    done = pe.matmul(o, w_low[:, s, w], x_high(x), start=False, stop=last and a == len(terms) - 1)
            done.then_inc(used.sem, 1)

        def split_next(act_or_dve, f, n, n0):
            if n0 + SPLIT_SLOTS < N_UNITS:
                f(act_or_dve, n + SPLIT_SLOTS, n0 + SPLIT_SLOTS)

        stages = []

        class Stage:
            def tensor(self, pe): pass
            def scalar(self, act): pass
            def vector(self, dve): pass
            def pool(self, pool): pass

        class Modulation(Stage):
            GROUPS = N_MOD * D // MOD_GROUP

            def __init__(self, layer):
                self.l, self.n0 = layer, STARTS[layer, "mod"]
                self.c_silu = signals.new("c_silu", 1)
                self.c_parts = signals.new("c_parts", 3)
                self.row_copied = signals.new("mod_row_copied", self.GROUPS)
                self.turned = signals.new("mod_turned", self.GROUPS)
                self.added = signals.new("mod_added", self.GROUPS)
                self.derived = signals.new("mod_derived", 3)
                self.lam_steps = signals.new("lam_steps", 5)
                self.lam_exp = signals.new("lam_exp", 1)

            def tensor(self, pe):
                pe.wait_ge(self.c_parts.sem, self.c_parts.at(3))

                def two_groups(i):
                    for g in range(2):
                        if isinstance(i, int) and i == 0:
                            pass
                        else:
                            if past(2 * i + g - 1):
                                pe.wait_ge(self.row_copied.sem, self.row_copied.at(2 * i + g - 1))
                        for k2 in range(4):
                            n = self.n0 + 8 * i + 4 * g + k2
                            n0 = self.n0 + 4 * g + k2
                            s = n0 % SPLIT_SLOTS
                            pe.wait_ge(high_made.sem, n + 1)
                            for part, w in ((0, w_high), (1, w_low)):
                                if part:
                                    pe.wait_ge(low_made.sem, n + 1)
                                for a in range(2):
                                    done = pe.matmul(ps[:, g], c_split[:, 2 * k2 + a], w[:, s, 4 * a:4 * a + 4].rearrange("p a b -> p (a b)"),
                                                     start=k2 == 0 and part == 0 and a == 0,
                                                     stop=k2 == 3 and part == 1 and a == 1)
                            done.then_inc(used.sem, 1)
                    for g in range(2):
                        pe.wait_ge(self.row_copied.sem, self.row_copied.at(2 * i + g + 1))
                        if not (isinstance(i, int) and i == 0):
                            if past(2 * i + g - 1):
                                pe.wait_ge(self.added.sem, self.added.at(2 * i + g - 1))
                        for c in range(4):
                            t = pe.matmul(ps[:, 2 + g, 2 * c:2 * c + 2], mod_row[0:4, g, c * P:(c + 1) * P],
                                          smalls[0:4, SMALL["pick"][0]:SMALL["pick"][0] + 2], start=c == 0, stop=c == 3,
                                          skip_group_check=True)
                        t.then_inc(self.turned.sem, 1)
                repeat(pe, self.GROUPS // 2, two_groups)

            def scalar(self, act):
                act.wait_ge(loaded.sem, loaded.at(32))
                act.activation(silu_c[:, :, :], smv("c", pattern="p (k s) -> p k s", s=2), ACT.Silu).then_inc(self.c_silu.sem, 1)
                act.wait_ge(self.lam_steps.sem, self.lam_steps.at(3))
                act.activation(lam[:, 2:4], lam[:, 0:2], ACT.Exp).then_inc(self.lam_exp.sem, 1)

                def two_groups(i):
                    for g in range(2):
                        for k2 in range(4):
                            n, n0 = self.n0 + 8 * i + 4 * g + k2, self.n0 + 4 * g + k2
                            split_next(act, split_high, n, n0)
                            if k2 == 3:
                                act.wait_ge(used.sem, n + 1)
                                if not (isinstance(i, int) and i == 0):
                                    if past(2 * i + g - 1):
                                        act.wait_ge(self.turned.sem, self.turned.at(2 * i + g - 1))
                                act.activation(mod_row[0:4, g], ps[0:4, g], ACT.Copy).then_inc(self.row_copied.sem, 1)
                repeat(act, self.GROUPS // 2, two_groups)

            def vector(self, dve):
                l = self.l
                dve.wait_ge(self.c_silu.sem, self.c_silu.at(1))
                dve.memset(c_split[:, :, :].bitcast(F32), 0.0).then_inc(self.c_parts.sem, 1)
                dve.wait_ge(self.c_parts.sem, self.c_parts.at(1))
                dve.tensor_copy(c_split[:, :, 0:2], silu_c[:, :, :]).then_inc(self.c_parts.sem, 1)
                dve.wait_ge(self.c_parts.sem, self.c_parts.at(2))
                dve.tensor_tensor(c_split[:, :, 2:4], silu_c[:, :, :], c_split[:, :, 0:2], ALU.subtract).then_inc(self.c_parts.sem, 1)
                lam_init = 0.8 - 0.6 * math.exp(-0.3 * l)
                dl = smv("lam", l, DEPTH, "p (a b d) -> p a b d", a=2, b=2)
                prod = tmp[:, 0, 0:2 * HD].rearrange("p (a d) -> p a d", a=2)
                st = self.lam_steps
                dve.tensor_tensor(prod, dl[:, :, 0], dl[:, :, 1], ALU.mult).then_inc(st.sem, 1)
                dve.wait_ge(st.sem, st.at(1))
                dve.tensor_reduce(lam[:, 0:2], prod, AX.X, ALU.add).then_inc(st.sem, 1)
                dve.tensor_scalar(lam[:, 6:7], smv("subln", l, DEPTH), 1.0 - lam_init, None, ALU.mult).then_inc(st.sem, 1)
                dve.wait_ge(self.lam_exp.sem, self.lam_exp.at(1))
                dve.tensor_tensor(lam[:, 4:5], lam[:, 3:4], lam[:, 2:3], ALU.subtract).then_inc(st.sem, 1)
                dve.wait_ge(st.sem, st.at(4))
                dve.tensor_scalar(lam[:, 5:6], lam[:, 4:5], -lam_init, None, ALU.add).then_inc(st.sem, 1)

                def two_groups(i):
                    for g in range(2):
                        for k2 in range(4):
                            n, n0 = self.n0 + 8 * i + 4 * g + k2, self.n0 + 4 * g + k2
                            split_next(dve, split_low, n, n0)
                    for g in range(2):
                        dve.wait_ge(self.turned.sem, self.turned.at(2 * i + g + 1))
                        tiles = bass.ds(4 * (2 * i + g), 4)
                        for s in range(2):
                            put = dve.tensor_tensor(mod[:, tiles, s], ps[:, 2 + g, s:8:2], b_mod_of[l][:, tiles], ALU.add)
                        put.then_inc(self.added.sem, 1)
                repeat(dve, self.GROUPS // 2, two_groups)
                dve.wait_ge(self.added.sem, self.added.at(self.GROUPS))
                for j, weight in enumerate((0.5, 1.0, 0.5)):
                    for s in range(2):
                        m = dve.scalar_tensor_tensor(out=pre[:, j, :, s], in0=mod[:, (3 * j + 1) * KT:(3 * j + 2) * KT, s], scalar=1.0,
                                                     in1=gain_of[l][:, 2 * j], op0=ALU.add, op1=ALU.mult)
                        m = dve.scalar_tensor_tensor(out=post[:, j, :, s], in0=mod[:, (3 * j + 2) * KT:(3 * j + 3) * KT, s], scalar=weight,
                                                     in1=gain_of[l][:, 2 * j + 1], op0=ALU.mult, op1=ALU.mult)
                    m.then_inc(self.derived.sem, 1)
                dve.wait_ge(self.derived.sem, self.derived.at(3))

        def segments(T):
            return [(0, 0, S_X)] + ([(1, S_X, S_ALL)] if T > S_X else [])

        class Norm(Stage):
            def __init__(self, layer, j, T, h_ready):
                self.l, self.j, self.T, self.h_ready = layer, j, T, h_ready
                self.squared = signals.new("norm_squared", KT)
                self.summed = signals.new("norm_summed", KT)
                self.rstd_steps = signals.new("norm_rstd", 2)
                self.scaled = signals.new("norm_scaled", KT)
                self.high = signals.new("u_high_made", KT)
                self.ready = signals.new("u_ready", KT)

            def scalar(self, act):
                T = self.T
                for k in range(KT):
                    if self.h_ready:
                        act.wait_ge(self.h_ready.sem, self.h_ready.at(k + 1))
                    if past(k - 1):
                        act.wait_ge(self.summed.sem, self.summed.at(k - 1))
                    act.activation(sq[:, k % 2, 0:T], h[:, k, 0:T], ACT.Square).then_inc(self.squared.sem, 1)
                make_rstd(act, self.summed, KT, self.rstd_steps, ps[:, 7, 0:T], rstd[:, 0, 0:T], 1.0 / D)
                for k in range(KT):
                    act.wait_ge(self.scaled.sem, self.scaled.at(k + 1))
                    for s, a, b in segments(T):
                        i = act.activation(u_high[:, k, a:b], tmp[:, k % 2, a:b], ACT.Identity,
                                           bias=mod[:, 3 * self.j * KT + k, s:s + 1])
                    i.then_inc(self.high.sem, 1)

            def tensor(self, pe):
                for k in range(KT):
                    pe.wait_ge(self.squared.sem, self.squared.at(k + 1))
                    if self.l == 0 and self.j == 0 and k == 0:
                        pe.wait_ge(ones_set.sem, ones_set.at(1))
                    pe.matmul(ps[:, 7, 0:self.T], ones[:, :], sq[:, k % 2, 0:self.T], start=k == 0, stop=k == KT - 1)\
                        .then_inc(self.summed.sem, 1)

            def vector(self, dve):
                dve.wait_ge(self.rstd_steps.sem, self.rstd_steps.at(2))

                def scale(k):
                    if past(k - 1):
                        dve.wait_ge(self.ready.sem, self.ready.at(k - 1))
                    for s, a, b in segments(self.T):
                        i = dve.scalar_tensor_tensor(out=tmp[:, k % 2, a:b], in0=h[:, k, a:b], scalar=pre[:, self.j, k, s:s + 1],
                                                     in1=rstd[:, 0, a:b], op0=ALU.mult, op1=ALU.mult)
                    i.then_inc(self.scaled.sem, 1)
                scale(0)
                for k in range(KT):
                    if k + 1 < KT:
                        scale(k + 1)
                    dve.wait_ge(self.high.sem, self.high.at(k + 1))
                    for s, a, b in segments(self.T):
                        i = dve.scalar_tensor_tensor(out=u_low[:, k, a:b], in0=tmp[:, k % 2, a:b],
                                                     scalar=mod[:, 3 * self.j * KT + k, s:s + 1],
                                                     in1=u_high[:, k, a:b], op0=ALU.add, op1=ALU.subtract)
                    i.then_inc(self.ready.sem, 1)

        def make_rstd(act, source, count, steps, total, into, scale, step=0):
            act.wait_ge(source.sem, source.at(count))
            act.activation(into, total, ACT.Ln, scale=scale, bias=eps[:, 0:1]).then_inc(steps.sem, 1)
            act.wait_ge(steps.sem, steps.at(step + 1))
            act.activation(into, into, ACT.Exp, scale=-0.5).then_inc(steps.sem, 1)

        class Hidden(Stage):
            def __init__(self, layer, j, T, norm):
                self.n0, self.T, self.norm = STARTS[layer, f"up{j}"], T, norm
                self.silu = signals.new("silu_ready", FT)
                self.steps = signals.new("hidden_steps", 2 * FT)
                self.ready = signals.new("hidden_ready", FT)

            def tensor(self, pe):
                def two_tiles(i):
                    for f in range(2):
                        if past(2 * i + f - 1):
                            pe.wait_ge(self.ready.sem, self.ready.at(2 * i + f - 1))
                        for g in range(2):
                            n0 = self.n0 + 2 * f + g
                            first = isinstance(i, int) and f == 0 and g == 0
                            product(pe, n0 + 4 * i, n0, [(ps[:, 2 * f + g, 0:self.T], [(k, k) for k in range(KT)])],
                                    lambda k: u_high[:, k, 0:self.T], lambda k: u_low[:, k, 0:self.T],
                                    before=(lambda k: pe.wait_ge(self.norm.ready.sem, self.norm.ready.at(k + 1))) if first else None)
                repeat(pe, FT // 2, two_tiles)

            def scalar(self, act):
                def two_tiles(i):
                    for f in range(2):
                        for g in range(2):
                            n0 = self.n0 + 2 * f + g
                            split_next(act, split_high, n0 + 4 * i, n0)
                            if g == 0:
                                if past(2 * i + f - 1):
                                    act.wait_ge(self.ready.sem, self.ready.at(2 * i + f - 1))
                                act.wait_ge(used.sem, n0 + 4 * i + 1)
                                act.activation(silu_g[:, f, 0:self.T], ps[:, 2 * f, 0:self.T], ACT.Silu).then_inc(self.silu.sem, 1)
                repeat(act, FT // 2, two_tiles)

            def vector(self, dve):
                T = self.T

                def two_tiles(i):
                    for f in range(2):
                        t = 2 * i + f
                        for g in range(2):
                            n0 = self.n0 + 2 * f + g
                            split_next(dve, split_low, n0 + 4 * i, n0)
                        dve.wait_ge(used.sem, n0 + 4 * i + 1)
                        dve.wait_ge(self.silu.sem, self.silu.at(t + 1))
                        if past(t - 1):
                            dve.wait_ge(self.ready.sem, self.ready.at(t - 1))
                        dve.tensor_tensor(hid[:, f, 0:T], silu_g[:, f, 0:T], ps[:, 2 * f + 1, 0:T], ALU.mult).then_inc(self.steps.sem, 1)
                        dve.wait_ge(self.steps.sem, self.steps.at(2 * t + 1))
                        dst_h = hid_high[:, bass.ds(t, 1), 0:T].rearrange("p a t -> p (a t)")
                        dst_l = hid_low[:, bass.ds(t, 1), 0:T].rearrange("p a t -> p (a t)")
                        dve.tensor_copy(dst_h, hid[:, f, 0:T]).then_inc(self.steps.sem, 1)
                        dve.wait_ge(self.steps.sem, self.steps.at(2 * t + 2))
                        dve.tensor_tensor(dst_l, hid[:, f, 0:T], dst_h, ALU.subtract).then_inc(self.ready.sem, 1)
                repeat(dve, FT // 2, two_tiles)

        class Result(Stage):
            def result_signals(self):
                self.copied = signals.new("y_squared", KT)
                self.added = signals.new("square_added", KT)

            def take(self, act, m, b):
                T = self.T
                act.activation(y[:, bass.ds(m, 1), 0:T].rearrange("p a t -> p (a t)"), ps[:, b, 0:T], ACT.Copy)
                if past(m - 1):
                    act.wait_ge(self.added.sem, self.added.at(m - 1))
                act.activation(sq[:, b, 0:T], ps[:, b, 0:T], ACT.Square).then_inc(self.copied.sem, 1)

            def add(self, dve, m, b):
                T = self.T
                dve.wait_ge(self.copied.sem, self.copied.at(m + 1))
                if isinstance(m, int) and m == 0:
                    dve.tensor_copy(ssq[:, 0:T], sq[:, b, 0:T]).then_inc(self.added.sem, 1)
                else:
                    if past(m):
                        dve.wait_ge(self.added.sem, self.added.at(m))
                    dve.tensor_tensor(ssq[:, 0:T], ssq[:, 0:T], sq[:, b, 0:T], ALU.add).then_inc(self.added.sem, 1)

        class Down(Result):
            def __init__(self, layer, j, T, hidden):
                self.n0, self.T, self.hidden = STARTS[layer, f"down{j}"], T, hidden
                self.last = self.n0 + 4 * KT == N_UNITS
                self.result_signals()

            def rows(self, eng, body):
                body(0, False)
                with eng.Fori(1, KT // 2 - self.last) as i:
                    body(i, False)
                if self.last:
                    body(KT // 2 - 1, True)

            def tensor(self, pe):
                pe.wait_ge(self.hidden.ready.sem, self.hidden.ready.at(FT))

                def two_rows(i, last):
                    for r in range(2):
                        if past(2 * i + r - 1):
                            pe.wait_ge(self.copied.sem, self.copied.at(2 * i + r - 1))
                        k0 = 0
                        for part, nk in enumerate(DOWN_K):
                            n0 = self.n0 + 4 * r + part
                            product(pe, n0 + 8 * i, n0, [(ps[:, r, 0:self.T], [(w, k0 + w) for w in range(nk)])],
                                    lambda k: hid_high[:, k, 0:self.T], lambda k: hid_low[:, k, 0:self.T],
                                    first=part == 0, last=part == 3)
                            k0 += nk
                self.rows(pe, two_rows)

            def scalar(self, act):
                def two_rows(i, last):
                    for r in range(2):
                        for part in range(4):
                            n0 = self.n0 + 4 * r + part
                            if not (last and r == 1 and part >= 2):
                                split_high(act, n0 + 8 * i + 2, n0 + 2)
                        act.wait_ge(used.sem, n0 + 8 * i + 1)
                        self.take(act, 2 * i + r, r)
                self.rows(act, two_rows)

            def vector(self, dve):
                def two_rows(i, last):
                    for r in range(2):
                        for part in range(4):
                            n0 = self.n0 + 4 * r + part
                            if not (last and r == 1 and part >= 2):
                                split_low(dve, n0 + 8 * i + 2, n0 + 2)
                        self.add(dve, 2 * i + r, r)
                self.rows(dve, two_rows)

        class Residual(Stage):
            def __init__(self, j, T, result):
                self.j, self.T, self.result = j, T, result
                self.summed = signals.new("y_summed", 1)
                self.rstd_steps = signals.new("y_rstd", 2)
                self.scaled = signals.new("y_scaled", KT)
                self.h_ready = signals.new("h_ready", KT)

            def tensor(self, pe):
                pe.wait_ge(self.result.added.sem, self.result.added.at(KT))
                pe.matmul(ps[:, 7, 0:self.T], ones[:, :], ssq[:, 0:self.T], start=True, stop=True).then_inc(self.summed.sem, 1)

            def scalar(self, act):
                make_rstd(act, self.summed, 1, self.rstd_steps, ps[:, 7, 0:self.T], rstd[:, 0, 0:self.T], 1.0 / D)

            def vector(self, dve):
                dve.wait_ge(self.rstd_steps.sem, self.rstd_steps.at(2))

                def scale(k):
                    if past(k - 1):
                        dve.wait_ge(self.h_ready.sem, self.h_ready.at(k - 1))
                    for s, a, b in segments(self.T):
                        i = dve.scalar_tensor_tensor(out=tmp[:, k % 2, a:b], in0=y[:, k, a:b], scalar=post[:, self.j, k, s:s + 1],
                                                     in1=rstd[:, 0, a:b], op0=ALU.mult, op1=ALU.mult)
                    i.then_inc(self.scaled.sem, 1)
                scale(0)
                for k in range(KT):
                    if k + 1 < KT:
                        scale(k + 1)
                    dve.wait_ge(self.scaled.sem, self.scaled.at(k + 1))
                    dve.tensor_tensor(h[:, k, 0:self.T], h[:, k, 0:self.T], tmp[:, k % 2, 0:self.T], ALU.add).then_inc(self.h_ready.sem, 1)

        class Branch(Stage):
            def __init__(self, layer, index, T, norm, before):
                self.before = before
                self.l, self.index, self.b, self.T, self.norm = layer, index, BRANCHES[index], T, norm
                b = self.b
                self.nk = N_K[b]
                self.nq = {w: STARTS[layer, b + w] for w in ("q", "kv", "gate", "mix")}
                self.tiles = BT + 2 * self.nk
                self.roped = b != "B"
                self.normed = b == "C"
                self.prep = [(BT + i, S_ALL, k_high[:, i], k_low[:, i]) for i in range(self.nk)]
                self.prep += [(i, T, q_high[:, i], q_low[:, i]) for i in range(BT)]
                n = len(self.prep)
                self.projected = signals.new("projected", self.tiles)
                self.v_turned = signals.new("v_turned", 4)
                self.v_high = signals.new("v_high_made", 4)
                self.v_low = signals.new("v_low_made", 4)
                self.head_squared = signals.new("head_squared", n if self.normed else 0)
                self.head_summed = signals.new("head_summed", n if self.normed else 0)
                self.head_rstd = signals.new("head_rstd", 2 * n if self.normed else 0)
                self.head_normed = signals.new("head_normed", n if self.normed else 0)
                self.shuffled = signals.new("rope_shuffled", n if self.roped else 0)
                self.sined = signals.new("rope_sine", n if self.roped else 0)
                self.cosined = signals.new("rope_cosine", n if self.roped else 0)
                self.turned = signals.new("rope_added", n if self.roped else 0)
                self.part_high = signals.new("qk_high_made", n)
                self.part_low = signals.new("qk_low_made", n)
                self.gated = signals.new("gate_ready", KT)
                self.steps = [(t, q, 0, S_ALL) for t in range(BT) for q in (0, P)]
                if T > S_X:
                    self.steps += [(t, q, S_X, S_C) for t in range(BT) for q in (S_X, S_X + P)]
                J = len(self.steps)
                self.scored = signals.new("scores_ready", J)
                self.maxed = signals.new("row_max", J)
                self.shifted = signals.new("shift_ready", J)
                self.sunk = signals.new("sink_shifted", J if b == "D" else 0)
                self.expd = signals.new("exp_ready", J)
                self.sums = signals.new("sum_steps", 3 * J)
                self.probs = signals.new("probs_ready", J)
                self.flipped = signals.new("probs_turned", J)
                self.pt_high = signals.new("probs_high_made", J)
                self.pt_low = signals.new("probs_low_made", J)
                self.mixed = signals.new("values_mixed", J)
                self.y_high = signals.new("branch_high_made", J if b != "A" else J + BT)
                self.y_low = signals.new("branch_low_made", J if b != "A" else BT)
                self.sub_squared = signals.new("sub_squared", BT if b == "A" else 0)
                self.sub_summed = signals.new("sub_summed", BT if b == "A" else 0)
                self.sub_rstd = signals.new("sub_rstd", 2 * BT if b == "A" else 0)
                self.sub_scaled = signals.new("sub_scaled", BT if b == "A" else 0)
                self.z_gated = signals.new("branch_gated", KT if index else 0)
                self.merged = signals.new("branch_merged", KT)
                if b in "BD":
                    self.masked = signals.new("scores_biased" if b == "B" else "scores_masked", 8)
                if index == 3:
                    self.a_high = signals.new("merged_high_made", KT)
                    self.a_low = signals.new("merged_low_made", KT)

            def tensor(self, pe):
                b, T = self.b, self.T
                full = [(k, k) for k in range(KT)]

                def project(i, n0, base, W):
                    for c in range(min(4, self.tiles - base)):
                        if past(4 * i + base + c - 3):
                            pe.wait_ge(self.projected.sem, self.projected.at(4 * i + base + c - 3))
                        if self.before and base == 0:
                            if past(KT - 3 + c):
                                pe.wait_ge(self.before.merged.sem, self.before.merged.at(KT - 3 + c))
                        n = n0 + c
                        product(pe, n + 4 * i, n, [(ps[:, c, 0:W], full)], lambda k: u_high[:, k, 0:W], lambda k: u_low[:, k, 0:W],
                                before=(lambda k: pe.wait_ge(self.norm.ready.sem, self.norm.ready.at(k + 1))) if self.index == 0 and base == 0 and c == 0 else None)
                project(0, self.nq["q"], 0, T)
                if self.nk == BT:
                    repeat(pe, 2, lambda i: project(i, self.nq["kv"], BT, S_ALL))
                else:
                    project(0, self.nq["kv"], BT, S_ALL)
                pe.wait_ge(self.projected.sem, self.projected.at(self.tiles))
                for tt in range(4):
                    for c in range(self.nk):
                        v = pe.transpose(ps[:, 4 + tt, c * P:(c + 1) * P], proj[:, BT + self.nk + c, tt * P:(tt + 1) * P], ident)
                    v.then_inc(self.v_turned.sem, 1)
                if self.normed:
                    for i, (slot, W, _, _) in enumerate(self.prep):
                        pe.wait_ge(self.head_squared.sem, self.head_squared.at(i + 1))
                        if past(2 * (i - 4) + 2):
                            pe.wait_ge(self.head_rstd.sem, self.head_rstd.at(2 * (i - 4) + 2))
                        pe.matmul(ps[:, i % 4, 0:W], pairs, sq[:, i % 2, 0:W], start=True, stop=True).then_inc(self.head_summed.sem, 1)
                    pe.wait_ge(self.head_rstd.sem, self.head_rstd.at(2 * len(self.prep)))

                def gates(i):
                    for c in range(4):
                        if past(4 * i + c - 3):
                            pe.wait_ge(self.gated.sem, self.gated.at(4 * i + c - 3))
                        n = self.nq["gate"] + c
                        product(pe, n + 4 * i, n, [(ps[:, c, 0:T], full)], lambda k: u_high[:, k, 0:T], lambda k: u_low[:, k, 0:T])
                repeat(pe, KT // 4, gates)
                pe.wait_ge(self.gated.sem, self.gated.at(KT))
                pe.wait_ge(self.part_low.sem, self.part_low.at(len(self.prep)))
                pe.wait_ge(self.v_low.sem, self.v_low.at(4))
                J = len(self.steps)

                def scores(j):
                    t, q, key, nkeys = self.steps[j]
                    kt = t if self.nk == BT else 0
                    if past(j - 1):
                        pe.wait_ge(self.expd.sem, self.expd.at(j - 1))
                    for s in range(2):
                        rows = slice(s * HD, (s + 1) * HD)
                        o = ps[:, 2 * (j % 2) + s, 0:nkeys]
                        for a, (qq, kk) in enumerate(((q_high, k_high), (q_high, k_low), (q_low, k_high))):
                            m = pe.matmul(o, qq[rows, t, q:q + P], kk[rows, kt, key:key + nkeys], start=a == 0, stop=a == 2)
                    m.then_inc(self.scored.sem, 1)

                def flip(j):
                    nkeys = self.steps[j][3]
                    pe.wait_ge(self.probs.sem, self.probs.at(j + 1))
                    if past(j):
                        pe.wait_ge(self.pt_low.sem, self.pt_low.at(j))
                    for s in range(1 if b == "A" else 2):
                        for c in range(nkeys // P):
                            m = pe.transpose(ps[:, 4 + s, c * P:(c + 1) * P], prob[:, j % 2, s, c * P:(c + 1) * P], ident)
                    m.then_inc(self.flipped.sem, 1)

                def mix(j):
                    t, q, key, nkeys = self.steps[j]
                    vt = t if self.nk == BT else 0
                    pe.wait_ge(self.pt_low.sem, self.pt_low.at(j + 1))
                    free = self.y_high if b == "A" else self.y_low
                    if past(j - 1):
                        pe.wait_ge(free.sem, free.at(j - 1))
                    for s in range(1 if b == "A" else 2):
                        terms = [(c, vv, pp) for c in range(nkeys // P)
                                 for vv, pp in ((v_high, pt_high), (v_high, pt_low), (v_low, pt_high))]
                        for a, (c, vv, pp) in enumerate(terms):
                            m = pe.matmul(ps[:, 6 + j % 2, s * P:(s + 1) * P], vv[:, key // P + c, vt * P:(vt + 1) * P],
                                          pp[:, s, c * P:(c + 1) * P], start=a == 0, stop=a == len(terms) - 1)
                    m.then_inc(self.mixed.sem, 1)
                scores(0)
                for j in range(J):
                    if j + 1 < J:
                        scores(j + 1)
                    flip(j)
                    if j:
                        mix(j - 1)
                mix(J - 1)
                if b == "A":
                    for t in range(BT):
                        pe.wait_ge(self.sub_squared.sem, self.sub_squared.at(t + 1))
                        if past(2 * (t - 2) + 2):
                            pe.wait_ge(self.sub_rstd.sem, self.sub_rstd.at(2 * (t - 2) + 2))
                        pe.matmul(ps[:, 4 + t % 2, 0:T], ones[:, :], sq[:, t % 2, 0:T], start=True, stop=True).then_inc(self.sub_summed.sem, 1)
                    pe.wait_ge(self.y_low.sem, self.y_low.at(BT))
                else:
                    pe.wait_ge(self.y_low.sem, self.y_low.at(J))
                for c in range(BT):
                    if past(2 * c - 2):
                        pe.wait_ge(self.merged.sem, self.merged.at(2 * c - 2))
                    product(pe, self.nq["mix"] + c, self.nq["mix"] + c,
                            [(ps[:, (2 * c + r) % 4, 0:T], [(4 * r + k, k) for k in range(BT)]) for r in range(2)],
                            lambda k: q_high[:, k, 0:T], lambda k: q_low[:, k, 0:T])

            def scalar(self, act):
                b, T = self.b, self.T

                def project(i, n0, base, W):
                    for c in range(min(4, self.tiles - base)):
                        n = n0 + c
                        split_next(act, split_high, n + 4 * i, n)
                        act.wait_ge(used.sem, n + 4 * i + 1)
                        slot = 4 * i + base + c
                        if self.before and base == BT and c == 0 and isinstance(i, int) and i == 0:
                            act.wait_ge(self.before.merged.sem, self.before.merged.at(KT))
                        act.activation(proj[:, bass.ds(slot, 1), 0:W].rearrange("p a t -> p (a t)"), ps[:, c, 0:W], ACT.Copy)\
                            .then_inc(self.projected.sem, 1)
                project(0, self.nq["q"], 0, T)
                if self.nk == BT:
                    repeat(act, 2, lambda i: project(i, self.nq["kv"], BT, S_ALL))
                else:
                    project(0, self.nq["kv"], BT, S_ALL)
                act.wait_ge(self.projected.sem, self.projected.at(self.tiles))

                def v_high_part(tt):
                    act.wait_ge(self.v_turned.sem, self.v_turned.at(tt + 1))
                    act.activation(v_high[:, tt, 0:self.nk * P], ps[:, 4 + tt, 0:self.nk * P], ACT.Copy).then_inc(self.v_high.sem, 1)
                for tt in range(4):
                    v_high_part(tt)
                if self.normed:
                    for i, (slot, W, _, _) in enumerate(self.prep):
                        if past(i - 1):
                            act.wait_ge(self.head_summed.sem, self.head_summed.at(i - 1))
                        act.activation(sq[:, i % 2, 0:W], proj[:, slot, 0:W], ACT.Square).then_inc(self.head_squared.sem, 1)
                        if i:
                            self.head_norm(act, i - 1)
                    self.head_norm(act, len(self.prep) - 1)
                for i, (slot, W, hi, lo) in enumerate(self.prep):
                    if self.roped:
                        act.wait_ge(self.turned.sem, self.turned.at(i + 1))
                    act.activation(hi[:, 0:W], proj[:, slot, 0:W], ACT.Copy).then_inc(self.part_high.sem, 1)

                def gates(i):
                    for c in range(4):
                        n = self.nq["gate"] + c
                        split_next(act, split_high, n + 4 * i, n)
                        if isinstance(i, int) and i == 0 and c == 0:
                            act.wait_ge(self.part_low.sem, self.part_low.at(len(self.prep)))
                        act.wait_ge(used.sem, n + 4 * i + 1)
                        act.activation(gate[:, bass.ds(4 * i + c, 1), 0:T].rearrange("p a t -> p (a t)"), ps[:, c, 0:T], ACT.Sigmoid)\
                            .then_inc(self.gated.sem, 1)
                repeat(act, KT // 4, gates)

                def exps(j):
                    nkeys = self.steps[j][3]
                    act.wait_ge(self.shifted.sem, self.shifted.at(j + 1))
                    if past(j - 1):
                        act.wait_ge(self.flipped.sem, self.flipped.at(j - 1))
                    if b == "D":
                        act.wait_ge(self.sunk.sem, self.sunk.at(j + 1))
                        act.activation(stat[:, j % 2, 4], stat[:, j % 2, 3], ACT.Exp)
                    for s in range(2):
                        e = act.activation(prob[:, j % 2, s, 0:nkeys], ps[:, 2 * (j % 2) + s, 0:nkeys], ACT.Exp,
                                           bias=stat[:, j % 2, 1, s:s + 1], scale=SCALE, accum_out=stat[:, j % 2, 2, s:s + 1])
                    e.then_inc(self.expd.sem, 1)

                def high_of_probs(j):
                    nkeys, ns = self.steps[j][3], 1 if b == "A" else 2
                    act.wait_ge(self.flipped.sem, self.flipped.at(j + 1))
                    if past(j):
                        act.wait_ge(self.mixed.sem, self.mixed.at(j))
                    act.activation(pt_high[:, 0:ns, 0:nkeys], ps[:, 4:4 + ns, 0:nkeys], ACT.Copy).then_inc(self.pt_high.sem, 1)

                def high_of_out(j):
                    t, q, _, _ = self.steps[j]
                    act.wait_ge(self.mixed.sem, self.mixed.at(j + 1))
                    if b == "A":
                        o = act.activation(diff_out[:, t, q:q + P], ps[:, 6 + j % 2, 0:P], ACT.Copy)
                    else:
                        for s in range(2):
                            rows = slice(s * HD, (s + 1) * HD)
                            o = act.activation(q_high[rows, t, q:q + P], ps[rows, 6 + j % 2, s * P:(s + 1) * P], ACT.Copy)
                    o.then_inc(self.y_high.sem, 1)
                J = len(self.steps)
                exps(0)
                for j in range(J):
                    if j + 1 < J:
                        exps(j + 1)
                    if j:
                        high_of_out(j - 1)
                    high_of_probs(j)
                high_of_out(J - 1)
                if b == "A":
                    act.wait_ge(self.y_high.sem, self.y_high.at(J))
                    for t in range(BT):
                        if past(t - 1):
                            act.wait_ge(self.sub_summed.sem, self.sub_summed.at(t - 1))
                        act.activation(sq[:, t % 2, 0:T], diff_out[:, t, 0:T], ACT.Square).then_inc(self.sub_squared.sem, 1)
                    for t in range(BT):
                        if past(t - 1):
                            act.wait_ge(self.sub_scaled.sem, self.sub_scaled.at(t - 1))
                        make_rstd(act, self.sub_summed, t + 1, self.sub_rstd, ps[:, 4 + t % 2, 0:T], rstd[:, t % 2, 0:T], 1.0 / P, 2 * t)
                    for t in range(BT):
                        act.wait_ge(self.sub_scaled.sem, self.sub_scaled.at(t + 1))
                        act.activation(q_high[:, t, 0:T], diff_out[:, t, 0:T], ACT.Copy).then_inc(self.y_high.sem, 1)
                for c in range(BT):
                    split_next(act, split_high, self.nq["mix"] + c, self.nq["mix"] + c)
                if self.index == 3:
                    for m in range(KT):
                        act.wait_ge(self.merged.sem, self.merged.at(m + 1))
                        act.activation(a_high[:, m, 0:T], acc[:, m, 0:T], ACT.Copy).then_inc(self.a_high.sem, 1)

            def head_norm(self, act, i):
                slot, W, _, _ = self.prep[i]
                if past(i - 1):
                    act.wait_ge(self.head_normed.sem, self.head_normed.at(i - 1))
                make_rstd(act, self.head_summed, i + 1, self.head_rstd, ps[:, i % 4, 0:W], rstd[:, i % 2, 0:W], 1.0 / HD, 2 * i)

            def vector(self, dve):
                b, T = self.b, self.T

                def project(i, n0, base):
                    for c in range(min(4, self.tiles - base)):
                        split_next(dve, split_low, n0 + c + 4 * i, n0 + c)
                project(0, self.nq["q"], 0)
                if self.nk == BT:
                    repeat(dve, 2, lambda i: project(i, self.nq["kv"], BT))
                else:
                    project(0, self.nq["kv"], BT)
                for tt in range(4):
                    dve.wait_ge(self.v_high.sem, self.v_high.at(tt + 1))
                    w = self.nk * P
                    dve.tensor_tensor(v_low[:, tt, 0:w], ps[:, 4 + tt, 0:w], v_high[:, tt, 0:w], ALU.subtract).then_inc(self.v_low.sem, 1)
                if self.normed:
                    for i, (slot, W, hi, lo) in enumerate(self.prep):
                        dve.wait_ge(self.head_rstd.sem, self.head_rstd.at(2 * i + 2))
                        g = smv("qk_gain", self.l, DEPTH)[:, (1 if slot >= BT else 0):(2 if slot >= BT else 1)]
                        dve.scalar_tensor_tensor(out=proj[:, slot, 0:W], in0=proj[:, slot, 0:W], scalar=g, in1=rstd[:, i % 2, 0:W],
                                                 op0=ALU.mult, op1=ALU.mult).then_inc(self.head_normed.sem, 1)
                    dve.wait_ge(self.head_normed.sem, self.head_normed.at(len(self.prep)))
                else:
                    dve.wait_ge(self.projected.sem, self.projected.at(self.tiles))
                for i, (slot, W, hi, lo) in enumerate(self.prep):
                    x = proj[:, slot, 0:S_X]
                    if self.roped:
                        if past(i - 3):
                            dve.wait_ge(self.turned.sem, self.turned.at(i - 3))
                        r = rot[:, i % 4]
                        dve.stream_shuffle(r, x, [(p + 16) % 32 for p in range(32)]).then_inc(self.shuffled.sem, 1)
                        dve.wait_ge(self.shuffled.sem, self.shuffled.at(i + 1))
                        dve.tensor_tensor(r, r, sm("sin"), ALU.mult).then_inc(self.sined.sem, 1)
                        dve.wait_ge(self.cosined.sem, self.cosined.at(i + 1))
                        dve.wait_ge(self.sined.sem, self.sined.at(i + 1))
                        dve.tensor_tensor(x, x, r, ALU.add).then_inc(self.turned.sem, 1)
                    if i:
                        self.low_of_qk(dve, i - 1)
                self.low_of_qk(dve, len(self.prep) - 1)

                def gates(i):
                    for c in range(4):
                        n = self.nq["gate"] + c
                        split_next(dve, split_low, n + 4 * i, n)
                repeat(dve, KT // 4, gates)

                def row_max(j):
                    t, q, key, nkeys = self.steps[j]
                    both = ps[:, 2 * (j % 2):2 * (j % 2) + 2]
                    dve.wait_ge(self.scored.sem, self.scored.at(j + 1))
                    if b == "B" and key == 0:
                        n = self.l * 8 + j
                        dve.wait_ge(bias_landed[j % 2].sem, 16 * (n // 2 + 1))
                        dve.scalar_tensor_tensor(out=both[:, :, 0:S_X], in0=na_bias[:, j % 2], scalar=1.0 / SCALE,
                                                 in1=both[:, :, 0:S_X], op0=ALU.mult, op1=ALU.add).then_inc(self.masked.sem, 1)
                        dve.wait_ge(self.masked.sem, self.masked.at(j + 1))
                    if b == "D" and key == 0:
                        a = P - q
                        m = smv("mask", pattern="p (i s k) -> p i s k", i=2, s=2)[:, q // P]
                        dve.tensor_tensor(both[:, :, a:a + P], both[:, :, a:a + P], m, ALU.add).then_inc(self.masked.sem, 1)
                        dve.wait_ge(self.masked.sem, self.masked.at(j + 1))
                    if past(j - 1):
                        dve.wait_ge(self.probs.sem, self.probs.at(j - 1))
                    dve.tensor_reduce(stat[:, j % 2, 0], both[:, :, 0:nkeys], AX.X, ALU.max).then_inc(self.maxed.sem, 1)
                    dve.wait_ge(self.maxed.sem, self.maxed.at(j + 1))
                    if b == "D":
                        sink = smv("sink", self.l, DEPTH, "p (t s) -> p t s", s=2)[:, t]
                        dve.scalar_tensor_tensor(out=stat[:, j % 2, 5], in0=stat[:, j % 2, 0], scalar=SCALE, in1=sink,
                                                 op0=ALU.mult, op1=ALU.max).then_inc(self.sums.sem, 1)
                        dve.wait_ge(self.sums.sem, self.sums.at(3 * j + 1))
                        dve.tensor_tensor(stat[:, j % 2, 3], sink, stat[:, j % 2, 5], ALU.subtract).then_inc(self.sunk.sem, 1)
                        dve.tensor_scalar(stat[:, j % 2, 1], stat[:, j % 2, 5], -1.0, None, ALU.mult).then_inc(self.shifted.sem, 1)
                    else:
                        dve.tensor_scalar(stat[:, j % 2, 1], stat[:, j % 2, 0], -SCALE, None, ALU.mult).then_inc(self.shifted.sem, 1)

                def scale_probs(j):
                    nkeys = self.steps[j][3]
                    st = stat[:, j % 2]
                    total = st[:, 2]
                    dve.wait_ge(self.expd.sem, self.expd.at(j + 1))
                    if b == "D":
                        dve.tensor_tensor(st[:, 5], st[:, 2], st[:, 4], ALU.add).then_inc(self.sums.sem, 1)
                        dve.wait_ge(self.sums.sem, self.sums.at(3 * j + 2))
                        total = st[:, 5]
                    k = {"A": 3, "D": 3}.get(b, 3)
                    if b == "A":
                        dve.reciprocal(st[:, 3], total).then_inc(self.sums.sem, 1)
                        dve.wait_ge(self.sums.sem, self.sums.at(3 * j + 1))
                        dve.tensor_scalar(prob[:, j % 2, 0, 0:nkeys], prob[:, j % 2, 0, 0:nkeys], st[:, 3, 0:1], None, ALU.mult)
                        dve.tensor_scalar(st[:, 4, 1:2], st[:, 3, 1:2], lam[:, 5:6], None, ALU.mult).then_inc(self.sums.sem, 2)
                        dve.wait_ge(self.sums.sem, self.sums.at(3 * j + 3))
                        dve.scalar_tensor_tensor(out=prob[:, j % 2, 0, 0:nkeys], in0=prob[:, j % 2, 1, 0:nkeys], scalar=st[:, 4, 1:2],
                                                 in1=prob[:, j % 2, 0, 0:nkeys], op0=ALU.mult, op1=ALU.add).then_inc(self.probs.sem, 1)
                    else:
                        dve.reciprocal(st[:, 3], total).then_inc(self.sums.sem, 1 if b == "D" else 3)
                        dve.wait_ge(self.sums.sem, self.sums.at(3 * j + 3))
                        for s in range(2):
                            m = dve.tensor_scalar(prob[:, j % 2, s, 0:nkeys], prob[:, j % 2, s, 0:nkeys], st[:, 3, s:s + 1], None, ALU.mult)
                        m.then_inc(self.probs.sem, 1)

                def low_of_probs(j):
                    nkeys, ns = self.steps[j][3], 1 if b == "A" else 2
                    dve.wait_ge(self.pt_high.sem, self.pt_high.at(j + 1))
                    dve.tensor_tensor(pt_low[:, 0:ns, 0:nkeys], ps[:, 4:4 + ns, 0:nkeys], pt_high[:, 0:ns, 0:nkeys], ALU.subtract)\
                        .then_inc(self.pt_low.sem, 1)

                def low_of_out(j):
                    if b == "A":
                        return
                    t, q, _, _ = self.steps[j]
                    dve.wait_ge(self.y_high.sem, self.y_high.at(j + 1))
                    for s in range(2):
                        rows = slice(s * HD, (s + 1) * HD)
                        o = dve.tensor_tensor(q_low[rows, t, q:q + P], ps[rows, 6 + j % 2, s * P:(s + 1) * P],
                                              q_high[rows, t, q:q + P], ALU.subtract)
                    o.then_inc(self.y_low.sem, 1)
                J = len(self.steps)
                row_max(0)
                for j in range(J):
                    scale_probs(j)
                    if j + 1 < J:
                        row_max(j + 1)
                    if j:
                        low_of_out(j - 1)
                    low_of_probs(j)
                low_of_out(J - 1)
                if b == "A":
                    for t in range(BT):
                        dve.wait_ge(self.sub_rstd.sem, self.sub_rstd.at(2 * t + 2))
                        dve.scalar_tensor_tensor(out=diff_out[:, t, 0:T], in0=diff_out[:, t, 0:T], scalar=lam[:, 6:7],
                                                 in1=rstd[:, t % 2, 0:T], op0=ALU.mult, op1=ALU.mult).then_inc(self.sub_scaled.sem, 1)
                    for t in range(BT):
                        dve.wait_ge(self.y_high.sem, self.y_high.at(J + t + 1))
                        dve.tensor_tensor(q_low[:, t, 0:T], diff_out[:, t, 0:T], q_high[:, t, 0:T], ALU.subtract).then_inc(self.y_low.sem, 1)
                for c in range(BT):
                    n = self.nq["mix"] + c
                    split_next(dve, split_low, n, n)
                    dve.wait_ge(used.sem, n + 1)
                    for r in range(2):
                        m = 2 * c + r
                        z = ps[:, m % 4, 0:T]
                        if self.index == 0:
                            dve.tensor_tensor(acc[:, m, 0:T], gate[:, m, 0:T], z, ALU.mult).then_inc(self.merged.sem, 1)
                        else:
                            if past(m - 1):
                                dve.wait_ge(self.merged.sem, self.merged.at(m - 1))
                            dve.tensor_tensor(tmp[:, m % 2, 0:T], gate[:, m, 0:T], z, ALU.mult).then_inc(self.z_gated.sem, 1)
                            dve.wait_ge(self.z_gated.sem, self.z_gated.at(m + 1))
                            dve.tensor_tensor(acc[:, m, 0:T], acc[:, m, 0:T], tmp[:, m % 2, 0:T], ALU.add).then_inc(self.merged.sem, 1)
                if self.index == 3:
                    for m in range(KT):
                        dve.wait_ge(self.a_high.sem, self.a_high.at(m + 1))
                        dve.tensor_tensor(a_low[:, m, 0:T], acc[:, m, 0:T], a_high[:, m, 0:T], ALU.subtract).then_inc(self.a_low.sem, 1)

            def low_of_qk(self, dve, i):
                slot, W, hi, lo = self.prep[i]
                dve.wait_ge(self.part_high.sem, self.part_high.at(i + 1))
                dve.tensor_tensor(lo[:, 0:W], proj[:, slot, 0:W], hi[:, 0:W], ALU.subtract).then_inc(self.part_low.sem, 1)

            def pool(self, pool):
                if self.roped:
                    for i, (slot, W, hi, lo) in enumerate(self.prep):
                        x = proj[:, slot, 0:S_X]
                        pool.wait_ge(self.shuffled.sem, self.shuffled.at(i + 1))
                        pool.tensor_tensor(x, x, sm("cos"), ALU.mult).then_inc(self.cosined.sem, 1)
                if self.b == "B":
                    for j in range(8):
                        n = self.l * 8 + j
                        if past(j - 1):
                            pool.wait_ge(self.masked.sem, self.masked.at(j - 1))
                        if j == 0:
                            pool.wait_ge(used.sem, self.nq["q"] + 1)
                        pool.dma_start(na_bias[:, j % 2], na_rows[self.l, j]).then_inc(bias_landed[j % 2].sem, 16)

        class Out(Result):
            def __init__(self, layer, T, branch):
                self.n0, self.T, self.branch = STARTS[layer, "out"], T, branch
                self.result_signals()

            def tensor(self, pe):
                for m in range(KT):
                    if past(m - 1):
                        pe.wait_ge(self.copied.sem, self.copied.at(m - 1))
                    if m == 0:
                        pe.wait_ge(self.branch.merged.sem, self.branch.merged.at(KT))
                    product(pe, self.n0 + m, self.n0 + m, [(ps[:, m % 2, 0:self.T], [(k, k) for k in range(KT)])],
                            lambda k: a_high[:, k, 0:self.T], lambda k: a_low[:, k, 0:self.T],
                            before=(lambda k: pe.wait_ge(self.branch.a_low.sem, self.branch.a_low.at(k + 1))) if m == 0 else None)

            def scalar(self, act):
                for m in range(KT):
                    split_next(act, split_high, self.n0 + m, self.n0 + m)
                    act.wait_ge(used.sem, self.n0 + m + 1)
                    self.take(act, m, m % 2)

            def vector(self, dve):
                for m in range(KT):
                    split_next(dve, split_low, self.n0 + m, self.n0 + m)
                    self.add(dve, m, m % 2)

        h_ready = None
        for layer in range(DEPTH):
            last = layer == DEPTH - 1
            stages.append(Modulation(layer))
            for j in range(3):
                T = S_ALL if j < 2 or not last else S_X
                norm = Norm(layer, j, T, h_ready)
                stages.append(norm)
                if j == 1:
                    T = S_X if last else S_ALL
                    branches = []
                    for i in range(len(BRANCHES)):
                        branches.append(Branch(layer, i, T, norm, branches[-1] if branches else None))
                    stages += branches
                    result = Out(layer, T, branches[-1])
                else:
                    hidden = Hidden(layer, j, T, norm)
                    stages.append(hidden)
                    result = Down(layer, j, T, hidden)
                stages.append(result)
                residual = Residual(j, T, result)
                stages.append(residual)
                h_ready = residual.h_ready
        if stop:
            del stages[stop:]

        block = ctx.enter_context(nc.Block())

        @block.sync
        def _(sp):
            sp.dma_start(h[:, :, :], tokens).then_inc(loaded.sem, 16)
            sp.dma_start(smalls[:, :], small).then_inc(loaded.sem, 16)
            n = 0
            down = {STARTS[l, f"down{j}"] for l in range(DEPTH) for j in (0, 2)}
            ends = sorted(down | {d + 4 * KT for d in down})
            for end in ends:
                width = UNIT if end in down else DOWN_WIDTH

                def four(i, n=n, width=width):
                    for c in range(RAW_SLOTS):
                        fetch(sp, n + c + RAW_SLOTS * i, width, c)
                repeat(sp, (end - n) // RAW_SLOTS, four)
                n = end
            for k in range(KT):
                sp.wait_ge(h_ready.sem, h_ready.at(k + 1))
                sp.dma_start(out[:, k], h[:, k, 0:S_X]).then_inc(stored.sem, 16)
            sp.wait_ge(stored.sem, 16 * KT)

        @block.gpsimd
        def _(pool):
            pool.memset(ones[:, :], 1.0).then_inc(ones_set.sem, 1)
            pool.memset(eps[:, :], EPS).then_inc(ones_set.sem, 1)
            for st in stages:
                st.pool(pool)

        @block.scalar
        def _(act):
            act.wait_ge(ones_set.sem, ones_set.at(2))
            split_high(act, 0, 0)
            split_high(act, 1, 1)
            for st in stages:
                st.scalar(act)

        @block.vector
        def _(dve):
            split_low(dve, 0, 0)
            split_low(dve, 1, 1)
            dve.wait_ge(loaded.sem, loaded.at(32))
            for st in stages:
                st.vector(dve)

        @block.tensor
        def _(pe):
            pe.wait_ge(ones_set.sem, ones_set.at(2))
            pe.wait_ge(loaded.sem, loaded.at(32))
            for st in stages:
                st.tensor(pe)


def segments_of_w_in():
    widths = [("a_q", BW), ("a_k", BW), ("a_v", BW), ("b_q", BW), ("b_k", BW), ("b_v", BW),
              ("c_q", BW), ("c_k", P), ("c_v", P), ("d_q", BW), ("d_k", P), ("d_v", P)] + [(f"gate{i}", D) for i in range(4)]
    seg, at = {}, 0
    for name, w in widths:
        seg[name] = slice(at, at + w)
        at += w
    return seg


GQA_ORDER = np.concatenate([np.arange(HD) + HD * hh for t in range(4) for hh in (t, 4 + t)])


def k8(w):
    n = w.shape[1] // P
    return w.reshape(KT, P, n, P).transpose(2, 1, 0, 3).reshape(n, P, UNIT)


def lay_out(inp):
    a = {k: np.asarray(v) for k, v in inp.items()}
    f = np.float32
    tokens = np.concatenate([a["x"][0], a["ctx"][0]]).T.reshape(KT, P, S_ALL).transpose(1, 0, 2)
    _, total = unit_starts()
    weights = np.zeros((total, P, UNIT), f)
    n = 0
    seg = segments_of_w_in()

    def put(units):
        nonlocal n
        weights[n:n + len(units), :, :units.shape[-1]] = units
        n += len(units)
    for l in range(DEPTH):
        g = N_MOD * D // MOD_GROUP
        put(a["w_mod"][l].reshape(4, 2, P, g, MOD_GROUP).transpose(3, 0, 2, 1, 4).reshape(4 * g, P, UNIT))

        def ffn(j):
            both = np.stack([k8(a["ffn_w_gate"][l, j]), k8(a["ffn_w_up"][l, j])], 1)
            put(both.reshape(2 * FT, P, UNIT))
            w = a["ffn_w_down"][l, j].reshape(FT, P, KT, P)
            for m in range(KT):
                k0 = 0
                for nk in DOWN_K:
                    put(w[k0:k0 + nk, :, m].transpose(1, 0, 2).reshape(1, P, nk * P))
                    k0 += nk
        ffn(0)
        w_in = a["w_in"][l]
        for i, b in enumerate(BRANCHES.lower()):
            q = w_in[:, seg[b + "_q"]]
            wb = a["w_branch"][l, i]
            if b in "cd":
                q, wb = q[:, GQA_ORDER], wb[GQA_ORDER]
            put(k8(q))
            put(k8(w_in[:, seg[b + "_k"]]))
            put(k8(w_in[:, seg[b + "_v"]]))
            put(k8(w_in[:, seg[f"gate{i}"]]))
            put(wb.reshape(BT, P, 4, 2, P).transpose(2, 1, 3, 0, 4).reshape(4, P, UNIT))
        put(k8(a["w_out"][l]))
        ffn(1)
    assert n == total
    s = {}
    s["c"] = np.stack([a["c"][0].reshape(KT, P), a["c_ctx"].reshape(KT, P)], -1).transpose(1, 0, 2)
    s["b_mod"] = a["b_mod"].reshape(DEPTH, MODT, P).transpose(2, 0, 1)
    s["gain"] = a["norm_gain"].reshape(DEPTH, 6, KT, P).transpose(3, 0, 1, 2)
    s["lam"] = np.broadcast_to(a["diff_lambda"].reshape(1, -1), (P, DEPTH * 4 * HD))
    s["subln"] = a["diff_subln"].T
    s["qk_gain"] = np.concatenate([a["qk_norm"]] * 2, -1).transpose(2, 0, 1)
    s["sink"] = np.broadcast_to(a["sink"].reshape(1, DEPTH, 2, 4).transpose(0, 1, 3, 2).reshape(1, -1), (P, DEPTH * 8))
    t = np.arange(S_X)
    inv = (f(10000.0) ** (-np.arange(HD // 4, dtype=f) / f(HD // 4))).astype(f)
    ang = np.stack([(t // GRID_W).astype(f)[:, None] * inv, (t % GRID_W).astype(f)[:, None] * inv], 1)
    cos, sin = np.cos(ang), np.sin(ang)
    row = np.arange(P) % HD
    part, half, fr = row // 32, row % 32 // 16, row % 16
    s["cos"] = cos[:, part, fr].T
    s["sin"] = (sin[:, part, fr] * np.where(half, 1, -1)).T
    s["ident"] = np.eye(P)
    s["pairs"] = np.kron(np.eye(2), np.ones((HD, HD)))
    pick = np.zeros((P, 2))
    pick[[0, 2], 0] = pick[[1, 3], 1] = 1
    s["pick"] = pick
    q, k = np.arange(P)[:, None], np.arange(P)[None]
    m = np.stack([np.where(k + P - q <= SWA_WINDOW, 0, MASKED), np.where(q + P - k <= SWA_WINDOW, 0, MASKED)], 1)
    s["mask"] = np.stack([m, m], 2)
    small = np.concatenate([np.asarray(s[name]).reshape(P, w).astype(f) for name, (_, w) in SMALL.items()], 1)
    rows = S_X // GRID_W
    kh = min(NA_KH, rows)
    r, c = t // GRID_W, t % GRID_W
    r0, c0 = np.clip(r - kh // 2, 0, rows - kh), np.clip(c - NA_KW // 2, 0, GRID_W - NA_KW)
    inside = ((r[None] >= r0[:, None]) & (r[None] < r0[:, None] + kh) & (c[None] >= c0[:, None]) & (c[None] < c0[:, None] + NA_KW))
    dr = np.where(inside, r[None] - r[:, None] + NA_KH - 1, 0)
    dc = np.where(inside, c[None] - c[:, None] + NA_KW - 1, 0)
    na = np.where(inside, a["na_bias"][:, :, dr, dc], f(MASKED))
    na = na.reshape(DEPTH, 4, 2, 2, P, S_X).transpose(0, 1, 3, 4, 2, 5).reshape(DEPTH, 8, P, 2, S_X)
    return {"tokens": tokens, "small": small, "weights": weights, "na_rows": na}


def kernel(**inputs):
    import concourse.bacc as bacc
    from concourse.bass_utils import run_bass_kernel_spmd

    nc = bacc.Bacc("TRN2", target_bir_lowering=False, num_devices=1)
    arrays, args = {}, []
    for name, v in lay_out(inputs).items():
        v = np.ascontiguousarray(v, dtype=np.float32)
        arrays[f"in_{name}"] = v
        args.append(nc.dram_tensor(f"in_{name}", v.shape, F32, kind="ExternalInput").ap())
    args.append(nc.dram_tensor("out_tokens", (P, KT, S_X), F32, kind="ExternalOutput").ap())
    build(nc, *args)
    r = run_bass_kernel_spmd(nc, [arrays], core_ids=[0])
    got = r.results[0]["out_tokens"]
    return got.transpose(1, 0, 2).reshape(D, S_X).T.reshape(1, S_X, D)
```

```python
import math
from contextlib import ExitStack

import numpy as np
import concourse.bass as bass
from concourse import mybir

F32 = mybir.dt.float32
F32R = mybir.dt.float32r
ALU = mybir.AluOpType
ACT = mybir.ActivationFunctionType
AX = mybir.AxisListType

P = 128
D = 1024
DEPTH = 2
S_X = 256
S_C = 256
S_ALL = S_X + S_C
GRID_W = 64
HD = 64
KT = D // P
BW = D // 2
BT = BW // P
FF = ((8 * D // 3 + 255) // 256) * 256
FT = FF // P
N_MOD = 9
MODT = N_MOD * KT
NA_KH, NA_KW = 8, 16
SWA_WINDOW = 128
EPS = 1e-6
SCALE = HD ** -0.5
MASKED = -1e30

UNIT = 8 * P
RAW_SLOTS = 4
SPLIT_SLOTS = 2
DOWN_K = (6, 5, 6, 5)
DOWN_WIDTH = max(DOWN_K) * P
MOD_GROUP = 512

BRANCHES = "ABCD"
N_K = {"A": BT, "B": BT, "C": 1, "D": 1}

SMALL = {}
_at = 0
for _name, _w in (("c", KT * 2), ("b_mod", DEPTH * MODT), ("gain", DEPTH * 6 * KT), ("lam", DEPTH * 4 * HD),
                  ("subln", DEPTH), ("qk_gain", DEPTH * 2), ("sink", DEPTH * 8), ("cos", S_X), ("sin", S_X),
                  ("ident", P), ("pairs", P), ("pick", 2), ("mask", 2 * 2 * P)):
    SMALL[_name] = (_at, _w)
    _at += _w
SMALL_W = _at


def layer_units():
    out = [("mod", N_MOD * D // MOD_GROUP * 4)]
    out += [("up0", 2 * FT), ("down0", 4 * KT)]
    out += [("Aproj", 3 * BT)]
    for b, follows in zip(BRANCHES, BRANCHES[1:] + " "):
        out += [(b + "window", KT + (BT + 2 * N_K[follows] if follows in BRANCHES else 0)), (b + "mix", BT)]
    out += [("out", KT), ("up2", 2 * FT), ("down2", 4 * KT)]
    return out


def unit_starts():
    at, starts = 0, {}
    for layer in range(DEPTH):
        for name, n in layer_units():
            starts[layer, name] = at
            at += n
    return starts, at


class Signal:

    def __init__(self, sem, base):
        self.sem, self.base = sem, base

    def at(self, k):
        return self.base + k


class Signals:

    def __init__(self, nc, ctx):
        self.nc, self.ctx, self.sems, self.counts = nc, ctx, {}, {}

    def new(self, name, total):
        if name not in self.sems:
            self.sems[name] = self.ctx.enter_context(self.nc.semaphore(name))
            self.counts[name] = 0
        s = Signal(self.sems[name], self.counts[name])
        self.counts[name] += total
        return s


def past(k):
    return not isinstance(k, int) or k > 0


def repeat(eng, count, body):
    body(0)
    if count == 2:
        body(1)
    elif count > 2:
        with eng.Fori(1, count) as i:
            body(i)


def build(nc, tokens, small, weights, na_rows, h_kept, out, stop=None):
    STARTS, N_UNITS = unit_starts()
    with ExitStack() as ctx:
        start = (nc.sbuf_base + 31) // 32 * 32
        slab = ctx.enter_context(nc.sbuf_tensor("slab", [P, 207 * 256 - 40], F32))
        del slab

        def place(name, shape, dt, at):
            return nc.alloc_sbuf_tensor_at(name, [P] + shape, dt, offset=start + at)

        KB = 1024
        at = 0
        raw = place("raw", [RAW_SLOTS, UNIT], F32, at); at += 16 * KB
        w_high = place("w_high", [SPLIT_SLOTS, 8, P], F32R, at); at += 8 * KB
        w_low = place("w_low", [SPLIT_SLOTS, 8, P], F32R, at); at += 8 * KB
        u_high = place("u_high", [KT, S_ALL], F32R, at)
        u_low = place("u_low", [KT, S_ALL], F32R, at + 16 * KB)
        y = place("y", [KT, S_ALL], F32, at); at += 32 * KB
        h = place("h", [KT, S_ALL], F32, at); at += 16 * KB
        big = at; at += 88 * KB
        acc_at = at; at += 16 * KB
        smalls = place("smalls", [SMALL_W], F32, at); at += (SMALL_W * 4 + 31) // 32 * 32
        mod = place("mod", [MODT, 2], F32, at); at += MODT * 8
        pre = place("pre", [3, KT, 2], F32, at); at += 3 * KT * 8
        post = place("post", [3, KT, 2], F32, at); at += 3 * KT * 8
        sq = place("sq", [2, S_ALL], F32, at); at += 4 * KB
        rstd = place("rstd", [2, S_ALL], F32, at)
        na_bias = place("na_bias", [2, 2, S_X], F32, at); at += 4 * KB
        tmp = place("tmp", [2, S_ALL], F32, at); at += 4 * KB
        ones = place("ones", [P], F32, at); at += 512
        stat = place("stat", [2, 6, 2], F32, at); at += 96
        lam = place("lam", [8], F32, at); at += 32
        eps = place("eps", [2], F32, at); at += 32
        assert start + at <= nc.sbuf_usable_end, (start + at, nc.sbuf_usable_end)
        hid_high = place("hid_high", [FT, S_ALL], F32R, big)
        hid_low = place("hid_low", [FT, S_ALL], F32R, big + 44 * KB)
        proj = place("proj", [12, S_ALL], F32, big - 16 * KB)
        at_mix = big + 8 * KB
        q_high = place("q_high", [BT, S_ALL], F32R, at_mix)
        q_low = place("q_low", [BT, S_ALL], F32R, at_mix + 8 * KB)
        k_high = place("k_high", [BT, S_ALL], F32R, at_mix + 16 * KB)
        k_low = place("k_low", [BT, S_ALL], F32R, at_mix + 24 * KB)
        v_high = place("v_high", [4, BW], F32R, at_mix + 32 * KB)
        v_low = place("v_low", [4, BW], F32R, at_mix + 40 * KB)
        a_high = place("a_high", [KT, S_ALL], F32R, at_mix + 16 * KB)
        a_low = place("a_low", [KT, S_ALL], F32R, at_mix + 32 * KB)
        pt_high = place("pt_high", [2, 4 * P], F32R, at_mix + 48 * KB)
        pt_low = place("pt_low", [2, 4 * P], F32R, at_mix + 52 * KB)
        prob = place("prob", [2, 2, S_ALL], F32, at_mix + 56 * KB)
        gate = place("gate", [KT, S_ALL], F32, at_mix + 64 * KB)
        acc = place("acc", [KT, S_ALL], F32, acc_at)
        silu_g = place("silu_g", [2, S_ALL], F32, acc_at)
        hid = place("hid", [2, S_ALL], F32, acc_at + 4 * KB)
        ssq = place("ssq", [S_ALL], F32, acc_at + 8 * KB)
        mod_row = place("mod_row", [2, MOD_GROUP], F32, acc_at + 8 * KB)
        c_split = place("c_split", [KT, P], F32R, acc_at + 12 * KB)
        silu_c = place("silu_c", [KT, 2], F32, acc_at)

        ps = ctx.enter_context(nc.psum_tensor("ps", [P, 8, 512], F32))

        def sm(name, layer=0, n=1):
            a, w = SMALL[name]
            w //= n
            return smalls[:, a + layer * w:a + (layer + 1) * w]

        def smv(name, layer=0, n=1, pattern=None, **k):
            v = sm(name, layer, n)
            return v.rearrange(pattern, **k) if pattern else v

        ident = sm("ident")
        pairs = sm("pairs")
        gain_of = [smv("gain", l, DEPTH, "p (a k) -> p a k", a=6) for l in range(DEPTH)]
        b_mod_of = [sm("b_mod", l, DEPTH) for l in range(DEPTH)]

        signals = Signals(nc, ctx)
        loaded = signals.new("inputs_loaded", 32)
        landed = [signals.new(f"weights_landed{i}", 0) for i in range(RAW_SLOTS)]
        high_made = signals.new("weights_high_made", 0)
        low_made = signals.new("weights_low_made", 0)
        used = signals.new("weights_used", 0)
        ones_set = signals.new("ones_set", 3)
        stored = signals.new("stored", 0)
        bias_landed = [signals.new(f"bias_landed{i}", 0) for i in range(2)]
        h_saved = signals.new("h_saved", 0)
        h_back = signals.new("h_back", 0)

        def fetch(sp, n, width, j):
            if not isinstance(n, int) or n >= RAW_SLOTS:
                sp.wait_ge(low_made.sem, n - RAW_SLOTS + 1)
            src = weights[n, :, 0:width] if isinstance(n, int) else weights[bass.ds(n, 1), :, 0:width].rearrange("a p w -> (a p) w")
            sp.dma_start(raw[:, j, 0:width], src).then_inc(landed[j].sem, 16)

        def split_high(act, n, n0):
            act.wait_ge(landed[n0 % RAW_SLOTS].sem, (n0 // RAW_SLOTS + 1) * 16 + (n - n0) * (16 // RAW_SLOTS))
            if n0 >= SPLIT_SLOTS:
                act.wait_ge(used.sem, n - SPLIT_SLOTS + 1)
            s = n0 % SPLIT_SLOTS
            act.activation(w_high[:, s].rearrange("p a b -> p (a b)"), raw[:, n0 % RAW_SLOTS], ACT.Copy).then_inc(high_made.sem, 1)

        def split_low(dve, n, n0):
            dve.wait_ge(high_made.sem, n + 1)
            s = n0 % SPLIT_SLOTS
            dve.tensor_tensor(w_low[:, s].rearrange("p a b -> p (a b)"), raw[:, n0 % RAW_SLOTS],
                              w_high[:, s].rearrange("p a b -> p (a b)"), ALU.subtract).then_inc(low_made.sem, 1)

        def product(pe, n, n0, outs, x_high, x_low, first=True, last=True, before=None):
            s = n0 % SPLIT_SLOTS
            pe.wait_ge(high_made.sem, n + 1)
            for o, terms in outs:
                for a, (w, x) in enumerate(terms):
                    if before:
                        before(x)
                    pe.matmul(o, w_high[:, s, w], x_high(x), start=first and a == 0, stop=False)
                    pe.matmul(o, w_high[:, s, w], x_low(x), start=False, stop=False)
            pe.wait_ge(low_made.sem, n + 1)
            for o, terms in outs:
                for a, (w, x) in enumerate(terms):
                    done = pe.matmul(o, w_low[:, s, w], x_high(x), start=False, stop=last and a == len(terms) - 1)
            done.then_inc(used.sem, 1)

        def split_next(act_or_dve, f, n, n0):
            if n0 + SPLIT_SLOTS < N_UNITS:
                f(act_or_dve, n + SPLIT_SLOTS, n0 + SPLIT_SLOTS)

        stages = []

        class Stage:
            def tensor(self, pe): pass
            def scalar(self, act): pass
            def vector(self, dve): pass
            def pool(self, pool): pass

        class Modulation(Stage):
            GROUPS = N_MOD * D // MOD_GROUP

            def __init__(self, layer):
                self.l, self.n0 = layer, STARTS[layer, "mod"]
                self.c_silu = signals.new("c_silu", 1)
                self.c_parts = signals.new("c_parts", 3)
                self.row_copied = signals.new("mod_row_copied", self.GROUPS)
                self.turned = signals.new("mod_turned", self.GROUPS)
                self.added = signals.new("mod_added", self.GROUPS)
                self.derived = signals.new("mod_derived", 3)
                self.lam_steps = signals.new("lam_steps", 5)
                self.lam_exp = signals.new("lam_exp", 1)

            def tensor(self, pe):
                pe.wait_ge(self.c_parts.sem, self.c_parts.at(3))

                def two_groups(i):
                    for g in range(2):
                        if isinstance(i, int) and i == 0:
                            pass
                        else:
                            if past(2 * i + g - 1):
                                pe.wait_ge(self.row_copied.sem, self.row_copied.at(2 * i + g - 1))
                        for k2 in range(4):
                            n = self.n0 + 8 * i + 4 * g + k2
                            n0 = self.n0 + 4 * g + k2
                            s = n0 % SPLIT_SLOTS
                            pe.wait_ge(high_made.sem, n + 1)
                            for part, w in ((0, w_high), (1, w_low)):
                                if part:
                                    pe.wait_ge(low_made.sem, n + 1)
                                for a in range(2):
                                    done = pe.matmul(ps[:, g], c_split[:, 2 * k2 + a], w[:, s, 4 * a:4 * a + 4].rearrange("p a b -> p (a b)"),
                                                     start=k2 == 0 and part == 0 and a == 0,
                                                     stop=k2 == 3 and part == 1 and a == 1)
                            done.then_inc(used.sem, 1)
                    for g in range(2):
                        pe.wait_ge(self.row_copied.sem, self.row_copied.at(2 * i + g + 1))
                        if not (isinstance(i, int) and i == 0):
                            if past(2 * i + g - 1):
                                pe.wait_ge(self.added.sem, self.added.at(2 * i + g - 1))
                        for c in range(4):
                            t = pe.matmul(ps[:, 2 + g, 2 * c:2 * c + 2], mod_row[0:4, g, c * P:(c + 1) * P],
                                          smalls[0:4, SMALL["pick"][0]:SMALL["pick"][0] + 2], start=c == 0, stop=c == 3,
                                          skip_group_check=True)
                        t.then_inc(self.turned.sem, 1)
                repeat(pe, self.GROUPS // 2, two_groups)

            def scalar(self, act):
                act.wait_ge(loaded.sem, loaded.at(32))
                act.activation(silu_c[:, :, :], smv("c", pattern="p (k s) -> p k s", s=2), ACT.Silu).then_inc(self.c_silu.sem, 1)
                act.wait_ge(self.lam_steps.sem, self.lam_steps.at(3))
                act.activation(lam[:, 2:4], lam[:, 0:2], ACT.Exp).then_inc(self.lam_exp.sem, 1)

                def two_groups(i):
                    for g in range(2):
                        for k2 in range(4):
                            n, n0 = self.n0 + 8 * i + 4 * g + k2, self.n0 + 4 * g + k2
                            split_next(act, split_high, n, n0)
                            if k2 == 3:
                                act.wait_ge(used.sem, n + 1)
                                if not (isinstance(i, int) and i == 0):
                                    if past(2 * i + g - 1):
                                        act.wait_ge(self.turned.sem, self.turned.at(2 * i + g - 1))
                                act.activation(mod_row[0:4, g], ps[0:4, g], ACT.Copy).then_inc(self.row_copied.sem, 1)
                repeat(act, self.GROUPS // 2, two_groups)

            def vector(self, dve):
                l = self.l
                dve.wait_ge(self.c_silu.sem, self.c_silu.at(1))
                dve.memset(c_split[:, :, :].bitcast(F32), 0.0).then_inc(self.c_parts.sem, 1)
                dve.wait_ge(self.c_parts.sem, self.c_parts.at(1))
                dve.tensor_copy(c_split[:, :, 0:2], silu_c[:, :, :]).then_inc(self.c_parts.sem, 1)
                dve.wait_ge(self.c_parts.sem, self.c_parts.at(2))
                dve.tensor_tensor(c_split[:, :, 2:4], silu_c[:, :, :], c_split[:, :, 0:2], ALU.subtract).then_inc(self.c_parts.sem, 1)
                lam_init = 0.8 - 0.6 * math.exp(-0.3 * l)
                dl = smv("lam", l, DEPTH, "p (a b d) -> p a b d", a=2, b=2)
                prod = tmp[:, 0, 0:2 * HD].rearrange("p (a d) -> p a d", a=2)
                st = self.lam_steps
                dve.tensor_tensor(prod, dl[:, :, 0], dl[:, :, 1], ALU.mult).then_inc(st.sem, 1)
                dve.wait_ge(st.sem, st.at(1))
                dve.tensor_reduce(lam[:, 0:2], prod, AX.X, ALU.add).then_inc(st.sem, 1)
                dve.tensor_scalar(lam[:, 6:7], smv("subln", l, DEPTH), 1.0 - lam_init, None, ALU.mult).then_inc(st.sem, 1)
                dve.wait_ge(self.lam_exp.sem, self.lam_exp.at(1))
                dve.tensor_tensor(lam[:, 4:5], lam[:, 3:4], lam[:, 2:3], ALU.subtract).then_inc(st.sem, 1)
                dve.wait_ge(st.sem, st.at(4))
                dve.tensor_scalar(lam[:, 5:6], lam[:, 4:5], -lam_init, None, ALU.add).then_inc(st.sem, 1)

                def two_groups(i):
                    for g in range(2):
                        for k2 in range(4):
                            n, n0 = self.n0 + 8 * i + 4 * g + k2, self.n0 + 4 * g + k2
                            split_next(dve, split_low, n, n0)
                    for g in range(2):
                        dve.wait_ge(self.turned.sem, self.turned.at(2 * i + g + 1))
                        tiles = bass.ds(4 * (2 * i + g), 4)
                        for s in range(2):
                            put = dve.tensor_tensor(mod[:, tiles, s], ps[:, 2 + g, s:8:2], b_mod_of[l][:, tiles], ALU.add)
                        put.then_inc(self.added.sem, 1)
                repeat(dve, self.GROUPS // 2, two_groups)
                dve.wait_ge(self.added.sem, self.added.at(self.GROUPS))
                for j, weight in enumerate((0.5, 1.0, 0.5)):
                    for s in range(2):
                        m = dve.scalar_tensor_tensor(out=pre[:, j, :, s], in0=mod[:, (3 * j + 1) * KT:(3 * j + 2) * KT, s], scalar=1.0,
                                                     in1=gain_of[l][:, 2 * j], op0=ALU.add, op1=ALU.mult)
                        m = dve.scalar_tensor_tensor(out=post[:, j, :, s], in0=mod[:, (3 * j + 2) * KT:(3 * j + 3) * KT, s], scalar=weight,
                                                     in1=gain_of[l][:, 2 * j + 1], op0=ALU.mult, op1=ALU.mult)
                    m.then_inc(self.derived.sem, 1)
                dve.wait_ge(self.derived.sem, self.derived.at(3))

        def segments(T):
            return [(0, 0, S_X)] + ([(1, S_X, S_ALL)] if T > S_X else [])

        class Norm(Stage):
            def __init__(self, layer, j, T, h_ready):
                self.l, self.j, self.T, self.h_ready = layer, j, T, h_ready
                self.squared = signals.new("norm_squared", KT)
                self.summed = signals.new("norm_summed", KT)
                self.rstd_steps = signals.new("norm_rstd", 2)
                self.scaled = signals.new("norm_scaled", KT)
                self.high = signals.new("u_high_made", KT)
                self.ready = signals.new("u_ready", KT)

            def scalar(self, act):
                T = self.T
                for k in range(KT):
                    if self.h_ready:
                        act.wait_ge(self.h_ready.sem, self.h_ready.at(k + 1))
                    if past(k - 1):
                        act.wait_ge(self.summed.sem, self.summed.at(k - 1))
                    act.activation(sq[:, k % 2, 0:T], h[:, k, 0:T], ACT.Square).then_inc(self.squared.sem, 1)
                make_rstd(act, self.summed, KT, self.rstd_steps, ps[:, 7, 0:T], rstd[:, 0, 0:T], 1.0 / D)
                for k in range(KT):
                    act.wait_ge(self.scaled.sem, self.scaled.at(k + 1))
                    for s, a, b in segments(T):
                        i = act.activation(u_high[:, k, a:b], tmp[:, k % 2, a:b], ACT.Identity,
                                           bias=mod[:, 3 * self.j * KT + k, s:s + 1])
                    i.then_inc(self.high.sem, 1)

            def tensor(self, pe):
                for k in range(KT):
                    pe.wait_ge(self.squared.sem, self.squared.at(k + 1))
                    if self.l == 0 and self.j == 0 and k == 0:
                        pe.wait_ge(ones_set.sem, ones_set.at(1))
                    pe.matmul(ps[:, 7, 0:self.T], ones[:, :], sq[:, k % 2, 0:self.T], start=k == 0, stop=k == KT - 1)\
                        .then_inc(self.summed.sem, 1)

            def vector(self, dve):
                dve.wait_ge(self.rstd_steps.sem, self.rstd_steps.at(2))

                def scale(k):
                    if past(k - 1):
                        dve.wait_ge(self.ready.sem, self.ready.at(k - 1))
                    for s, a, b in segments(self.T):
                        i = dve.scalar_tensor_tensor(out=tmp[:, k % 2, a:b], in0=h[:, k, a:b], scalar=pre[:, self.j, k, s:s + 1],
                                                     in1=rstd[:, 0, a:b], op0=ALU.mult, op1=ALU.mult)
                    i.then_inc(self.scaled.sem, 1)
                scale(0)
                for k in range(KT):
                    if k + 1 < KT:
                        scale(k + 1)
                    dve.wait_ge(self.high.sem, self.high.at(k + 1))
                    for s, a, b in segments(self.T):
                        i = dve.scalar_tensor_tensor(out=u_low[:, k, a:b], in0=tmp[:, k % 2, a:b],
                                                     scalar=mod[:, 3 * self.j * KT + k, s:s + 1],
                                                     in1=u_high[:, k, a:b], op0=ALU.add, op1=ALU.subtract)
                    i.then_inc(self.ready.sem, 1)

        def make_rstd(act, source, count, steps, total, into, scale, step=0):
            act.wait_ge(source.sem, source.at(count))
            act.activation(into, total, ACT.Ln, scale=scale, bias=eps[:, 0:1]).then_inc(steps.sem, 1)
            act.wait_ge(steps.sem, steps.at(step + 1))
            act.activation(into, into, ACT.Exp, scale=-0.5).then_inc(steps.sem, 1)

        class Hidden(Stage):
            def __init__(self, layer, j, T, norm):
                self.n0, self.T, self.norm = STARTS[layer, f"up{j}"], T, norm
                self.silu = signals.new("silu_ready", FT)
                self.steps = signals.new("hidden_steps", 2 * FT)
                self.ready = signals.new("hidden_ready", FT)

            def tensor(self, pe):
                def two_tiles(i):
                    for f in range(2):
                        if past(2 * i + f - 1):
                            pe.wait_ge(self.ready.sem, self.ready.at(2 * i + f - 1))
                        for g in range(2):
                            n0 = self.n0 + 2 * f + g
                            first = isinstance(i, int) and f == 0 and g == 0
                            product(pe, n0 + 4 * i, n0, [(ps[:, 2 * f + g, 0:self.T], [(k, k) for k in range(KT)])],
                                    lambda k: u_high[:, k, 0:self.T], lambda k: u_low[:, k, 0:self.T],
                                    before=(lambda k: pe.wait_ge(self.norm.ready.sem, self.norm.ready.at(k + 1))) if first else None)
                repeat(pe, FT // 2, two_tiles)

            def scalar(self, act):
                def two_tiles(i):
                    for f in range(2):
                        for g in range(2):
                            n0 = self.n0 + 2 * f + g
                            split_next(act, split_high, n0 + 4 * i, n0)
                            if g == 0:
                                if past(2 * i + f - 1):
                                    act.wait_ge(self.ready.sem, self.ready.at(2 * i + f - 1))
                                act.wait_ge(used.sem, n0 + 4 * i + 1)
                                act.activation(silu_g[:, f, 0:self.T], ps[:, 2 * f, 0:self.T], ACT.Silu).then_inc(self.silu.sem, 1)
                repeat(act, FT // 2, two_tiles)

            def vector(self, dve):
                T = self.T

                def two_tiles(i):
                    for f in range(2):
                        t = 2 * i + f
                        for g in range(2):
                            n0 = self.n0 + 2 * f + g
                            split_next(dve, split_low, n0 + 4 * i, n0)
                        dve.wait_ge(used.sem, n0 + 4 * i + 1)
                        dve.wait_ge(self.silu.sem, self.silu.at(t + 1))
                        if past(t - 1):
                            dve.wait_ge(self.ready.sem, self.ready.at(t - 1))
                        dve.tensor_tensor(hid[:, f, 0:T], silu_g[:, f, 0:T], ps[:, 2 * f + 1, 0:T], ALU.mult).then_inc(self.steps.sem, 1)
                        dve.wait_ge(self.steps.sem, self.steps.at(2 * t + 1))
                        dst_h = hid_high[:, bass.ds(t, 1), 0:T].rearrange("p a t -> p (a t)")
                        dst_l = hid_low[:, bass.ds(t, 1), 0:T].rearrange("p a t -> p (a t)")
                        dve.tensor_copy(dst_h, hid[:, f, 0:T]).then_inc(self.steps.sem, 1)
                        dve.wait_ge(self.steps.sem, self.steps.at(2 * t + 2))
                        dve.tensor_tensor(dst_l, hid[:, f, 0:T], dst_h, ALU.subtract).then_inc(self.ready.sem, 1)
                repeat(dve, FT // 2, two_tiles)

        class Result(Stage):
            def result_signals(self):
                self.copied = signals.new("y_squared", KT)
                self.added = signals.new("square_added", KT)

            def take(self, act, m, b):
                T = self.T
                act.activation(y[:, bass.ds(m, 1), 0:T].rearrange("p a t -> p (a t)"), ps[:, b, 0:T], ACT.Copy)
                if past(m - 1):
                    act.wait_ge(self.added.sem, self.added.at(m - 1))
                act.activation(sq[:, b, 0:T], ps[:, b, 0:T], ACT.Square).then_inc(self.copied.sem, 1)

            def add(self, dve, m, b):
                T = self.T
                dve.wait_ge(self.copied.sem, self.copied.at(m + 1))
                if isinstance(m, int) and m == 0:
                    dve.tensor_copy(ssq[:, 0:T], sq[:, b, 0:T]).then_inc(self.added.sem, 1)
                else:
                    if past(m):
                        dve.wait_ge(self.added.sem, self.added.at(m))
                    dve.tensor_tensor(ssq[:, 0:T], ssq[:, 0:T], sq[:, b, 0:T], ALU.add).then_inc(self.added.sem, 1)

        class Down(Result):
            def __init__(self, layer, j, T, hidden):
                self.n0, self.T, self.hidden = STARTS[layer, f"down{j}"], T, hidden
                self.last = self.n0 + 4 * KT == N_UNITS
                self.result_signals()

            def rows(self, eng, body):
                body(0, False)
                with eng.Fori(1, KT // 2 - self.last) as i:
                    body(i, False)
                if self.last:
                    body(KT // 2 - 1, True)

            def tensor(self, pe):
                pe.wait_ge(self.hidden.ready.sem, self.hidden.ready.at(FT))

                def two_rows(i, last):
                    for r in range(2):
                        if past(2 * i + r - 1):
                            pe.wait_ge(self.copied.sem, self.copied.at(2 * i + r - 1))
                        k0 = 0
                        for part, nk in enumerate(DOWN_K):
                            n0 = self.n0 + 4 * r + part
                            product(pe, n0 + 8 * i, n0, [(ps[:, r, 0:self.T], [(w, k0 + w) for w in range(nk)])],
                                    lambda k: hid_high[:, k, 0:self.T], lambda k: hid_low[:, k, 0:self.T],
                                    first=part == 0, last=part == 3)
                            k0 += nk
                self.rows(pe, two_rows)

            def scalar(self, act):
                def two_rows(i, last):
                    for r in range(2):
                        for part in range(4):
                            n0 = self.n0 + 4 * r + part
                            if not (last and r == 1 and part >= 2):
                                split_high(act, n0 + 8 * i + 2, n0 + 2)
                        act.wait_ge(used.sem, n0 + 8 * i + 1)
                        self.take(act, 2 * i + r, r)
                self.rows(act, two_rows)

            def vector(self, dve):
                def two_rows(i, last):
                    for r in range(2):
                        for part in range(4):
                            n0 = self.n0 + 4 * r + part
                            if not (last and r == 1 and part >= 2):
                                split_low(dve, n0 + 8 * i + 2, n0 + 2)
                        self.add(dve, 2 * i + r, r)
                self.rows(dve, two_rows)

        class Residual(Stage):
            def __init__(self, layer, j, T, result):
                self.l, self.j, self.T, self.result = layer, j, T, result
                self.summed = signals.new("y_summed", 1)
                self.rstd_steps = signals.new("y_rstd", 2)
                self.scaled = signals.new("y_scaled", KT)
                self.h_ready = signals.new("h_ready", KT)

            def tensor(self, pe):
                pe.wait_ge(self.result.added.sem, self.result.added.at(KT))
                pe.matmul(ps[:, 7, 0:self.T], ones[:, :], ssq[:, 0:self.T], start=True, stop=True).then_inc(self.summed.sem, 1)

            def scalar(self, act):
                make_rstd(act, self.summed, 1, self.rstd_steps, ps[:, 7, 0:self.T], rstd[:, 0, 0:self.T], 1.0 / D)

            def vector(self, dve):
                dve.wait_ge(self.rstd_steps.sem, self.rstd_steps.at(2))

                def scale(k):
                    if past(k - 1):
                        dve.wait_ge(self.h_ready.sem, self.h_ready.at(k - 1))
                    for s, a, b in segments(self.T):
                        i = dve.scalar_tensor_tensor(out=tmp[:, k % 2, a:b], in0=y[:, k, a:b], scalar=post[:, self.j, k, s:s + 1],
                                                     in1=rstd[:, 0, a:b], op0=ALU.mult, op1=ALU.mult)
                    i.then_inc(self.scaled.sem, 1)
                scale(0)
                if self.j == 1:
                    dve.wait_ge(h_back.sem, 16 * (self.l + 1))
                for k in range(KT):
                    if k + 1 < KT:
                        scale(k + 1)
                    dve.wait_ge(self.scaled.sem, self.scaled.at(k + 1))
                    dve.tensor_tensor(h[:, k, 0:self.T], h[:, k, 0:self.T], tmp[:, k % 2, 0:self.T], ALU.add).then_inc(self.h_ready.sem, 1)

        class Branch(Stage):

            def __init__(self, layer, index, T, norm, before):
                self.l, self.index, self.b, self.T, self.norm, self.before = layer, index, BRANCHES[index], T, norm, before
                b = self.b
                self.nk = N_K[b]
                self.tiles = BT + 2 * self.nk
                self.roped, self.normed = b != "B", b == "C"
                self.prep = [(BT + i, S_ALL, k_high[:, i], k_low[:, i]) for i in range(self.nk)]
                self.prep += [(i, T, q_high[:, i], q_low[:, i]) for i in range(BT)]
                n = len(self.prep)
                self.steps = [(t, q, 0, S_ALL) for t in range(BT) for q in (0, P)]
                if T > S_X:
                    self.steps += [(t, q, S_X, S_C) for t in range(BT) for q in (S_X, S_X + P)]
                J = self.J = len(self.steps)
                follows = BRANCHES[index + 1] if index + 1 < len(BRANCHES) else None
                self.window = [("gate", m, T) for m in range(KT)]
                if follows:
                    self.window += [("proj", t, T if t < BT else S_ALL) for t in range(BT + 2 * N_K[follows])]
                self.n_window = STARTS[layer, b + "window"]
                self.n_mix = STARTS[layer, b + "mix"]
                self.ahead = (2 if T > S_X else 4) if before else 4
                rest = len(self.window) - self.ahead
                self.share = [(self.ahead + rest * j // J, self.ahead + rest * (j + 1) // J) for j in range(J)]

                if not before:
                    self.projected = signals.new("projected", self.tiles)
                    self.staged, self.staged_at = self.projected, self.tiles
                else:
                    self.staged, self.staged_at = before.taken, len(before.window)
                self.taken = signals.new("product_taken", len(self.window))
                self.v_turned = signals.new("v_turned", 4)
                self.v_high = signals.new("v_high_made", 4)
                self.v_low = signals.new("v_low_made", 4)
                self.head_squared = signals.new("head_squared", n if self.normed else 0)
                self.head_summed = signals.new("head_summed", n if self.normed else 0)
                self.head_rstd = signals.new("head_rstd", 2 * n if self.normed else 0)
                self.head_normed = signals.new("head_normed", n if self.normed else 0)
                self.shuffled = signals.new("rope_shuffled", n if self.roped else 0)
                self.sined = signals.new("rope_sine", n if self.roped else 0)
                self.cosined = signals.new("rope_cosine", n if self.roped else 0)
                self.turned = signals.new("rope_added", n if self.roped else 0)
                self.part_high = signals.new("qk_high_made", n)
                self.part_low = signals.new("qk_low_made", n)
                self.scored = signals.new("scores_ready", J)
                self.maxed = signals.new("row_max", J)
                self.shifted = signals.new("shift_ready", J)
                self.sunk = signals.new("sink_shifted", J if b == "D" else 0)
                self.expd = signals.new("exp_ready", J)
                self.sums = signals.new("sum_steps", 3 * J)
                self.probs = signals.new("probs_ready", J)
                self.flipped = signals.new("probs_turned", J)
                self.pt_high = signals.new("probs_high_made", J)
                self.pt_low = signals.new("probs_low_made", J)
                self.mixed = signals.new("values_mixed", J)
                self.o_high = signals.new("branch_high_made", J)
                self.o_low = signals.new("branch_low_made", J)
                sub = BT if b == "A" else 0
                self.sub_joined = signals.new("sub_joined", sub)
                self.sub_squared = signals.new("sub_squared", sub)
                self.sub_summed = signals.new("sub_summed", sub)
                self.sub_rstd = signals.new("sub_rstd", 2 * sub)
                self.sub_scaled = signals.new("sub_scaled", sub)
                self.sub_high = signals.new("sub_high_made", sub)
                self.sub_low = signals.new("sub_low_made", sub)
                self.y_ready, self.y_count = (self.sub_low, BT) if b == "A" else (self.o_low, J)
                self.gated = signals.new("branch_gated", KT if index else 0)
                self.merged = signals.new("branch_merged", KT)
                if b in "BD":
                    self.masked = signals.new("scores_biased" if b == "B" else "scores_masked", 8)

            def carriers(self):
                keys, queries = list(range(self.nk)), list(range(self.nk, len(self.prep)))
                out = []
                if self.before:
                    for c in range(BT):
                        mine = [i for i in keys if (i + BT - self.nk) == c]
                        out.append(("mix", c, mine))
                    keys = []
                items = keys + queries
                for g in range(self.ahead):
                    out.append(("gate", g, items[len(items) * g // self.ahead:len(items) * (g + 1) // self.ahead]))
                return out

            def head_items(self, c):
                return [i for i in range(len(self.prep)) if self.normed and min(i // 2, BT - 1) == c]

            def first_projections(self, pe):
                W = [self.T] * BT + [S_ALL] * 2 * self.nk
                n1 = STARTS[self.l, "Aproj"]

                def four(i, base):
                    for c in range(4):
                        n = n1 + base + c
                        if past(4 * i + base + c - 1):
                            pe.wait_ge(self.projected.sem, self.projected.at(4 * i + base + c - 1))
                        w = W[base + c]
                        product(pe, n + 4 * i, n, [(ps[:, 6 + c % 2, 0:w], [(k, k) for k in range(KT)])],
                                lambda k: u_high[:, k, 0:w], lambda k: u_low[:, k, 0:w],
                                before=(lambda k: pe.wait_ge(self.norm.ready.sem, self.norm.ready.at(k + 1))) if base + c == 0 else None)
                four(0, 0)
                repeat(pe, 2, lambda i: four(i, BT))

            def window_unit(self, pe, w):
                kind, t, W = self.window[w]
                n = self.n_window + w
                if w >= 2:
                    pe.wait_ge(self.taken.sem, self.taken.at(w - 1))
                elif self.before:
                    pe.wait_ge(self.before.merged.sem, self.before.merged.at(6))
                else:
                    pe.wait_ge(self.projected.sem, self.projected.at(self.tiles))
                product(pe, n, n, [(ps[:, 6 + w % 2, 0:W], [(k, k) for k in range(KT)])],
                        lambda k: u_high[:, k, 0:W], lambda k: u_low[:, k, 0:W])

            def mix_unit(self, pe, c):
                if c == 0:
                    pe.wait_ge(self.taken.sem, self.taken.at(len(self.window)))
                if c >= 2:
                    pe.wait_ge(self.merged.sem, self.merged.at(2 * c - 2))
                T, n, b0 = self.T, self.n_mix + c, 6 - 2 * (c % 2)
                product(pe, n, n, [(ps[:, b0 + r, 0:T], [(4 * r + k, k) for k in range(BT)]) for r in range(2)],
                        lambda k: q_high[:, k, 0:T], lambda k: q_low[:, k, 0:T])

            def tensor(self, pe):
                b, T, J = self.b, self.T, self.J
                if not self.before:
                    self.first_projections(pe)
                else:
                    pe.wait_ge(self.before.y_ready.sem, self.before.y_ready.at(self.before.y_count))
                pe.wait_ge(self.staged.sem, self.staged.at(self.staged_at))
                for tt in range(4):
                    for c in range(self.nk):
                        v = pe.transpose(ps[:, tt, c * P:(c + 1) * P], proj[:, BT + self.nk + c, tt * P:(tt + 1) * P], ident)
                    v.then_inc(self.v_turned.sem, 1)
                for kind, c, _ in self.carriers():
                    if kind == "gate":
                        self.window_unit(pe, c)
                        continue
                    self.before.mix_unit(pe, c)
                    for i in self.head_items(c):
                        pe.wait_ge(self.head_squared.sem, self.head_squared.at(i + 1))
                        if i < 2:
                            pe.wait_ge(self.v_low.sem, self.v_low.at(i + 1))
                        else:
                            pe.wait_ge(self.head_rstd.sem, self.head_rstd.at(2 * (i - 2) + 2))
                        W = self.prep[i][1]
                        pe.matmul(ps[:, i % 2, 0:W], pairs, sq[:, i % 2, 0:W], start=True, stop=True).then_inc(self.head_summed.sem, 1)
                pe.wait_ge(self.part_low.sem, self.part_low.at(len(self.prep)))
                pe.wait_ge(self.v_low.sem, self.v_low.at(4))
                if self.before:
                    pe.wait_ge(self.before.merged.sem, self.before.merged.at(KT))

                def scores(j):
                    t, q, key, nkeys = self.steps[j]
                    kt = t if self.nk == BT else 0
                    if past(j):
                        pe.wait_ge(self.expd.sem, self.expd.at(j))
                    for s in range(2):
                        rows = slice(s * HD, (s + 1) * HD)
                        for a, (qq, kk) in enumerate(((q_high, k_high), (q_high, k_low), (q_low, k_high))):
                            m = pe.matmul(ps[:, s, 0:nkeys], qq[rows, t, q:q + P], kk[rows, kt, key:key + nkeys], start=a == 0, stop=a == 2)
                    m.then_inc(self.scored.sem, 1)

                def flip(j):
                    nkeys = self.steps[j][3]
                    pe.wait_ge(self.probs.sem, self.probs.at(j + 1))
                    if past(j):
                        pe.wait_ge(self.pt_low.sem, self.pt_low.at(j))
                    for s in range(1 if b == "A" else 2):
                        for c in range(nkeys // P):
                            m = pe.transpose(ps[:, 2 + s, c * P:(c + 1) * P], prob[:, j % 2, s, c * P:(c + 1) * P], ident)
                    m.then_inc(self.flipped.sem, 1)

                def mix(j):
                    t, q, key, nkeys = self.steps[j]
                    vt = t if self.nk == BT else 0
                    pe.wait_ge(self.pt_low.sem, self.pt_low.at(j + 1))
                    if past(j - 1):
                        pe.wait_ge(self.o_low.sem, self.o_low.at(j - 1))
                    for s in range(1 if b == "A" else 2):
                        terms = [(c, vv, pp) for c in range(nkeys // P)
                                 for vv, pp in ((v_high, pt_high), (v_high, pt_low), (v_low, pt_high))]
                        for a, (c, vv, pp) in enumerate(terms):
                            m = pe.matmul(ps[:, 4 + j % 2, s * P:(s + 1) * P], vv[:, key // P + c, vt * P:(vt + 1) * P],
                                          pp[:, s, c * P:(c + 1) * P], start=a == 0, stop=a == len(terms) - 1)
                    m.then_inc(self.mixed.sem, 1)
                scores(0)
                for j in range(J):
                    a, z = self.share[j]
                    half = (a + z + 1) // 2
                    if j + 1 < J:
                        scores(j + 1)
                    for w in range(a, half):
                        self.window_unit(pe, w)
                    flip(j)
                    if j:
                        mix(j - 1)
                    for w in range(half, z):
                        self.window_unit(pe, w)
                mix(J - 1)
                if b == "A":
                    for t in range(BT):
                        pe.wait_ge(self.sub_squared.sem, self.sub_squared.at(t + 1))
                        if past(t - 1):
                            pe.wait_ge(self.sub_rstd.sem, self.sub_rstd.at(2 * (t - 2) + 2))
                        pe.matmul(ps[:, t % 2, 0:T], ones[:, :], sq[:, t % 2, 0:T], start=True, stop=True).then_inc(self.sub_summed.sem, 1)

            def window_taken(self, act, w):
                kind, t, W = self.window[w]
                n = self.n_window + w
                split_next(act, split_high, n, n)
                act.wait_ge(used.sem, n + 1)
                if kind == "gate":
                    i = act.activation(gate[:, t, 0:W], ps[:, 6 + w % 2, 0:W], ACT.Tanh, scale=0.5)
                else:
                    i = act.activation(proj[:, t, 0:W], ps[:, 6 + w % 2, 0:W], ACT.Copy)
                i.then_inc(self.taken.sem, 1)

            def head_norm(self, act, i):
                W = self.prep[i][1]
                if past(i - 1):
                    act.wait_ge(self.head_normed.sem, self.head_normed.at(i - 1))
                make_rstd(act, self.head_summed, i + 1, self.head_rstd, ps[:, i % 2, 0:W], rstd[:, i % 2, 0:W], 1.0 / HD, 2 * i)

            def head_square(self, act, i):
                slot, W, _, _ = self.prep[i]
                if past(i - 1):
                    act.wait_ge(self.head_summed.sem, self.head_summed.at(i - 1))
                act.activation(sq[:, i % 2, 0:W], proj[:, slot, 0:W], ACT.Square).then_inc(self.head_squared.sem, 1)

            def high_of_qk(self, act, i):
                slot, W, hi, lo = self.prep[i]
                if self.roped:
                    act.wait_ge(self.turned.sem, self.turned.at(i + 1))
                act.activation(hi[:, 0:W], proj[:, slot, 0:W], ACT.Copy).then_inc(self.part_high.sem, 1)

            def scalar(self, act):
                b, T, J = self.b, self.T, self.J
                if not self.before:
                    n1 = STARTS[self.l, "Aproj"]
                    W = [T] * BT + [S_ALL] * 2 * self.nk
                    act.wait_ge(h_saved.sem, h_saved.at(16 * (self.l + 1)))

                    def four(i, base):
                        for c in range(4):
                            n = n1 + base + c
                            split_next(act, split_high, n + 4 * i, n)
                            act.wait_ge(used.sem, n + 4 * i + 1)
                            slot = 4 * i + base + c
                            w = W[base + c]
                            act.activation(proj[:, bass.ds(slot, 1), 0:w].rearrange("p a t -> p (a t)"), ps[:, 6 + c % 2, 0:w], ACT.Copy)\
                                .then_inc(self.projected.sem, 1)
                    four(0, 0)
                    repeat(act, 2, lambda i: four(i, BT))
                act.wait_ge(self.staged.sem, self.staged.at(self.staged_at))
                for tt in range(4):
                    act.wait_ge(self.v_turned.sem, self.v_turned.at(tt + 1))
                    act.activation(v_high[:, tt, 0:self.nk * P], ps[:, tt, 0:self.nk * P], ACT.Copy).then_inc(self.v_high.sem, 1)
                for i in self.head_items(0):
                    self.head_square(act, i)
                for kind, c, items in self.carriers():
                    if kind == "mix":
                        n = self.before.n_mix + c
                        split_next(act, split_high, n, n)
                        for i in self.head_items(c):
                            self.head_norm(act, i)
                        if c + 1 < BT:
                            for i in self.head_items(c + 1):
                                self.head_square(act, i)
                    else:
                        if c == 0 and self.before:
                            act.wait_ge(self.before.merged.sem, self.before.merged.at(KT))
                        self.window_taken(act, c)
                    for i in items:
                        self.high_of_qk(act, i)

                def exps(j):
                    nkeys = self.steps[j][3]
                    act.wait_ge(self.shifted.sem, self.shifted.at(j + 1))
                    if past(j - 1):
                        act.wait_ge(self.flipped.sem, self.flipped.at(j - 1))
                    if b == "D":
                        act.wait_ge(self.sunk.sem, self.sunk.at(j + 1))
                        act.activation(stat[:, j % 2, 4], stat[:, j % 2, 3], ACT.Exp)
                    for s in range(2):
                        e = act.activation(prob[:, j % 2, s, 0:nkeys], ps[:, s, 0:nkeys], ACT.Exp,
                                           bias=stat[:, j % 2, 1, s:s + 1], scale=SCALE, accum_out=stat[:, j % 2, 2, s:s + 1])
                    e.then_inc(self.expd.sem, 1)

                def high_of_probs(j):
                    nkeys, ns = self.steps[j][3], 1 if b == "A" else 2
                    act.wait_ge(self.flipped.sem, self.flipped.at(j + 1))
                    if past(j):
                        act.wait_ge(self.mixed.sem, self.mixed.at(j))
                    act.activation(pt_high[:, 0:ns, 0:nkeys], ps[:, 2:2 + ns, 0:nkeys], ACT.Copy).then_inc(self.pt_high.sem, 1)

                def high_of_out(j):
                    t, q, _, _ = self.steps[j]
                    act.wait_ge(self.mixed.sem, self.mixed.at(j + 1))
                    if b == "A":
                        o = act.activation(q_high[:, t, q:q + P], ps[:, 4 + j % 2, 0:P], ACT.Copy)
                    else:
                        for s in range(2):
                            rows = slice(s * HD, (s + 1) * HD)
                            o = act.activation(q_high[rows, t, q:q + P], ps[rows, 4 + j % 2, s * P:(s + 1) * P], ACT.Copy)
                    o.then_inc(self.o_high.sem, 1)
                exps(0)
                for j in range(J):
                    a, z = self.share[j]
                    half = (a + z + 1) // 2
                    if j + 1 < J:
                        exps(j + 1)
                    for w in range(a, half):
                        self.window_taken(act, w)
                    if j:
                        high_of_out(j - 1)
                    high_of_probs(j)
                    for w in range(half, z):
                        self.window_taken(act, w)
                high_of_out(J - 1)
                if b == "A":
                    for t in range(BT):
                        act.wait_ge(self.sub_joined.sem, self.sub_joined.at(t + 1))
                        if past(t - 1):
                            act.wait_ge(self.sub_summed.sem, self.sub_summed.at(t - 1))
                        act.activation(sq[:, t % 2, 0:T], prob[:, t // 2, t % 2, 0:T], ACT.Square).then_inc(self.sub_squared.sem, 1)
                        if t:
                            self.sub_norm(act, t - 1)
                    self.sub_norm(act, BT - 1)
                    for t in range(BT):
                        act.wait_ge(self.sub_scaled.sem, self.sub_scaled.at(t + 1))
                        act.activation(q_high[:, t, 0:T], prob[:, t // 2, t % 2, 0:T], ACT.Copy).then_inc(self.sub_high.sem, 1)

            def sub_norm(self, act, t):
                if past(t - 1):
                    act.wait_ge(self.sub_scaled.sem, self.sub_scaled.at(t - 1))
                make_rstd(act, self.sub_summed, t + 1, self.sub_rstd, ps[:, t % 2, 0:self.T], rstd[:, t % 2, 0:self.T], 1.0 / P, 2 * t)

            def rope(self, dve, i):
                slot = self.prep[i][0]
                x, r = proj[:, slot, 0:S_X], sq[:, i % 4 // 2, i % 2 * S_X:(i % 2 + 1) * S_X]
                if past(i - 3):
                    dve.wait_ge(self.turned.sem, self.turned.at(i - 3))
                dve.stream_shuffle(r, x, [(p + 16) % 32 for p in range(32)]).then_inc(self.shuffled.sem, 1)
                dve.wait_ge(self.shuffled.sem, self.shuffled.at(i + 1))
                dve.tensor_tensor(r, r, sm("sin"), ALU.mult).then_inc(self.sined.sem, 1)
                dve.wait_ge(self.cosined.sem, self.cosined.at(i + 1))
                dve.wait_ge(self.sined.sem, self.sined.at(i + 1))
                dve.tensor_tensor(x, x, r, ALU.add).then_inc(self.turned.sem, 1)

            def low_of_qk(self, dve, i):
                slot, W, hi, lo = self.prep[i]
                dve.wait_ge(self.part_high.sem, self.part_high.at(i + 1))
                dve.tensor_tensor(lo[:, 0:W], proj[:, slot, 0:W], hi[:, 0:W], ALU.subtract).then_inc(self.part_low.sem, 1)

            def head_scale(self, dve, i):
                slot, W, _, _ = self.prep[i]
                dve.wait_ge(self.head_rstd.sem, self.head_rstd.at(2 * i + 2))
                g = smv("qk_gain", self.l, DEPTH)[:, (1 if slot >= BT else 0):(2 if slot >= BT else 1)]
                dve.scalar_tensor_tensor(out=proj[:, slot, 0:W], in0=proj[:, slot, 0:W], scalar=g, in1=rstd[:, i % 2, 0:W],
                                         op0=ALU.mult, op1=ALU.mult).then_inc(self.head_normed.sem, 1)

            def merge(self, dve, c):
                b0, T = 6 - 2 * (c % 2), self.T
                dve.wait_ge(used.sem, self.n_mix + c + 1)
                for r in range(2):
                    m = 2 * c + r
                    z = ps[:, b0 + r, 0:T]
                    if self.index == 0:
                        dve.scalar_tensor_tensor(out=acc[:, m, 0:T], in0=gate[:, m, 0:T], scalar=1.0, in1=z,
                                                 op0=ALU.add, op1=ALU.mult).then_inc(self.merged.sem, 1)
                    else:
                        if past(m - 1):
                            dve.wait_ge(self.merged.sem, self.merged.at(m - 1))
                        dve.scalar_tensor_tensor(out=tmp[:, m % 2, 0:T], in0=gate[:, m, 0:T], scalar=1.0, in1=z,
                                                 op0=ALU.add, op1=ALU.mult).then_inc(self.gated.sem, 1)
                        dve.wait_ge(self.gated.sem, self.gated.at(m + 1))
                        dve.tensor_tensor(acc[:, m, 0:T], acc[:, m, 0:T], tmp[:, m % 2, 0:T], ALU.add).then_inc(self.merged.sem, 1)

            def vector(self, dve):
                b, T, J = self.b, self.T, self.J
                if not self.before:
                    n1 = STARTS[self.l, "Aproj"]

                    def four(i):
                        for c in range(4):
                            split_next(dve, split_low, n1 + c + 4 * i, n1 + c)
                    repeat(dve, 3, four)
                dve.wait_ge(self.staged.sem, self.staged.at(self.staged_at))
                for tt in range(4):
                    dve.wait_ge(self.v_high.sem, self.v_high.at(tt + 1))
                    w = self.nk * P
                    dve.tensor_tensor(v_low[:, tt, 0:w], ps[:, tt, 0:w], v_high[:, tt, 0:w], ALU.subtract).then_inc(self.v_low.sem, 1)
                heads_scaled = False
                for kind, c, items in self.carriers():
                    if kind == "mix":
                        n = self.before.n_mix + c
                        split_next(dve, split_low, n, n)
                        for i in self.head_items(c):
                            self.head_scale(dve, i)
                        self.before.merge(dve, c)
                    else:
                        n = self.n_window + c
                        split_next(dve, split_low, n, n)
                    if items and self.normed and not heads_scaled:
                        dve.wait_ge(self.head_normed.sem, self.head_normed.at(len(self.prep)))
                        heads_scaled = True
                    for i in items:
                        if self.roped:
                            self.rope(dve, i)
                        self.low_of_qk(dve, i)

                def row_max(j):
                    t, q, key, nkeys = self.steps[j]
                    both = ps[:, 0:2]
                    dve.wait_ge(self.scored.sem, self.scored.at(j + 1))
                    if b == "B" and key == 0:
                        n = self.l * 8 + j
                        dve.wait_ge(bias_landed[j % 2].sem, 16 * (n // 2 + 1))
                        dve.scalar_tensor_tensor(out=both[:, :, 0:S_X], in0=na_bias[:, j % 2], scalar=1.0 / SCALE,
                                                 in1=both[:, :, 0:S_X], op0=ALU.mult, op1=ALU.add).then_inc(self.masked.sem, 1)
                        dve.wait_ge(self.masked.sem, self.masked.at(j + 1))
                    if b == "D" and key == 0:
                        a = P - q
                        m = smv("mask", pattern="p (i s k) -> p i s k", i=2, s=2)[:, q // P]
                        dve.tensor_tensor(both[:, :, a:a + P], both[:, :, a:a + P], m, ALU.add).then_inc(self.masked.sem, 1)
                        dve.wait_ge(self.masked.sem, self.masked.at(j + 1))
                    if past(j - 1):
                        dve.wait_ge(self.probs.sem, self.probs.at(j - 1))
                    dve.tensor_reduce(stat[:, j % 2, 0], both[:, :, 0:nkeys], AX.X, ALU.max).then_inc(self.maxed.sem, 1)
                    dve.wait_ge(self.maxed.sem, self.maxed.at(j + 1))
                    if b == "D":
                        sink = smv("sink", self.l, DEPTH, "p (t s) -> p t s", s=2)[:, t]
                        dve.scalar_tensor_tensor(out=stat[:, j % 2, 5], in0=stat[:, j % 2, 0], scalar=SCALE, in1=sink,
                                                 op0=ALU.mult, op1=ALU.max).then_inc(self.sums.sem, 1)
                        dve.wait_ge(self.sums.sem, self.sums.at(3 * j + 1))
                        dve.tensor_tensor(stat[:, j % 2, 3], sink, stat[:, j % 2, 5], ALU.subtract).then_inc(self.sunk.sem, 1)
                        dve.tensor_scalar(stat[:, j % 2, 1], stat[:, j % 2, 5], -1.0, None, ALU.mult).then_inc(self.shifted.sem, 1)
                    else:
                        dve.tensor_scalar(stat[:, j % 2, 1], stat[:, j % 2, 0], -SCALE, None, ALU.mult).then_inc(self.shifted.sem, 1)

                def scale_probs(j):
                    nkeys = self.steps[j][3]
                    st = stat[:, j % 2]
                    total = st[:, 2]
                    dve.wait_ge(self.expd.sem, self.expd.at(j + 1))
                    if b == "D":
                        dve.tensor_tensor(st[:, 5], st[:, 2], st[:, 4], ALU.add).then_inc(self.sums.sem, 1)
                        dve.wait_ge(self.sums.sem, self.sums.at(3 * j + 2))
                        total = st[:, 5]
                    if b == "A":
                        dve.reciprocal(st[:, 3], total).then_inc(self.sums.sem, 1)
                        dve.wait_ge(self.sums.sem, self.sums.at(3 * j + 1))
                        dve.tensor_scalar(prob[:, j % 2, 0, 0:nkeys], prob[:, j % 2, 0, 0:nkeys], st[:, 3, 0:1], None, ALU.mult)
                        dve.tensor_scalar(st[:, 4, 1:2], st[:, 3, 1:2], lam[:, 5:6], None, ALU.mult).then_inc(self.sums.sem, 2)
                        dve.wait_ge(self.sums.sem, self.sums.at(3 * j + 3))
                        dve.scalar_tensor_tensor(out=prob[:, j % 2, 0, 0:nkeys], in0=prob[:, j % 2, 1, 0:nkeys], scalar=st[:, 4, 1:2],
                                                 in1=prob[:, j % 2, 0, 0:nkeys], op0=ALU.mult, op1=ALU.add).then_inc(self.probs.sem, 1)
                    else:
                        dve.reciprocal(st[:, 3], total).then_inc(self.sums.sem, 1 if b == "D" else 3)
                        dve.wait_ge(self.sums.sem, self.sums.at(3 * j + 3))
                        for s in range(2):
                            m = dve.tensor_scalar(prob[:, j % 2, s, 0:nkeys], prob[:, j % 2, s, 0:nkeys], st[:, 3, s:s + 1], None, ALU.mult)
                        m.then_inc(self.probs.sem, 1)

                def low_of_probs(j):
                    nkeys, ns = self.steps[j][3], 1 if b == "A" else 2
                    dve.wait_ge(self.pt_high.sem, self.pt_high.at(j + 1))
                    dve.tensor_tensor(pt_low[:, 0:ns, 0:nkeys], ps[:, 2:2 + ns, 0:nkeys], pt_high[:, 0:ns, 0:nkeys], ALU.subtract)\
                        .then_inc(self.pt_low.sem, 1)

                def low_of_out(j):
                    t, q, _, _ = self.steps[j]
                    dve.wait_ge(self.o_high.sem, self.o_high.at(j + 1))
                    if b == "A":
                        o = dve.tensor_tensor(q_low[:, t, q:q + P], ps[:, 4 + j % 2, 0:P], q_high[:, t, q:q + P], ALU.subtract)
                    else:
                        for s in range(2):
                            rows = slice(s * HD, (s + 1) * HD)
                            o = dve.tensor_tensor(q_low[rows, t, q:q + P], ps[rows, 4 + j % 2, s * P:(s + 1) * P],
                                                  q_high[rows, t, q:q + P], ALU.subtract)
                    o.then_inc(self.o_low.sem, 1)

                def splits(first, last):
                    for w in range(first, last):
                        split_next(dve, split_low, self.n_window + w, self.n_window + w)
                row_max(0)
                scale_probs(0)
                for j in range(J):
                    a, z = self.share[j]
                    half = (a + z + 1) // 2
                    if j + 1 < J:
                        row_max(j + 1)
                    splits(a, half)
                    if j + 1 < J:
                        scale_probs(j + 1)
                    if j:
                        low_of_out(j - 1)
                    low_of_probs(j)
                    splits(half, z)
                low_of_out(J - 1)
                if b == "A":
                    dve.wait_ge(self.o_low.sem, self.o_low.at(J))
                    for t in range(BT):
                        dve.tensor_tensor(prob[:, t // 2, t % 2, 0:T], q_high[:, t, 0:T], q_low[:, t, 0:T], ALU.add).then_inc(self.sub_joined.sem, 1)
                    for t in range(BT):
                        dve.wait_ge(self.sub_rstd.sem, self.sub_rstd.at(2 * t + 2))
                        dve.scalar_tensor_tensor(out=prob[:, t // 2, t % 2, 0:T], in0=prob[:, t // 2, t % 2, 0:T], scalar=lam[:, 6:7],
                                                 in1=rstd[:, t % 2, 0:T], op0=ALU.mult, op1=ALU.mult).then_inc(self.sub_scaled.sem, 1)
                    for t in range(BT):
                        dve.wait_ge(self.sub_high.sem, self.sub_high.at(t + 1))
                        dve.tensor_tensor(q_low[:, t, 0:T], prob[:, t // 2, t % 2, 0:T], q_high[:, t, 0:T], ALU.subtract).then_inc(self.sub_low.sem, 1)

            def pool(self, pool):
                if not self.before:
                    pool.wait_ge(self.norm.ready.sem, self.norm.ready.at(KT))
                    pool.dma_start(h_kept, h[:, :, :]).then_inc(h_saved.sem, 16)
                if self.roped:
                    for i, (slot, W, hi, lo) in enumerate(self.prep):
                        x = proj[:, slot, 0:S_X]
                        pool.wait_ge(self.shuffled.sem, self.shuffled.at(i + 1))
                        pool.tensor_tensor(x, x, sm("cos"), ALU.mult).then_inc(self.cosined.sem, 1)
                if self.b == "B":
                    pool.wait_ge(self.before.sub_low.sem, self.before.sub_low.at(BT))
                    for j in range(8):
                        if past(j - 1):
                            pool.wait_ge(self.masked.sem, self.masked.at(j - 1))
                        pool.dma_start(na_bias[:, j % 2], na_rows[self.l, j]).then_inc(bias_landed[j % 2].sem, 16)
                if self.index == 3:
                    pool.wait_ge(self.part_low.sem, self.part_low.at(len(self.prep)))
                    pool.wait_ge(self.v_turned.sem, self.v_turned.at(4))
                    pool.dma_start(h[:, :, :], h_kept).then_inc(h_back.sem, 16)

        class Merge(Stage):
            def __init__(self, layer, T, branch):
                self.l, self.T, self.branch = layer, T, branch
                self.high = signals.new("merged_high_made", KT)
                self.low = signals.new("merged_low_made", KT)

            def tensor(self, pe):
                pe.wait_ge(self.branch.y_ready.sem, self.branch.y_ready.at(self.branch.y_count))
                for c in range(BT):
                    self.branch.mix_unit(pe, c)

            def scalar(self, act):
                for c in range(BT):
                    n = self.branch.n_mix + c
                    split_next(act, split_high, n, n)
                    if c == 0:
                        act.wait_ge(self.branch.o_low.sem, self.branch.o_low.at(self.branch.J))
                    for m in (2 * c, 2 * c + 1):
                        act.wait_ge(self.branch.merged.sem, self.branch.merged.at(m + 1))
                        act.activation(a_high[:, m, 0:self.T], acc[:, m, 0:self.T], ACT.Copy, scale=0.5).then_inc(self.high.sem, 1)

            def vector(self, dve):
                for c in range(BT):
                    n = self.branch.n_mix + c
                    split_next(dve, split_low, n, n)
                    self.branch.merge(dve, c)
                    for m in (2 * c, 2 * c + 1):
                        dve.wait_ge(self.high.sem, self.high.at(m + 1))
                        dve.scalar_tensor_tensor(out=a_low[:, m, 0:self.T], in0=acc[:, m, 0:self.T], scalar=0.5, in1=a_high[:, m, 0:self.T],
                                                 op0=ALU.mult, op1=ALU.subtract).then_inc(self.low.sem, 1)

        class Out(Result):
            def __init__(self, layer, T, merge):
                self.n0, self.T, self.merge = STARTS[layer, "out"], T, merge
                self.result_signals()

            def tensor(self, pe):
                for m in range(KT):
                    if past(m - 1):
                        pe.wait_ge(self.copied.sem, self.copied.at(m - 1))
                    product(pe, self.n0 + m, self.n0 + m, [(ps[:, m % 2, 0:self.T], [(k, k) for k in range(KT)])],
                            lambda k: a_high[:, k, 0:self.T], lambda k: a_low[:, k, 0:self.T],
                            before=(lambda k: pe.wait_ge(self.merge.low.sem, self.merge.low.at(k + 1))) if m == 0 else None)

            def scalar(self, act):
                for m in range(KT):
                    split_next(act, split_high, self.n0 + m, self.n0 + m)
                    act.wait_ge(used.sem, self.n0 + m + 1)
                    self.take(act, m, m % 2)

            def vector(self, dve):
                for m in range(KT):
                    split_next(dve, split_low, self.n0 + m, self.n0 + m)
                    self.add(dve, m, m % 2)

        h_ready = None
        for layer in range(DEPTH):
            last = layer == DEPTH - 1
            stages.append(Modulation(layer))
            for j in range(3):
                T = S_ALL if j < 2 or not last else S_X
                norm = Norm(layer, j, T, h_ready)
                stages.append(norm)
                if j == 1:
                    T = S_X if last else S_ALL
                    branches = []
                    for i in range(len(BRANCHES)):
                        branches.append(Branch(layer, i, T, norm, branches[-1] if branches else None))
                    stages += branches
                    merge = Merge(layer, T, branches[-1])
                    stages.append(merge)
                    result = Out(layer, T, merge)
                else:
                    hidden = Hidden(layer, j, T, norm)
                    stages.append(hidden)
                    result = Down(layer, j, T, hidden)
                stages.append(result)
                residual = Residual(layer, j, T, result)
                stages.append(residual)
                h_ready = residual.h_ready
        if stop:
            del stages[stop:]

        block = ctx.enter_context(nc.Block())

        @block.sync
        def _(sp):
            sp.dma_start(h[:, :, :], tokens).then_inc(loaded.sem, 16)
            sp.dma_start(smalls[:, :], small).then_inc(loaded.sem, 16)
            n = 0
            down = {STARTS[l, f"down{j}"] for l in range(DEPTH) for j in (0, 2)}
            ends = sorted(down | {d + 4 * KT for d in down})
            for end in ends:
                width = UNIT if end in down else DOWN_WIDTH

                def four(i, n=n, width=width):
                    for c in range(RAW_SLOTS):
                        fetch(sp, n + c + RAW_SLOTS * i, width, c)
                repeat(sp, (end - n) // RAW_SLOTS, four)
                n = end
            for k in range(KT):
                sp.wait_ge(h_ready.sem, h_ready.at(k + 1))
                sp.dma_start(out[:, k], h[:, k, 0:S_X]).then_inc(stored.sem, 16)
            sp.wait_ge(stored.sem, 16 * KT)

        @block.gpsimd
        def _(pool):
            pool.memset(ones[:, :], 1.0).then_inc(ones_set.sem, 1)
            pool.memset(eps[:, :], EPS).then_inc(ones_set.sem, 1)
            for st in stages:
                st.pool(pool)

        @block.scalar
        def _(act):
            act.wait_ge(ones_set.sem, ones_set.at(2))
            split_high(act, 0, 0)
            split_high(act, 1, 1)
            for st in stages:
                st.scalar(act)

        @block.vector
        def _(dve):
            split_low(dve, 0, 0)
            split_low(dve, 1, 1)
            dve.wait_ge(loaded.sem, loaded.at(32))
            for st in stages:
                st.vector(dve)

        @block.tensor
        def _(pe):
            pe.wait_ge(ones_set.sem, ones_set.at(2))
            pe.wait_ge(loaded.sem, loaded.at(32))
            for st in stages:
                st.tensor(pe)


def segments_of_w_in():
    widths = [("a_q", BW), ("a_k", BW), ("a_v", BW), ("b_q", BW), ("b_k", BW), ("b_v", BW),
              ("c_q", BW), ("c_k", P), ("c_v", P), ("d_q", BW), ("d_k", P), ("d_v", P)] + [(f"gate{i}", D) for i in range(4)]
    seg, at = {}, 0
    for name, w in widths:
        seg[name] = slice(at, at + w)
        at += w
    return seg


GQA_ORDER = np.concatenate([np.arange(HD) + HD * hh for t in range(4) for hh in (t, 4 + t)])


def k8(w):
    n = w.shape[1] // P
    return w.reshape(KT, P, n, P).transpose(2, 1, 0, 3).reshape(n, P, UNIT)


def lay_out(inp):
    a = {k: np.asarray(v) for k, v in inp.items()}
    f = np.float32
    tokens = np.concatenate([a["x"][0], a["ctx"][0]]).T.reshape(KT, P, S_ALL).transpose(1, 0, 2)
    _, total = unit_starts()
    weights = np.zeros((total, P, UNIT), f)
    n = 0
    seg = segments_of_w_in()

    def put(units):
        nonlocal n
        weights[n:n + len(units), :, :units.shape[-1]] = units
        n += len(units)
    for l in range(DEPTH):
        g = N_MOD * D // MOD_GROUP
        put(a["w_mod"][l].reshape(4, 2, P, g, MOD_GROUP).transpose(3, 0, 2, 1, 4).reshape(4 * g, P, UNIT))

        def ffn(j):
            both = np.stack([k8(a["ffn_w_gate"][l, j]), k8(a["ffn_w_up"][l, j])], 1)
            put(both.reshape(2 * FT, P, UNIT))
            w = a["ffn_w_down"][l, j].reshape(FT, P, KT, P)
            for m in range(KT):
                k0 = 0
                for nk in DOWN_K:
                    put(w[k0:k0 + nk, :, m].transpose(1, 0, 2).reshape(1, P, nk * P))
                    k0 += nk
        ffn(0)
        w_in = a["w_in"][l]
        projections, gates, mixes = [], [], []
        for i, b in enumerate(BRANCHES.lower()):
            q, wb = w_in[:, seg[b + "_q"]], a["w_branch"][l, i]
            if b in "cd":
                q, wb = q[:, GQA_ORDER], wb[GQA_ORDER]
            projections.append(np.concatenate([k8(q), k8(w_in[:, seg[b + "_k"]]), k8(w_in[:, seg[b + "_v"]])]))
            gates.append(k8(w_in[:, seg[f"gate{i}"]]))
            mixes.append(wb.reshape(BT, P, 4, 2, P).transpose(2, 1, 3, 0, 4).reshape(4, P, UNIT))
        put(projections[0])
        for i in range(4):
            put(gates[i])
            if i < 3:
                put(projections[i + 1])
            put(mixes[i])
        put(k8(a["w_out"][l]))
        ffn(1)
    assert n == total
    s = {}
    s["c"] = np.stack([a["c"][0].reshape(KT, P), a["c_ctx"].reshape(KT, P)], -1).transpose(1, 0, 2)
    s["b_mod"] = a["b_mod"].reshape(DEPTH, MODT, P).transpose(2, 0, 1)
    s["gain"] = a["norm_gain"].reshape(DEPTH, 6, KT, P).transpose(3, 0, 1, 2)
    s["lam"] = np.broadcast_to(a["diff_lambda"].reshape(1, -1), (P, DEPTH * 4 * HD))
    s["subln"] = a["diff_subln"].T
    s["qk_gain"] = np.concatenate([a["qk_norm"]] * 2, -1).transpose(2, 0, 1)
    s["sink"] = np.broadcast_to(a["sink"].reshape(1, DEPTH, 2, 4).transpose(0, 1, 3, 2).reshape(1, -1), (P, DEPTH * 8))
    t = np.arange(S_X)
    inv = (f(10000.0) ** (-np.arange(HD // 4, dtype=f) / f(HD // 4))).astype(f)
    ang = np.stack([(t // GRID_W).astype(f)[:, None] * inv, (t % GRID_W).astype(f)[:, None] * inv], 1)
    cos, sin = np.cos(ang), np.sin(ang)
    row = np.arange(P) % HD
    part, half, fr = row // 32, row % 32 // 16, row % 16
    s["cos"] = cos[:, part, fr].T
    s["sin"] = (sin[:, part, fr] * np.where(half, 1, -1)).T
    s["ident"] = np.eye(P)
    s["pairs"] = np.kron(np.eye(2), np.ones((HD, HD)))
    pick = np.zeros((P, 2))
    pick[[0, 2], 0] = pick[[1, 3], 1] = 1
    s["pick"] = pick
    q, k = np.arange(P)[:, None], np.arange(P)[None]
    m = np.stack([np.where(k + P - q <= SWA_WINDOW, 0, MASKED), np.where(q + P - k <= SWA_WINDOW, 0, MASKED)], 1)
    s["mask"] = np.stack([m, m], 2)
    small = np.concatenate([np.asarray(s[name]).reshape(P, w).astype(f) for name, (_, w) in SMALL.items()], 1)
    rows = S_X // GRID_W
    kh = min(NA_KH, rows)
    r, c = t // GRID_W, t % GRID_W
    r0, c0 = np.clip(r - kh // 2, 0, rows - kh), np.clip(c - NA_KW // 2, 0, GRID_W - NA_KW)
    inside = ((r[None] >= r0[:, None]) & (r[None] < r0[:, None] + kh) & (c[None] >= c0[:, None]) & (c[None] < c0[:, None] + NA_KW))
    dr = np.where(inside, r[None] - r[:, None] + NA_KH - 1, 0)
    dc = np.where(inside, c[None] - c[:, None] + NA_KW - 1, 0)
    na = np.where(inside, a["na_bias"][:, :, dr, dc], f(MASKED))
    na = na.reshape(DEPTH, 4, 2, 2, P, S_X).transpose(0, 1, 3, 4, 2, 5).reshape(DEPTH, 8, P, 2, S_X)
    return {"tokens": tokens, "small": small, "weights": weights, "na_rows": na}


def kernel(**inputs):
    import concourse.bacc as bacc
    from concourse.bass_utils import run_bass_kernel_spmd

    nc = bacc.Bacc("TRN2", target_bir_lowering=False, num_devices=1)
    arrays, args = {}, []
    for name, v in lay_out(inputs).items():
        v = np.ascontiguousarray(v, dtype=np.float32)
        arrays[f"in_{name}"] = v
        args.append(nc.dram_tensor(f"in_{name}", v.shape, F32, kind="ExternalInput").ap())
    args.append(nc.dram_tensor("h_kept", (P, KT, S_ALL), F32, kind="Internal").ap())
    args.append(nc.dram_tensor("out_tokens", (P, KT, S_X), F32, kind="ExternalOutput").ap())
    build(nc, *args)
    r = run_bass_kernel_spmd(nc, [arrays], core_ids=[0])
    got = r.results[0]["out_tokens"]
    return got.transpose(1, 0, 2).reshape(D, S_X).T.reshape(1, S_X, D)
```

```python
import math
from contextlib import ExitStack

import numpy as np
import concourse.bass as bass
from concourse import mybir

F32 = mybir.dt.float32
F32R = mybir.dt.float32r
ALU = mybir.AluOpType
ACT = mybir.ActivationFunctionType
AX = mybir.AxisListType

P = 128
D = 1024
DEPTH = 2
S_X = 256
S_C = 256
S_ALL = S_X + S_C
GRID_W = 64
HD = 64
KT = D // P
BW = D // 2
BT = BW // P
FF = ((8 * D // 3 + 255) // 256) * 256
FT = FF // P
N_MOD = 9
MODT = N_MOD * KT
NA_KH, NA_KW = 8, 16
SWA_WINDOW = 128
EPS = 1e-6
SCALE = HD ** -0.5
MASKED = -1e30
LN_EXP_SET = 6

UNIT = 8 * P
SLOTS = 4
AHEAD = 2
DOWN_K = (6, 5, 6, 5)
DOWN_WIDTH = max(DOWN_K) * P
MOD_GROUP = 4
MOD_GROUPS = DEPTH * MODT // MOD_GROUP

BRANCHES = "ABCD"
AHEAD_OF = {True: (4, 2, 3, 2), False: (4, 3, 4, 3)}
BEHIND_OF = (2, 1, 1, 1)
N_K = {"A": BT, "B": BT, "C": 1, "D": 1}

SMALL = {}
_at = 0
for _name, _w in (("c", KT * 2), ("b_mod", DEPTH * MODT * 2), ("gain", DEPTH * 6 * KT), ("lam", DEPTH * 4 * HD),
                  ("subln", DEPTH), ("qk_gain", DEPTH * 2), ("sink", DEPTH * 8), ("cos", S_X), ("sin", S_X),
                  ("ident", P), ("pairs", P), ("pick", 2), ("mask", 2 * 2 * P)):
    SMALL[_name] = (_at, _w)
    _at += _w
SMALL_W = _at


UP_ALONE = [(f, g) for f in range(2) for g in range(2)]
UP_BESIDE = [(0, 0), None, None, (0, 1), None, None, (1, 0), (1, 1)]
DOWN_ALONE = [(r, part) for r in range(2) for part in range(4)]
DOWN_BESIDE = [(0, 0), None, (0, 1), None, (0, 2), None, (0, 3), None, (1, 0), (1, 1), (1, 2), (1, 3)]
PICK_AFTER = (1, 0)


def beside(layer):
    return layer == 0


GROUPS_BESIDE = {"up": FT // 2, "down": KT // 2}
MOD_FIRST = MOD_GROUPS - 2 * sum(GROUPS_BESIDE.values())
N_FIRST = MOD_GROUP * MOD_FIRST
MOD_START, _at = {}, MOD_FIRST
for _name in ("up0", "down0", "up2", "down2"):
    MOD_START[_name] = _at
    _at += GROUPS_BESIDE[_name[:-1]]


def layer_units(layer):
    up, down = FT // 2 * len(UP_BESIDE if beside(layer) else UP_ALONE), KT // 2 * len(DOWN_BESIDE if beside(layer) else DOWN_ALONE)
    out = [("mod", N_FIRST)] if layer == 0 else []
    out += [("up0", up), ("down0", down), ("Aproj", 3 * BT)]
    for b, follows in zip(BRANCHES, BRANCHES[1:] + " "):
        out += [(b + "window", KT + (BT + 2 * N_K[follows] if follows in BRANCHES else 0)), (b + "mix", BT)]
    return out + [("out", KT), ("up2", up), ("down2", down)]


def unit_starts():
    at, starts = 0, {}
    for layer in range(DEPTH):
        for name, n in layer_units(layer):
            starts[layer, name] = at
            at += n
    return starts, at


STRETCHES = [("up0",), ("down0",), ("Aproj",) + tuple(b + kind for b in BRANCHES for kind in ("window", "mix")) + ("out",),
             ("up2",), ("down2",)]


def narrow(unit):
    return unit is not None and unit[1] >= AHEAD


class Signal:

    def __init__(self, sem, base):
        self.sem, self.base = sem, base

    def at(self, k):
        return self.base + k


class Signals:

    def __init__(self, nc, ctx):
        self.nc, self.ctx, self.sems, self.counts = nc, ctx, {}, {}

    def new(self, name, total):
        if name not in self.sems:
            self.sems[name] = self.ctx.enter_context(self.nc.semaphore(name))
            self.counts[name] = 0
        s = Signal(self.sems[name], self.counts[name])
        self.counts[name] += total
        return s


def past(k):
    return not isinstance(k, int) or k > 0


def repeat(eng, count, body):
    body(0)
    if count == 2:
        body(1)
    elif count > 2:
        with eng.Fori(1, count) as i:
            body(i)


def build(nc, tokens, small, weights, na_rows, h_kept, out, stop=None):
    STARTS, N_UNITS = unit_starts()
    with ExitStack() as ctx:
        start = (nc.sbuf_base + 31) // 32 * 32
        slab = ctx.enter_context(nc.sbuf_tensor("slab", [P, 207 * 256 - 40], F32))
        del slab

        def place(name, shape, dt, at):
            return nc.alloc_sbuf_tensor_at(name, [P] + shape, dt, offset=start + at)

        KB = 1024
        at = 0
        raw = [place(f"raw{i}", [8, P], F32, at + 4 * KB * i) for i in range(SLOTS)]
        w_low = [place(f"w_low{i}", [8, P], F32R, at + 4 * KB * i) for i in range(SLOTS)]
        at += 16 * KB
        w_high = place("w_high", [SLOTS, 8, P], F32R, at); at += 16 * KB
        u_high = place("u_high", [KT, S_ALL], F32R, at)
        u_low = place("u_low", [KT, S_ALL], F32R, at + 16 * KB)
        y = place("y", [KT, S_ALL], F32, at); at += 32 * KB
        h = place("h", [KT, S_ALL], F32, at); at += 16 * KB
        big = at; at += 88 * KB
        acc_at = at; at += 16 * KB
        smalls = place("smalls", [SMALL_W], F32, at); at += (SMALL_W * 4 + 31) // 32 * 32
        mod = place("mod", [DEPTH * MODT, 2], F32, at); at += DEPTH * MODT * 8
        pre = place("pre", [3 * DEPTH, KT, 2], F32, at); at += 3 * DEPTH * KT * 8
        post = place("post", [3 * DEPTH, KT, 2], F32, at); at += 3 * DEPTH * KT * 8
        c_split = place("c_split", [KT, 4], F32R, at); at += KT * 16
        sq = place("sq", [2, S_ALL], F32, at); at += 4 * KB
        rstd = place("rstd", [2, S_ALL], F32, at)
        ssq = place("ssq", [S_ALL], F32, at + 2 * KB)
        na_bias = place("na_bias", [2, 2, S_X], F32, at); at += 4 * KB
        tmp = place("tmp", [2, S_ALL], F32, at); at += 4 * KB
        ones = place("ones", [P], F32, at); at += 512
        stat = place("stat", [2, 6, 2], F32, at); at += 96
        lam = place("lam", [DEPTH, 8], F32, at); at += DEPTH * 32
        eps = place("eps", [2], F32, at); at += 32
        assert start + at <= nc.sbuf_usable_end, (start + at, nc.sbuf_usable_end)
        hid_high = place("hid_high", [FT, S_ALL], F32R, big)
        hid_low = place("hid_low", [FT, S_ALL], F32R, big + 44 * KB)
        first_at = [w_at + 4 * KB * i for w_at, count in ((32 * KB, 8), (big, N_FIRST - 8)) for i in range(count)]
        first_raw = [place(f"first_raw{i}", [8, P], F32, a) for i, a in enumerate(first_at)]
        first_low = [place(f"first_low{i}", [8, P], F32R, a) for i, a in enumerate(first_at)]
        proj = place("proj", [12, S_ALL], F32, big - 16 * KB)
        at_mix = big + 8 * KB
        q_high = place("q_high", [BT, S_ALL], F32R, at_mix)
        q_low = place("q_low", [BT, S_ALL], F32R, at_mix + 8 * KB)
        k_high = place("k_high", [BT, S_ALL], F32R, at_mix + 16 * KB)
        k_low = place("k_low", [BT, S_ALL], F32R, at_mix + 24 * KB)
        v_high = place("v_high", [4, BW], F32R, at_mix + 32 * KB)
        v_low = place("v_low", [4, BW], F32R, at_mix + 40 * KB)
        a_high = place("a_high", [KT, S_ALL], F32R, at_mix + 16 * KB)
        a_low = place("a_low", [KT, S_ALL], F32R, at_mix + 32 * KB)
        o_a = place("o_a", [BT, S_ALL], F32, at_mix)
        head_rstd = place("head_rstd", [4, S_ALL], F32, at_mix + 48 * KB)
        pt_high = place("pt_high", [2, 4 * P], F32R, at_mix + 48 * KB)
        pt_low = place("pt_low", [2, 4 * P], F32R, at_mix + 52 * KB)
        prob = place("prob", [2, 2, S_ALL], F32, at_mix + 56 * KB)
        gate = place("gate", [KT, S_ALL], F32, at_mix + 64 * KB)
        acc = place("acc", [KT, S_ALL], F32, acc_at)
        silu_g = place("silu_g", [2, S_ALL], F32, acc_at)
        hid = place("hid", [2, S_ALL], F32, acc_at + 4 * KB)
        mod_row = place("mod_row", [MOD_GROUP * P], F32, acc_at + 8 * KB)
        silu_c = place("silu_c", [KT, 2], F32, acc_at)

        ps = ctx.enter_context(nc.psum_tensor("ps", [P, 8, 512], F32))

        def sm(name, layer=0, n=1):
            a, w = SMALL[name]
            w //= n
            return smalls[:, a + layer * w:a + (layer + 1) * w]

        def smv(name, layer=0, n=1, pattern=None, **k):
            v = sm(name, layer, n)
            return v.rearrange(pattern, **k) if pattern else v

        ident = sm("ident")
        pairs = sm("pairs")
        gain_of = [smv("gain", l, DEPTH, "p (a k) -> p a k", a=6) for l in range(DEPTH)]
        b_mod = smv("b_mod", pattern="p (t s) -> p t s", s=2)

        signals = Signals(nc, ctx)
        loaded = signals.new("inputs_loaded", 32)
        first_landed = [signals.new(f"first_landed{i}", 0) for i in range(MOD_FIRST)]
        landed = [signals.new(f"weights_landed{i}", 0) for i in range(SLOTS)]
        high_made = signals.new("weights_high_made", 0)
        low_made = signals.new("weights_low_made", 0)
        used = signals.new("weights_used", 0)
        ones_set = signals.new("ones_set", 3)
        stored = signals.new("stored", 0)
        bias_landed = [signals.new(f"bias_landed{i}", 0) for i in range(2)]
        h_saved = signals.new("h_saved", 0)
        h_back = signals.new("h_back", 0)

        def fetch(sp, n, width, j):
            if not isinstance(n, int) or n >= N_FIRST + SLOTS:
                sp.wait_ge(used.sem, n - SLOTS + 1)
            src = weights[n, :, 0:width] if isinstance(n, int) else weights[bass.ds(n, 1), :, 0:width].rearrange("a p w -> (a p) w")
            sp.dma_start(raw[j][:, 0:width // P].rearrange("p a b -> p (a b)"), src).then_inc(landed[j].sem, 16)

        def split_high(act, n, n0, width=8):
            s = n0 % SLOTS
            if n0 < N_FIRST:
                act.wait_ge(first_landed[n0 // MOD_GROUP].sem, 16 * MOD_GROUP)
            else:
                act.wait_ge(landed[s].sem, ((n0 - N_FIRST) // SLOTS + 1) * 16 + (n - n0) * (16 // SLOTS))
            if SLOTS <= n0 < N_FIRST + SLOTS:
                act.wait_ge(used.sem, n - SLOTS + 1)
            act.activation(w_high[:, s, 0:width], (raw[s] if n0 >= N_FIRST else first_raw[n0])[:, 0:width], ACT.Copy).then_inc(high_made.sem, 1)

        def split_low(dve, n, n0, width=8):
            dve.wait_ge(high_made.sem, n + 1)
            s = n0 % SLOTS
            low, whole = (w_low[s], raw[s]) if n0 >= N_FIRST else (first_low[n0], first_raw[n0])
            dve.tensor_tensor(low[:, 0:width], whole[:, 0:width],
                              w_high[:, s, 0:width], ALU.subtract).then_inc(low_made.sem, 1)

        def product_high(pe, n, n0, outs, x_high, x_low, first=True, before=None):
            s = n0 % SLOTS
            pe.wait_ge(high_made.sem, n + 1)
            for o, terms in outs:
                for a, (w, x) in enumerate(terms):
                    if before:
                        before(x)
                    pe.matmul(o, w_high[:, s, w], x_high(x), start=first and a == 0, stop=False)
                    pe.matmul(o, w_high[:, s, w], x_low(x), start=False, stop=False)

        def product_low(pe, n, n0, outs, x_high, last=True):
            s = n0 % SLOTS
            pe.wait_ge(low_made.sem, n + 1)
            for o, terms in outs:
                for a, (w, x) in enumerate(terms):
                    done = pe.matmul(o, w_low[s][:, w], x_high(x), start=False, stop=last and a == len(terms) - 1)
            done.then_inc(used.sem, 1)

        def product(pe, n, n0, outs, x_high, x_low, first=True, last=True, before=None):
            product_high(pe, n, n0, outs, x_high, x_low, first, before)
            product_low(pe, n, n0, outs, x_high, last)

        def split_next(act_or_dve, f, n, n0, width=8):
            if n0 + AHEAD < N_UNITS:
                f(act_or_dve, n + AHEAD, n0 + AHEAD, width)

        mod_copied = signals.new("mod_row_copied", 0)
        mod_turned = signals.new("mod_turned", 0)
        mod_added = signals.new("mod_added", 0)
        c_parts = signals.new("c_parts", 2)

        def mod_unit(pe, n, n0, group, k2, bank=4):
            s = n0 % SLOTS
            if k2 == 0 and n0 >= N_FIRST:
                pe.wait_ge(mod_copied.sem, group)
            elif k2 == 0 and group > 1:
                pe.wait_ge(mod_copied.sem, group - 1)
            for part, w in ((high_made, w_high[:, s]), (low_made, w_low[s] if n0 >= N_FIRST else first_low[n0])):
                pe.wait_ge(part.sem, n + 1)
                for a in range(2):
                    done = pe.matmul(ps[0:4, bank], c_split[:, 2 * k2 + a], w[:, 4 * a:4 * a + 4].rearrange("p a b -> p (a b)"),
                                     start=k2 == 0 and part is high_made and a == 0, stop=k2 == 3 and part is low_made and a == 1)
            done.then_inc(used.sem, 1)

        def mod_copy(act, n, group, bank=4):
            act.wait_ge(used.sem, n + 1)
            if past(group):
                act.wait_ge(mod_turned.sem, group)
            act.activation(mod_row[0:4], ps[0:4, bank], ACT.Copy).then_inc(mod_copied.sem, 1)

        def mod_turn(pe, group):
            pe.wait_ge(mod_copied.sem, group + 1)
            if past(group):
                pe.wait_ge(mod_added.sem, group)
            for c in range(MOD_GROUP):
                t = pe.matmul(ps[:, 5, 2 * c:2 * c + 2], mod_row[0:4, c * P:(c + 1) * P], sm("pick")[0:4],
                              start=c == 0, stop=c == MOD_GROUP - 1, skip_group_check=True)
            t.then_inc(mod_turned.sem, 1)

        def mod_add(dve, group):
            dve.wait_ge(mod_turned.sem, group + 1)
            tiles = bass.ds(MOD_GROUP * group, MOD_GROUP)
            dve.tensor_tensor(mod[:, tiles], ps[:, 5, 0:2 * MOD_GROUP].rearrange("p (r s) -> p r s", s=2), b_mod[:, tiles], ALU.add)\
                .then_inc(mod_added.sem, 1)

        stages = []

        class Stage:
            def tensor(self, pe): pass
            def scalar(self, act): pass
            def vector(self, dve): pass
            def pool(self, pool): pass

        class Modulation(Stage):
            def __init__(self):
                self.c_silu = signals.new("c_silu", 1)
                self.lam_steps = signals.new("lam_steps", 5 * DEPTH)
                self.lam_exp = signals.new("lam_exp", DEPTH)

            def tensor(self, pe):
                pe.wait_ge(c_parts.sem, c_parts.at(2))

                for n in range(N_FIRST):
                    mod_unit(pe, n, n, n // 4, n % 4, 4 + n // 4 % 2 * 2)
                    if n > 4 and n % 4 == 1:
                        mod_turn(pe, n // 4 - 1)
                mod_turn(pe, MOD_FIRST - 1)

            def scalar(self, act):
                act.wait_ge(loaded.sem, loaded.at(32))
                act.activation(silu_c[:, :, :], smv("c", pattern="p (k s) -> p k s", s=2), ACT.Silu).then_inc(self.c_silu.sem, 1)
                for l in range(DEPTH):
                    act.wait_ge(self.lam_steps.sem, self.lam_steps.at(5 * l + 3))
                    act.activation(lam[:, l, 2:4], lam[:, l, 0:2], ACT.Exp).then_inc(self.lam_exp.sem, 1)
                for i in range(MOD_FIRST):
                    for k2 in range(4):
                        split_next(act, split_high, 4 * i + k2, 4 * i + k2)
                    mod_copy(act, 4 * i + 3, i, 4 + i % 2 * 2)

            def vector(self, dve):
                dve.wait_ge(self.c_silu.sem, self.c_silu.at(1))
                dve.tensor_copy(c_split[:, :, 0:2], silu_c[:, :, :]).then_inc(c_parts.sem, 1)
                dve.wait_ge(c_parts.sem, c_parts.at(1))
                dve.tensor_tensor(c_split[:, :, 2:4], silu_c[:, :, :], c_split[:, :, 0:2], ALU.subtract).then_inc(c_parts.sem, 1)
                st = self.lam_steps
                for l in range(DEPTH):
                    lam_init = 0.8 - 0.6 * math.exp(-0.3 * l)
                    dl = smv("lam", l, DEPTH, "p (a b d) -> p a b d", a=2, b=2)
                    prod = tmp[:, l, 0:2 * HD].rearrange("p (a d) -> p a d", a=2)
                    dve.tensor_tensor(prod, dl[:, :, 0], dl[:, :, 1], ALU.mult).then_inc(st.sem, 1)
                    dve.wait_ge(st.sem, st.at(5 * l + 1))
                    dve.tensor_reduce(lam[:, l, 0:2], prod, AX.X, ALU.add).then_inc(st.sem, 1)
                    dve.tensor_scalar(lam[:, l, 6:7], smv("subln", l, DEPTH), 1.0 - lam_init, None, ALU.mult).then_inc(st.sem, 1)
                    dve.wait_ge(self.lam_exp.sem, self.lam_exp.at(l + 1))
                    dve.tensor_tensor(lam[:, l, 4:5], lam[:, l, 3:4], lam[:, l, 2:3], ALU.subtract).then_inc(st.sem, 1)
                    dve.wait_ge(st.sem, st.at(5 * l + 4))
                    dve.tensor_scalar(lam[:, l, 5:6], lam[:, l, 4:5], -lam_init, None, ALU.add).then_inc(st.sem, 1)
                for i in range(MOD_FIRST):
                    for k2 in range(4):
                        split_next(dve, split_low, 4 * i + k2, 4 * i + k2)
                    if i:
                        mod_add(dve, i - 1)
                mod_add(dve, MOD_FIRST - 1)

        def segments(T):
            return [(0, 0, S_X)] + ([(1, S_X, S_ALL)] if T > S_X else [])

        class Norm(Stage):
            def __init__(self, layer, j, T, h_ready):
                self.l, self.j, self.T, self.h_ready = layer, j, T, h_ready
                self.shift = layer * MODT + 3 * j * KT
                self.derived = signals.new("pre_derived", 1)
                self.squared = signals.new("norm_squared", KT)
                self.summed = signals.new("norm_summed", KT)
                self.rstd_steps = signals.new("norm_rstd", 2)
                self.scaled = signals.new("norm_scaled", KT)
                self.high = signals.new("u_high_made", KT)
                self.ready = signals.new("u_ready", KT)

            def scalar(self, act):
                if self.h_ready:
                    self.statistics(act)
                T = self.T
                for k in range(KT):
                    act.wait_ge(self.scaled.sem, self.scaled.at(k + 1))
                    for s, a, b in segments(T):
                        i = act.activation(u_high[:, k, a:b], tmp[:, k % 2, a:b], ACT.Identity,
                                           bias=mod[:, self.shift + k, s:s + 1])
                    i.then_inc(self.high.sem, 1)

            def statistics(self, act):
                T = self.T
                for k in range(KT):
                    if self.h_ready:
                        act.wait_ge(self.h_ready.sem, self.h_ready.at(k + 1))
                    if past(k - 1):
                        act.wait_ge(self.summed.sem, self.summed.at(k - 1))
                    act.activation(sq[:, k % 2, 0:T], h[:, k, 0:T], ACT.Square).then_inc(self.squared.sem, 1)
                make_rstd(act, self.summed, KT, self.rstd_steps, ps[:, 7, 0:T], rstd[:, 0, 0:T], 1.0 / D)

            def tensor(self, pe):
                if self.h_ready:
                    self.sums(pe)

            def sums(self, pe):
                for k in range(KT):
                    pe.wait_ge(self.squared.sem, self.squared.at(k + 1))
                    if self.l == 0 and self.j == 0 and k == 0:
                        pe.wait_ge(ones_set.sem, ones_set.at(1))
                    pe.matmul(ps[:, 7, 0:self.T], ones[:, :], sq[:, k % 2, 0:self.T], start=k == 0, stop=k == KT - 1)\
                        .then_inc(self.summed.sem, 1)

            def vector(self, dve):
                dve.wait_ge(mod_added.sem, (self.shift + 2 * KT) // MOD_GROUP)
                for s in range(2):
                    d = dve.scalar_tensor_tensor(out=pre[:, 3 * self.l + self.j, :, s], in0=mod[:, self.shift + KT:self.shift + 2 * KT, s], scalar=1.0,
                                                 in1=gain_of[self.l][:, 2 * self.j], op0=ALU.add, op1=ALU.mult)
                d.then_inc(self.derived.sem, 1)
                dve.wait_ge(self.derived.sem, self.derived.at(1))
                dve.wait_ge(self.rstd_steps.sem, self.rstd_steps.at(2))

                def scale(k):
                    if past(k - 1):
                        dve.wait_ge(self.ready.sem, self.ready.at(k - 1))
                    for s, a, b in segments(self.T):
                        i = dve.scalar_tensor_tensor(out=tmp[:, k % 2, a:b], in0=h[:, k, a:b], scalar=pre[:, 3 * self.l + self.j, k, s:s + 1],
                                                     in1=rstd[:, 0, a:b], op0=ALU.mult, op1=ALU.mult)
                    i.then_inc(self.scaled.sem, 1)
                scale(0)
                for k in range(KT):
                    if k + 1 < KT:
                        scale(k + 1)
                    dve.wait_ge(self.high.sem, self.high.at(k + 1))
                    for s, a, b in segments(self.T):
                        i = dve.scalar_tensor_tensor(out=u_low[:, k, a:b], in0=tmp[:, k % 2, a:b],
                                                     scalar=mod[:, self.shift + k, s:s + 1],
                                                     in1=u_high[:, k, a:b], op0=ALU.add, op1=ALU.subtract)
                    i.then_inc(self.ready.sem, 1)

        def load_ln_exp(act):
            act.add_instruction(mybir.InstLoadActFuncSet(name=nc.get_next_instruction_name(), engine=mybir.EngineType.Activation,
                                                         act_func_set_id=LN_EXP_SET))

        def make_rstd(act, source, count, steps, total, into, scale, step=0):
            load_ln_exp(act)
            act.wait_ge(source.sem, source.at(count))
            act.activation(into, total, ACT.Ln, scale=scale, bias=eps[:, 0:1]).then_inc(steps.sem, 1)
            act.wait_ge(steps.sem, steps.at(step + 1))
            act.activation(into, into, ACT.Exp, scale=-0.5).then_inc(steps.sem, 1)

        class Hidden(Stage):
            def __init__(self, layer, j, T, norm):
                self.n0, self.T, self.norm = STARTS[layer, f"up{j}"], T, norm
                self.mod0 = MOD_START[f"up{j}"] if beside(layer) else None
                self.units = UP_BESIDE if beside(layer) else UP_ALONE
                self.silu = signals.new("silu_ready", FT)
                self.steps = signals.new("hidden_steps", 2 * FT)
                self.ready = signals.new("hidden_ready", FT)

            def tensor(self, pe):
                def two_tiles(i):
                    for e, unit in enumerate(self.units):
                        n0 = self.n0 + e
                        n = n0 + len(self.units) * i
                        if unit is None:
                            mod_unit(pe, n, n0, self.mod0 + i, self.units[:e].count(None))
                            continue
                        f, g = unit
                        if g == 0 and past(2 * i + f - 1):
                            pe.wait_ge(self.ready.sem, self.ready.at(2 * i + f - 1))
                        first = isinstance(i, int) and e == 0
                        product(pe, n, n0, [(ps[:, 2 * f + g, 0:self.T], [(k, k) for k in range(KT)])],
                                lambda k: u_high[:, k, 0:self.T], lambda k: u_low[:, k, 0:self.T],
                                before=(lambda k: pe.wait_ge(self.norm.ready.sem, self.norm.ready.at(k + 1))) if first else None)
                        if self.mod0 and unit == PICK_AFTER:
                            mod_turn(pe, self.mod0 + i)
                repeat(pe, FT // 2, two_tiles)

            def scalar(self, act):
                def two_tiles(i):
                    for e, unit in enumerate(self.units):
                        n0 = self.n0 + e
                        n = n0 + len(self.units) * i
                        split_next(act, split_high, n, n0)
                        if unit is None:
                            if e + 1 == len(self.units) or self.units[e + 1] is not None:
                                if self.units[:e + 1].count(None) == MOD_GROUP:
                                    mod_copy(act, n, self.mod0 + i)
                        elif unit[1] == 0:
                            f = unit[0]
                            if past(2 * i + f - 1):
                                act.wait_ge(self.ready.sem, self.ready.at(2 * i + f - 1))
                            act.wait_ge(used.sem, n + 1)
                            act.activation(silu_g[:, f, 0:self.T], ps[:, 2 * f, 0:self.T], ACT.Silu).then_inc(self.silu.sem, 1)
                repeat(act, FT // 2, two_tiles)

            def vector(self, dve):
                T = self.T

                def two_tiles(i):
                    for e, unit in enumerate(self.units):
                        n0 = self.n0 + e
                        n = n0 + len(self.units) * i
                        split_next(dve, split_low, n, n0)
                        if unit is None or unit[1] == 0:
                            continue
                        f = unit[0]
                        t = 2 * i + f
                        dve.wait_ge(used.sem, n + 1)
                        dve.wait_ge(self.silu.sem, self.silu.at(t + 1))
                        if past(t - 1):
                            dve.wait_ge(self.ready.sem, self.ready.at(t - 1))
                        dve.tensor_tensor(hid[:, f, 0:T], silu_g[:, f, 0:T], ps[:, 2 * f + 1, 0:T], ALU.mult).then_inc(self.steps.sem, 1)
                        dve.wait_ge(self.steps.sem, self.steps.at(2 * t + 1))
                        dst_h = hid_high[:, bass.ds(t, 1), 0:T].rearrange("p a t -> p (a t)")
                        dst_l = hid_low[:, bass.ds(t, 1), 0:T].rearrange("p a t -> p (a t)")
                        dve.tensor_copy(dst_h, hid[:, f, 0:T]).then_inc(self.steps.sem, 1)
                        dve.wait_ge(self.steps.sem, self.steps.at(2 * t + 2))
                        dve.tensor_tensor(dst_l, hid[:, f, 0:T], dst_h, ALU.subtract).then_inc(self.ready.sem, 1)
                    if self.mod0:
                        mod_add(dve, self.mod0 + i)
                repeat(dve, FT // 2, two_tiles)

        class Result(Stage):
            def result_signals(self):
                self.copied = signals.new("y_squared", KT)
                self.added = signals.new("square_added", KT)

            def take(self, act, m, b):
                T = self.T
                act.activation(y[:, bass.ds(m, 1), 0:T].rearrange("p a t -> p (a t)"), ps[:, b, 0:T], ACT.Copy)
                if past(m - 1):
                    act.wait_ge(self.added.sem, self.added.at(m - 1))
                act.activation(sq[:, b, 0:T], ps[:, b, 0:T], ACT.Square).then_inc(self.copied.sem, 1)

            def add(self, dve, m, b):
                T = self.T
                dve.wait_ge(self.copied.sem, self.copied.at(m + 1))
                if isinstance(m, int) and m == 0:
                    dve.tensor_copy(ssq[:, 0:T], sq[:, b, 0:T]).then_inc(self.added.sem, 1)
                else:
                    if past(m):
                        dve.wait_ge(self.added.sem, self.added.at(m))
                    dve.tensor_tensor(ssq[:, 0:T], ssq[:, 0:T], sq[:, b, 0:T], ALU.add).then_inc(self.added.sem, 1)

        class Down(Result):
            def __init__(self, layer, j, T, hidden):
                self.n0, self.T, self.hidden = STARTS[layer, f"down{j}"], T, hidden
                self.mod0 = MOD_START[f"down{j}"] if beside(layer) else None
                self.units = DOWN_BESIDE if beside(layer) else DOWN_ALONE
                self.last = self.n0 + KT // 2 * len(self.units) == N_UNITS
                self.result_signals()

            def width(self, e):
                return DOWN_WIDTH // P if e < len(self.units) and narrow(self.units[e]) else 8

            def splits(self, eng, f, n, n0, e, last):
                if not (last and e >= len(self.units) - AHEAD):
                    f(eng, n + AHEAD, n0 + AHEAD, self.width(e + AHEAD))

            def rows(self, eng, body):
                body(0, False)
                with eng.Fori(1, KT // 2 - self.last) as i:
                    body(i, False)
                if self.last:
                    body(KT // 2 - 1, True)

            def tensor(self, pe):
                pe.wait_ge(self.hidden.ready.sem, self.hidden.ready.at(FT))

                def two_rows(i, last):
                    for e, unit in enumerate(self.units):
                        n0 = self.n0 + e
                        n = n0 + len(self.units) * i
                        if unit is None:
                            mod_unit(pe, n, n0, self.mod0 + i, self.units[:e].count(None))
                            continue
                        r, part = unit
                        if part == 0 and past(2 * i + r - 1):
                            pe.wait_ge(self.copied.sem, self.copied.at(2 * i + r - 1))
                        k0 = sum(DOWN_K[:part])
                        product(pe, n, n0, [(ps[:, r, 0:self.T], [(w, k0 + w) for w in range(DOWN_K[part])])],
                                lambda k: hid_high[:, k, 0:self.T], lambda k: hid_low[:, k, 0:self.T],
                                first=part == 0, last=part == 3)
                        if self.mod0 and unit == PICK_AFTER:
                            mod_turn(pe, self.mod0 + i)
                self.rows(pe, two_rows)

            def scalar(self, act):
                def two_rows(i, last):
                    for e, unit in enumerate(self.units):
                        n0 = self.n0 + e
                        n = n0 + len(self.units) * i
                        self.splits(act, split_high, n, n0, e, last)
                        if unit is None and self.units[:e + 1].count(None) == MOD_GROUP:
                            mod_copy(act, n, self.mod0 + i)
                        elif unit and unit[1] == 3:
                            act.wait_ge(used.sem, n + 1)
                            self.take(act, 2 * i + unit[0], unit[0])
                self.rows(act, two_rows)

            def vector(self, dve):
                def two_rows(i, last):
                    for e, unit in enumerate(self.units):
                        n0 = self.n0 + e
                        n = n0 + len(self.units) * i
                        self.splits(dve, split_low, n, n0, e, last)
                        if unit and unit[1] == 3:
                            self.add(dve, 2 * i + unit[0], unit[0])
                    if self.mod0:
                        mod_add(dve, self.mod0 + i)
                self.rows(dve, two_rows)

        class Residual(Stage):
            def __init__(self, layer, j, T, result):
                self.l, self.j, self.T, self.result = layer, j, T, result
                self.derived = signals.new("post_derived", 1)
                self.summed = signals.new("y_summed", 1)
                self.rstd_steps = signals.new("y_rstd", 2)
                self.scaled = signals.new("y_scaled", KT)
                self.h_ready = signals.new("h_ready", KT)

            def tensor(self, pe):
                pe.wait_ge(self.result.added.sem, self.result.added.at(KT))
                pe.matmul(ps[:, 7, 0:self.T], ones[:, :], ssq[:, 0:self.T], start=True, stop=True).then_inc(self.summed.sem, 1)

            def scalar(self, act):
                make_rstd(act, self.summed, 1, self.rstd_steps, ps[:, 7, 0:self.T], rstd[:, 0, 0:self.T], 1.0 / D)

            def vector(self, dve):
                g = self.l * MODT + (3 * self.j + 2) * KT
                dve.wait_ge(mod_added.sem, (g + KT) // MOD_GROUP)
                for s in range(2):
                    d = dve.scalar_tensor_tensor(out=post[:, 3 * self.l + self.j, :, s], in0=mod[:, g:g + KT, s],
                                                 scalar=1.0 if self.j == 1 else 0.5, in1=gain_of[self.l][:, 2 * self.j + 1],
                                                 op0=ALU.mult, op1=ALU.mult)
                d.then_inc(self.derived.sem, 1)
                dve.wait_ge(self.derived.sem, self.derived.at(1))
                dve.wait_ge(self.rstd_steps.sem, self.rstd_steps.at(2))

                def scale(k):
                    if past(k - 1):
                        dve.wait_ge(self.h_ready.sem, self.h_ready.at(k - 1))
                    for s, a, b in segments(self.T):
                        i = dve.scalar_tensor_tensor(out=tmp[:, k % 2, a:b], in0=y[:, k, a:b], scalar=post[:, 3 * self.l + self.j, k, s:s + 1],
                                                     in1=rstd[:, 0, a:b], op0=ALU.mult, op1=ALU.mult)
                    i.then_inc(self.scaled.sem, 1)
                scale(0)
                if self.j == 1:
                    dve.wait_ge(h_back.sem, 16 * (self.l + 1))
                for k in range(KT):
                    if k + 1 < KT:
                        scale(k + 1)
                    dve.wait_ge(self.scaled.sem, self.scaled.at(k + 1))
                    dve.tensor_tensor(h[:, k, 0:self.T], h[:, k, 0:self.T], tmp[:, k % 2, 0:self.T], ALU.add).then_inc(self.h_ready.sem, 1)

        class Branch(Stage):

            def __init__(self, layer, index, T, norm, before):
                self.l, self.index, self.b, self.T, self.norm, self.before = layer, index, BRANCHES[index], T, norm, before
                b = self.b
                self.nk = N_K[b]
                self.tiles = BT + 2 * self.nk
                self.roped, self.normed = b != "B", b == "C"
                self.prep = [(BT + i, S_ALL, k_high[:, i], k_low[:, i]) for i in range(self.nk)]
                self.prep += [(i, T, q_high[:, i], q_low[:, i]) for i in range(BT)]
                n = len(self.prep)
                self.steps = []
                for t in range(BT):
                    self.steps += [(t, q, 0, S_ALL) for q in (0, P)]
                    if T > S_X:
                        self.steps += [(t, q, S_X, S_C) for q in (S_X, S_X + P)]
                J = self.J = len(self.steps)
                follows = BRANCHES[index + 1] if index + 1 < len(BRANCHES) else None
                self.window = [("gate", m, T) for m in range(KT)]
                if follows:
                    self.window += [("proj", t, T if t < BT else S_ALL) for t in range(BT + 2 * N_K[follows])]
                self.n_window = STARTS[layer, b + "window"]
                self.n_mix = STARTS[layer, b + "mix"]
                self.ahead = AHEAD_OF[T > S_X][index]
                self.behind = BEHIND_OF[index]
                weights = [2]
                for _, _, key, _ in self.steps:
                    weights += [3, 3] if key == 0 else [2, 2]
                parts = [(w, part) for w in range(self.ahead, len(self.window) - self.behind) for part in ("high", "low")]
                self.points, total, done, upto = [], sum(weights), 0, 0
                for weight in weights:
                    upto += weight
                    end = len(parts) * upto // total
                    self.points.append(parts[done:end])
                    done = end
                self.points.append([(w, part) for w in range(len(self.window) - self.behind, len(self.window)) for part in ("high", "low")])

                if not before:
                    self.projected = signals.new("projected", self.tiles)
                    self.staged, self.staged_at = self.projected, self.tiles
                else:
                    self.staged, self.staged_at = before.taken, len(before.window)
                self.taken = signals.new("product_taken", len(self.window))
                self.v_turned = signals.new("v_turned", 4)
                self.v_high = signals.new("v_high_made", 4)
                self.v_low = signals.new("v_low_made", 4)
                self.head_squared = signals.new("head_squared", n if self.normed else 0)
                self.head_summed = signals.new("head_summed", n if self.normed else 0)
                self.head_rstd = signals.new("head_rstd", 2 * n if self.normed else 0)
                self.head_normed = signals.new("head_normed", n if self.normed else 0)
                self.shuffled = signals.new("rope_shuffled", n if self.roped else 0)
                self.sined = signals.new("rope_sine", n if self.roped else 0)
                self.cosined = signals.new("rope_cosine", n if self.roped else 0)
                self.turned = signals.new("rope_added", n if self.roped else 0)
                self.part_high = signals.new("qk_high_made", n)
                self.part_low = signals.new("qk_low_made", n)
                self.scored = signals.new("scores_ready", J)
                self.maxed = signals.new("row_max", J)
                self.shifted = signals.new("shift_ready", J)
                self.sunk = signals.new("sink_shifted", J if b == "D" else 0)
                self.expd = signals.new("exp_ready", J)
                self.sums = signals.new("sum_steps", 3 * J)
                self.probs = signals.new("probs_ready", J)
                self.flipped = signals.new("probs_turned", J)
                self.pt_high = signals.new("probs_high_made", J)
                self.pt_low = signals.new("probs_low_made", J)
                self.mixed = signals.new("values_mixed", J)
                self.o_high = signals.new("branch_high_made", J)
                self.o_low = signals.new("branch_low_made", J if b != "A" else 0)
                sub = BT if b == "A" else 0
                self.sub_squared = signals.new("sub_squared", sub)
                self.sub_summed = signals.new("sub_summed", sub)
                self.sub_rstd = signals.new("sub_rstd", 2 * sub)
                self.sub_scaled = signals.new("sub_scaled", sub)
                self.sub_high = signals.new("sub_high_made", sub)
                self.sub_low = signals.new("sub_low_made", sub)
                self.o_done = self.o_high if b == "A" else self.o_low
                self.y_ready, self.y_count = (self.sub_low, BT) if b == "A" else (self.o_low, J)
                self.gated = signals.new("branch_gated", KT if index else 0)
                self.merged = signals.new("branch_merged", KT)
                if b in "BD":
                    self.masked = signals.new("scores_biased" if b == "B" else "scores_masked", 8)

            def carriers(self):
                keys, queries = list(range(self.nk)), list(range(self.nk, len(self.prep)))
                out, rotated = [], keys + queries if self.roped else []
                if self.before:
                    for c in range(BT):
                        turn = [i for i in rotated if min(i, BT - 1) == c] if self.b == "D" else []
                        out.append(("mix", c, turn, [] if self.normed else [i for i in keys if i + BT - self.nk == c]))
                    if not self.normed:
                        keys = []
                    if self.b == "D":
                        rotated = []
                items = keys + queries
                n = self.ahead - (self.b == "C")
                for g in range(self.ahead):
                    turn = rotated[4 * g:4 * g + 4]
                    h = g - (self.b == "C")
                    out.append(("gate", g, turn, items[len(items) * h // n:len(items) * (h + 1) // n] if h >= 0 else []))
                return out

            def head_items(self, c):
                return [i for i in range(len(self.prep)) if self.normed and i // 2 == c]

            def first_projections(self, pe):
                W = [self.T] * BT + [S_ALL] * 2 * self.nk
                n1 = STARTS[self.l, "Aproj"]

                def four(i, base):
                    for c in range(4):
                        n = n1 + base + c
                        if past(4 * i + base + c - 1):
                            pe.wait_ge(self.projected.sem, self.projected.at(4 * i + base + c - 1))
                        w = W[base + c]
                        product(pe, n + 4 * i, n, [(ps[:, 6 + c % 2, 0:w], [(k, k) for k in range(KT)])],
                                lambda k: u_high[:, k, 0:w], lambda k: u_low[:, k, 0:w],
                                before=(lambda k: pe.wait_ge(self.norm.ready.sem, self.norm.ready.at(k + 1))) if base + c == 0 else None)
                four(0, 0)
                repeat(pe, 2, lambda i: four(i, BT))

            def window_part(self, pe, w, part):
                kind, t, W = self.window[w]
                n = self.n_window + w
                outs = [(ps[:, 6 + w % 2, 0:W], [(k, k) for k in range(KT)])]
                if part == "low":
                    product_low(pe, n, n, outs, lambda k: u_high[:, k, 0:W])
                    return
                if w >= 2:
                    pe.wait_ge(self.taken.sem, self.taken.at(w - 1))
                elif self.before:
                    pe.wait_ge(self.before.merged.sem, self.before.merged.at(6))
                else:
                    pe.wait_ge(self.projected.sem, self.projected.at(self.tiles))
                product_high(pe, n, n, outs, lambda k: u_high[:, k, 0:W], lambda k: u_low[:, k, 0:W])

            def window_parts(self, pe, point):
                for w, part in self.points[point]:
                    self.window_part(pe, w, part)

            def mix_unit(self, pe, c):
                if c == 0:
                    pe.wait_ge(self.taken.sem, self.taken.at(len(self.window)))
                if c >= 2:
                    pe.wait_ge(self.merged.sem, self.merged.at(2 * c - 2))
                T, n, b0 = self.T, self.n_mix + c, 6 - 2 * (c % 2)
                product(pe, n, n, [(ps[:, b0 + r, 0:T], [(4 * r + k, k) for k in range(BT)]) for r in range(2)],
                        lambda k: q_high[:, k, 0:T], lambda k: q_low[:, k, 0:T])

            def tensor(self, pe):
                b, T, J = self.b, self.T, self.J
                if not self.before:
                    self.first_projections(pe)
                else:
                    pe.wait_ge(self.before.y_ready.sem, self.before.y_ready.at(self.before.y_count))
                pe.wait_ge(self.staged.sem, self.staged.at(self.staged_at))
                for tt in range(4):
                    for c in range(self.nk):
                        v = pe.transpose(ps[:, tt, c * P:(c + 1) * P], proj[:, BT + self.nk + c, tt * P:(tt + 1) * P], ident)
                    v.then_inc(self.v_turned.sem, 1)
                for kind, c, _, _ in self.carriers():
                    if kind == "gate":
                        self.window_part(pe, c, "high")
                        self.window_part(pe, c, "low")
                        continue
                    self.before.mix_unit(pe, c)
                    for i in self.head_items(c):
                        pe.wait_ge(self.head_squared.sem, self.head_squared.at(i + 1))
                        if i < 4:
                            pe.wait_ge(self.v_low.sem, self.v_low.at(i + 1))
                        else:
                            pe.wait_ge(self.head_rstd.sem, self.head_rstd.at(i - 3))
                        W = self.prep[i][1]
                        pe.matmul(ps[:, i % 4, 0:W], pairs, sq[:, i % 2, 0:W], start=True, stop=True).then_inc(self.head_summed.sem, 1)
                pe.wait_ge(self.part_low.sem, self.part_low.at(len(self.prep)))
                pe.wait_ge(self.v_low.sem, self.v_low.at(4))
                if self.before:
                    pe.wait_ge(self.before.merged.sem, self.before.merged.at(KT))

                def scores(j):
                    t, q, key, nkeys = self.steps[j]
                    kt = t if self.nk == BT else 0
                    if past(j):
                        pe.wait_ge(self.expd.sem, self.expd.at(j))
                    for s in range(2):
                        rows = slice(s * HD, (s + 1) * HD)
                        for a, (qq, kk) in enumerate(((q_high, k_high), (q_high, k_low), (q_low, k_high))):
                            m = pe.matmul(ps[:, s, 0:nkeys], qq[rows, t, q:q + P], kk[rows, kt, key:key + nkeys], start=a == 0, stop=a == 2)
                    m.then_inc(self.scored.sem, 1)

                def flip(j):
                    nkeys = self.steps[j][3]
                    pe.wait_ge(self.probs.sem, self.probs.at(j + 1))
                    if past(j):
                        pe.wait_ge(self.pt_low.sem, self.pt_low.at(j))
                    for s in range(1 if b == "A" else 2):
                        for c in range(nkeys // P):
                            m = pe.transpose(ps[:, 2 + s, c * P:(c + 1) * P], prob[:, j % 2, s, c * P:(c + 1) * P], ident)
                    m.then_inc(self.flipped.sem, 1)

                def mix(j):
                    t, q, key, nkeys = self.steps[j]
                    vt = t if self.nk == BT else 0
                    pe.wait_ge(self.pt_low.sem, self.pt_low.at(j + 1))
                    if past(j - 1):
                        pe.wait_ge(self.o_done.sem, self.o_done.at(j - 1))
                    for s in range(1 if b == "A" else 2):
                        terms = [(c, vv, pp) for c in range(nkeys // P)
                                 for vv, pp in ((v_high, pt_high), (v_high, pt_low), (v_low, pt_high))]
                        for a, (c, vv, pp) in enumerate(terms):
                            m = pe.matmul(ps[:, 4 + j % 2, s * P:(s + 1) * P], vv[:, key // P + c, vt * P:(vt + 1) * P],
                                          pp[:, s, c * P:(c + 1) * P], start=a == 0, stop=a == len(terms) - 1)
                    m.then_inc(self.mixed.sem, 1)
                scores(0)
                self.window_parts(pe, 0)
                for j in range(J):
                    if j + 1 < J:
                        scores(j + 1)
                    self.window_parts(pe, 1 + 2 * j)
                    flip(j)
                    if j:
                        mix(j - 1)
                    self.window_parts(pe, 2 + 2 * j)
                mix(J - 1)
                self.window_parts(pe, 2 * J + 1)
                if b == "A":
                    for t in range(BT):
                        pe.wait_ge(self.sub_squared.sem, self.sub_squared.at(t + 1))
                        pe.matmul(ps[:, t, 0:T], ones[:, :], sq[:, t % 2, 0:T], start=True, stop=True).then_inc(self.sub_summed.sem, 1)

            def window_splits(self, eng, f, point):
                for w, part in self.points[point]:
                    if part == "high":
                        split_next(eng, f, self.n_window + w, self.n_window + w)

            def window_results(self, act, point):
                for w, part in self.points[point]:
                    if part == "high":
                        split_next(act, split_high, self.n_window + w, self.n_window + w)
                    else:
                        self.window_taken(act, w)

            def window_taken(self, act, w):
                kind, t, W = self.window[w]
                n = self.n_window + w
                act.wait_ge(used.sem, n + 1)
                if kind == "gate":
                    i = act.activation(gate[:, t, 0:W], ps[:, 6 + w % 2, 0:W], ACT.Tanh, scale=0.5)
                else:
                    i = act.activation(proj[:, t, 0:W], ps[:, 6 + w % 2, 0:W], ACT.Copy)
                i.then_inc(self.taken.sem, 1)

            def heads_rstd(self, act):
                n = len(self.prep)
                load_ln_exp(act)
                for i in range(n):
                    act.wait_ge(self.head_summed.sem, self.head_summed.at(i + 1))
                    W = self.prep[i][1]
                    act.activation(self.rstd_of(i)[:, 0:W], ps[:, i % 4, 0:W], ACT.Ln, scale=1.0 / HD, bias=eps[:, 0:1]).then_inc(self.head_rstd.sem, 1)
                for i in range(n):
                    act.wait_ge(self.head_rstd.sem, self.head_rstd.at(i + 1))
                    r = self.rstd_of(i)[:, 0:self.prep[i][1]]
                    act.activation(r, r, ACT.Exp, scale=-0.5).then_inc(self.head_rstd.sem, 1)

            def rstd_of(self, i):
                return head_rstd[:, i] if i < 4 else rstd[:, 0]

            def head_square(self, act, i):
                slot, W, _, _ = self.prep[i]
                if past(i - 1):
                    act.wait_ge(self.head_summed.sem, self.head_summed.at(i - 1))
                act.activation(sq[:, i % 2, 0:W], proj[:, slot, 0:W], ACT.Square).then_inc(self.head_squared.sem, 1)

            def high_of_qk(self, act, i):
                slot, W, hi, lo = self.prep[i]
                if self.roped:
                    act.wait_ge(self.turned.sem, self.turned.at(i + 1))
                act.activation(hi[:, 0:W], proj[:, slot, 0:W], ACT.Copy).then_inc(self.part_high.sem, 1)

            def scalar(self, act):
                b, T, J = self.b, self.T, self.J
                if not self.before:
                    n1 = STARTS[self.l, "Aproj"]
                    W = [T] * BT + [S_ALL] * 2 * self.nk
                    act.wait_ge(h_saved.sem, h_saved.at(16 * (self.l + 1)))

                    def four(i, base):
                        for c in range(4):
                            n = n1 + base + c
                            split_next(act, split_high, n + 4 * i, n)
                            act.wait_ge(used.sem, n + 4 * i + 1)
                            slot = 4 * i + base + c
                            w = W[base + c]
                            act.activation(proj[:, bass.ds(slot, 1), 0:w].rearrange("p a t -> p (a t)"), ps[:, 6 + c % 2, 0:w], ACT.Copy)\
                                .then_inc(self.projected.sem, 1)
                    four(0, 0)
                    repeat(act, 2, lambda i: four(i, BT))
                act.wait_ge(self.staged.sem, self.staged.at(self.staged_at))
                for tt in range(4):
                    act.wait_ge(self.v_turned.sem, self.v_turned.at(tt + 1))
                    act.activation(v_high[:, tt, 0:self.nk * P], ps[:, tt, 0:self.nk * P], ACT.Copy).then_inc(self.v_high.sem, 1)
                for i in self.head_items(0):
                    self.head_square(act, i)
                for kind, c, _, items in self.carriers():
                    if kind == "mix":
                        n = self.before.n_mix + c
                        split_next(act, split_high, n, n)
                        for i in self.head_items(c + 1):
                            self.head_square(act, i)
                        if self.normed and c == 2:
                            self.heads_rstd(act)
                    else:
                        split_next(act, split_high, self.n_window + c, self.n_window + c)
                        if c == 0 and self.before:
                            act.wait_ge(self.before.merged.sem, self.before.merged.at(KT))
                        self.window_taken(act, c)
                    for i in items:
                        self.high_of_qk(act, i)

                def exps(j):
                    nkeys = self.steps[j][3]
                    act.wait_ge(self.shifted.sem, self.shifted.at(j + 1))
                    if past(j - 1):
                        act.wait_ge(self.flipped.sem, self.flipped.at(j - 1))
                    if b == "D":
                        act.wait_ge(self.sunk.sem, self.sunk.at(j + 1))
                        act.activation(stat[:, j % 2, 4], stat[:, j % 2, 3], ACT.Exp)
                    for s in range(2):
                        e = act.activation(prob[:, j % 2, s, 0:nkeys], ps[:, s, 0:nkeys], ACT.Exp,
                                           bias=stat[:, j % 2, 1, s:s + 1], scale=SCALE, accum_out=stat[:, j % 2, 2, s:s + 1])
                    e.then_inc(self.expd.sem, 1)

                def high_of_probs(j):
                    nkeys, ns = self.steps[j][3], 1 if b == "A" else 2
                    act.wait_ge(self.flipped.sem, self.flipped.at(j + 1))
                    if past(j):
                        act.wait_ge(self.mixed.sem, self.mixed.at(j))
                    act.activation(pt_high[:, 0:ns, 0:nkeys], ps[:, 2:2 + ns, 0:nkeys], ACT.Copy).then_inc(self.pt_high.sem, 1)

                def high_of_out(j):
                    t, q, _, _ = self.steps[j]
                    act.wait_ge(self.mixed.sem, self.mixed.at(j + 1))
                    if b == "A":
                        o = act.activation(o_a[:, t, q:q + P], ps[:, 4 + j % 2, 0:P], ACT.Copy)
                    else:
                        for s in range(2):
                            rows = slice(s * HD, (s + 1) * HD)
                            o = act.activation(q_high[rows, t, q:q + P], ps[rows, 4 + j % 2, s * P:(s + 1) * P], ACT.Copy)
                    o.then_inc(self.o_high.sem, 1)
                exps(0)
                self.window_results(act, 0)
                for j in range(J):
                    if j + 1 < J:
                        exps(j + 1)
                    self.window_results(act, 1 + 2 * j)
                    high_of_probs(j)
                    if j:
                        high_of_out(j - 1)
                    self.window_results(act, 2 + 2 * j)
                high_of_out(J - 1)
                self.window_results(act, 2 * J + 1)
                if b == "A":
                    act.wait_ge(self.o_high.sem, self.o_high.at(J))
                    for t in range(BT):
                        if past(t - 1):
                            act.wait_ge(self.sub_summed.sem, self.sub_summed.at(t - 1))
                        act.activation(sq[:, t % 2, 0:T], o_a[:, t, 0:T], ACT.Square).then_inc(self.sub_squared.sem, 1)
                    for t in range(BT):
                        act.wait_ge(self.sub_summed.sem, self.sub_summed.at(t + 1))
                        act.activation(head_rstd[:, t, 0:T], ps[:, t, 0:T], ACT.Ln, scale=1.0 / P, bias=eps[:, 0:1]).then_inc(self.sub_rstd.sem, 1)
                    for t in range(BT):
                        act.wait_ge(self.sub_rstd.sem, self.sub_rstd.at(t + 1))
                        act.activation(head_rstd[:, t, 0:T], head_rstd[:, t, 0:T], ACT.Exp, scale=-0.5).then_inc(self.sub_rstd.sem, 1)
                    act.wait_ge(self.sub_scaled.sem, self.sub_scaled.at(BT))
                    for t in range(BT):
                        act.activation(q_high[:, t, 0:T], prob[:, t // 2, t % 2, 0:T], ACT.Copy).then_inc(self.sub_high.sem, 1)

            def ropes(self, dve, items):
                def buffer(i):
                    return sq[:, i % 4 // 2, i % 2 * S_X:(i % 2 + 1) * S_X]
                for i in items:
                    if past(i - 3):
                        dve.wait_ge(self.turned.sem, self.turned.at(i - 3))
                    dve.stream_shuffle(buffer(i), proj[:, self.prep[i][0], 0:S_X], [(p + 16) % 32 for p in range(32)])\
                        .then_inc(self.shuffled.sem, 1)
                for i in items:
                    dve.wait_ge(self.shuffled.sem, self.shuffled.at(i + 1))
                    dve.tensor_tensor(buffer(i), buffer(i), sm("sin"), ALU.mult).then_inc(self.sined.sem, 1)
                for i in items:
                    x = proj[:, self.prep[i][0], 0:S_X]
                    dve.wait_ge(self.cosined.sem, self.cosined.at(i + 1))
                    dve.wait_ge(self.sined.sem, self.sined.at(i + 1))
                    dve.tensor_tensor(x, x, buffer(i), ALU.add).then_inc(self.turned.sem, 1)

            def low_of_qk(self, dve, i):
                slot, W, hi, lo = self.prep[i]
                dve.wait_ge(self.part_high.sem, self.part_high.at(i + 1))
                dve.tensor_tensor(lo[:, 0:W], proj[:, slot, 0:W], hi[:, 0:W], ALU.subtract).then_inc(self.part_low.sem, 1)

            def head_scale(self, dve, i):
                slot, W, _, _ = self.prep[i]
                dve.wait_ge(self.head_rstd.sem, self.head_rstd.at(len(self.prep) + i + 1))
                g = smv("qk_gain", self.l, DEPTH)[:, (1 if slot >= BT else 0):(2 if slot >= BT else 1)]
                dve.scalar_tensor_tensor(out=proj[:, slot, 0:W], in0=proj[:, slot, 0:W], scalar=g, in1=self.rstd_of(i)[:, 0:W],
                                         op0=ALU.mult, op1=ALU.mult).then_inc(self.head_normed.sem, 1)

            def merge(self, dve, c):
                b0, T = 6 - 2 * (c % 2), self.T
                dve.wait_ge(used.sem, self.n_mix + c + 1)
                for r in range(2):
                    m = 2 * c + r
                    z = ps[:, b0 + r, 0:T]
                    if self.index == 0:
                        dve.scalar_tensor_tensor(out=acc[:, m, 0:T], in0=gate[:, m, 0:T], scalar=1.0, in1=z,
                                                 op0=ALU.add, op1=ALU.mult).then_inc(self.merged.sem, 1)
                    else:
                        if past(m - 1):
                            dve.wait_ge(self.merged.sem, self.merged.at(m - 1))
                        dve.scalar_tensor_tensor(out=tmp[:, m % 2, 0:T], in0=gate[:, m, 0:T], scalar=1.0, in1=z,
                                                 op0=ALU.add, op1=ALU.mult).then_inc(self.gated.sem, 1)
                        dve.wait_ge(self.gated.sem, self.gated.at(m + 1))
                        dve.tensor_tensor(acc[:, m, 0:T], acc[:, m, 0:T], tmp[:, m % 2, 0:T], ALU.add).then_inc(self.merged.sem, 1)

            def vector(self, dve):
                b, T, J = self.b, self.T, self.J
                if not self.before:
                    n1 = STARTS[self.l, "Aproj"]

                    def four(i):
                        for c in range(4):
                            split_next(dve, split_low, n1 + c + 4 * i, n1 + c)
                    repeat(dve, 3, four)
                dve.wait_ge(self.staged.sem, self.staged.at(self.staged_at))
                for tt in range(4):
                    dve.wait_ge(self.v_high.sem, self.v_high.at(tt + 1))
                    w = self.nk * P
                    dve.tensor_tensor(v_low[:, tt, 0:w], ps[:, tt, 0:w], v_high[:, tt, 0:w], ALU.subtract).then_inc(self.v_low.sem, 1)
                for kind, c, turn, items in self.carriers():
                    if kind == "mix":
                        n = self.before.n_mix + c
                        split_next(dve, split_low, n, n)
                        self.before.merge(dve, c)
                        if self.normed and c == BT - 1:
                            for i in range(len(self.prep)):
                                self.head_scale(dve, i)
                    else:
                        n = self.n_window + c
                        split_next(dve, split_low, n, n)
                        if self.normed and c == 0:
                            dve.wait_ge(self.head_normed.sem, self.head_normed.at(len(self.prep)))
                    self.ropes(dve, turn)
                    for i in items:
                        self.low_of_qk(dve, i)

                def row_max(j):
                    t, q, key, nkeys = self.steps[j]
                    f = sum(step[2] == 0 for step in self.steps[:j])
                    both = ps[:, 0:2]
                    dve.wait_ge(self.scored.sem, self.scored.at(j + 1))
                    if b == "B" and key == 0:
                        n = self.l * 8 + f
                        dve.wait_ge(bias_landed[f % 2].sem, 16 * (n // 2 + 1))
                        dve.scalar_tensor_tensor(out=both[:, :, 0:S_X], in0=na_bias[:, f % 2], scalar=1.0 / SCALE,
                                                 in1=both[:, :, 0:S_X], op0=ALU.mult, op1=ALU.add).then_inc(self.masked.sem, 1)
                        dve.wait_ge(self.masked.sem, self.masked.at(f + 1))
                    if b == "D" and key == 0:
                        a = P - q
                        m = smv("mask", pattern="p (i s k) -> p i s k", i=2, s=2)[:, q // P]
                        dve.tensor_tensor(both[:, :, a:a + P], both[:, :, a:a + P], m, ALU.add).then_inc(self.masked.sem, 1)
                        dve.wait_ge(self.masked.sem, self.masked.at(f + 1))
                    if past(j - 1):
                        dve.wait_ge(self.probs.sem, self.probs.at(j - 1))
                    dve.tensor_reduce(stat[:, j % 2, 0], both[:, :, 0:nkeys], AX.X, ALU.max).then_inc(self.maxed.sem, 1)
                    dve.wait_ge(self.maxed.sem, self.maxed.at(j + 1))
                    if b == "D":
                        sink = smv("sink", self.l, DEPTH, "p (t s) -> p t s", s=2)[:, t]
                        dve.scalar_tensor_tensor(out=stat[:, j % 2, 5], in0=stat[:, j % 2, 0], scalar=SCALE, in1=sink,
                                                 op0=ALU.mult, op1=ALU.max).then_inc(self.sums.sem, 1)
                        dve.wait_ge(self.sums.sem, self.sums.at(3 * j + 1))
                        dve.tensor_tensor(stat[:, j % 2, 3], sink, stat[:, j % 2, 5], ALU.subtract).then_inc(self.sunk.sem, 1)
                        dve.tensor_scalar(stat[:, j % 2, 1], stat[:, j % 2, 5], -1.0, None, ALU.mult).then_inc(self.shifted.sem, 1)
                    else:
                        dve.tensor_scalar(stat[:, j % 2, 1], stat[:, j % 2, 0], -SCALE, None, ALU.mult).then_inc(self.shifted.sem, 1)

                def scale_probs(j):
                    nkeys = self.steps[j][3]
                    st = stat[:, j % 2]
                    total = st[:, 2]
                    dve.wait_ge(self.expd.sem, self.expd.at(j + 1))
                    if b == "D":
                        dve.tensor_tensor(st[:, 5], st[:, 2], st[:, 4], ALU.add).then_inc(self.sums.sem, 1)
                        dve.wait_ge(self.sums.sem, self.sums.at(3 * j + 2))
                        total = st[:, 5]
                    if b == "A":
                        dve.reciprocal(st[:, 3], total).then_inc(self.sums.sem, 1)
                        dve.wait_ge(self.sums.sem, self.sums.at(3 * j + 1))
                        dve.tensor_scalar(prob[:, j % 2, 0, 0:nkeys], prob[:, j % 2, 0, 0:nkeys], st[:, 3, 0:1], None, ALU.mult)
                        dve.tensor_scalar(st[:, 4, 1:2], st[:, 3, 1:2], lam[:, self.l, 5:6], None, ALU.mult).then_inc(self.sums.sem, 2)
                        dve.wait_ge(self.sums.sem, self.sums.at(3 * j + 3))
                        dve.scalar_tensor_tensor(out=prob[:, j % 2, 0, 0:nkeys], in0=prob[:, j % 2, 1, 0:nkeys], scalar=st[:, 4, 1:2],
                                                 in1=prob[:, j % 2, 0, 0:nkeys], op0=ALU.mult, op1=ALU.add).then_inc(self.probs.sem, 1)
                    else:
                        dve.reciprocal(st[:, 3], total).then_inc(self.sums.sem, 1 if b == "D" else 3)
                        dve.wait_ge(self.sums.sem, self.sums.at(3 * j + 3))
                        for s in range(2):
                            m = dve.tensor_scalar(prob[:, j % 2, s, 0:nkeys], prob[:, j % 2, s, 0:nkeys], st[:, 3, s:s + 1], None, ALU.mult)
                        m.then_inc(self.probs.sem, 1)

                def low_of_probs(j):
                    nkeys, ns = self.steps[j][3], 1 if b == "A" else 2
                    dve.wait_ge(self.pt_high.sem, self.pt_high.at(j + 1))
                    dve.tensor_tensor(pt_low[:, 0:ns, 0:nkeys], ps[:, 2:2 + ns, 0:nkeys], pt_high[:, 0:ns, 0:nkeys], ALU.subtract)\
                        .then_inc(self.pt_low.sem, 1)

                def low_of_out(j):
                    t, q, _, _ = self.steps[j]
                    dve.wait_ge(self.o_high.sem, self.o_high.at(j + 1))
                    for s in range(2):
                        rows = slice(s * HD, (s + 1) * HD)
                        o = dve.tensor_tensor(q_low[rows, t, q:q + P], ps[rows, 4 + j % 2, s * P:(s + 1) * P],
                                              q_high[rows, t, q:q + P], ALU.subtract)
                    o.then_inc(self.o_low.sem, 1)

                row_max(0)
                self.window_splits(dve, split_low, 0)
                scale_probs(0)
                for j in range(J):
                    if j + 1 < J:
                        row_max(j + 1)
                    self.window_splits(dve, split_low, 1 + 2 * j)
                    if j + 1 < J:
                        scale_probs(j + 1)
                    low_of_probs(j)
                    if j and b != "A":
                        low_of_out(j - 1)
                    self.window_splits(dve, split_low, 2 + 2 * j)
                if b != "A":
                    low_of_out(J - 1)
                self.window_splits(dve, split_low, 2 * J + 1)
                if b == "A":
                    for t in range(BT):
                        dve.wait_ge(self.sub_rstd.sem, self.sub_rstd.at(BT + t + 1))
                        dve.scalar_tensor_tensor(out=prob[:, t // 2, t % 2, 0:T], in0=o_a[:, t, 0:T], scalar=lam[:, self.l, 6:7],
                                                 in1=head_rstd[:, t, 0:T], op0=ALU.mult, op1=ALU.mult).then_inc(self.sub_scaled.sem, 1)
                    for t in range(BT):
                        dve.wait_ge(self.sub_high.sem, self.sub_high.at(t + 1))
                        dve.tensor_tensor(q_low[:, t, 0:T], prob[:, t // 2, t % 2, 0:T], q_high[:, t, 0:T], ALU.subtract).then_inc(self.sub_low.sem, 1)

            def pool(self, pool):
                if not self.before:
                    pool.wait_ge(self.norm.ready.sem, self.norm.ready.at(KT))
                    pool.dma_start(h_kept, h[:, :, :]).then_inc(h_saved.sem, 16)
                if self.roped:
                    for i, (slot, W, hi, lo) in enumerate(self.prep):
                        x = proj[:, slot, 0:S_X]
                        pool.wait_ge(self.shuffled.sem, self.shuffled.at(i + 1))
                        pool.tensor_tensor(x, x, sm("cos"), ALU.mult).then_inc(self.cosined.sem, 1)
                if self.b == "B":
                    pool.wait_ge(self.before.sub_low.sem, self.before.sub_low.at(BT))
                    for j in range(8):
                        if past(j - 1):
                            pool.wait_ge(self.masked.sem, self.masked.at(j - 1))
                        pool.dma_start(na_bias[:, j % 2], na_rows[self.l, j]).then_inc(bias_landed[j % 2].sem, 16)
                if self.index == 3:
                    pool.wait_ge(self.part_low.sem, self.part_low.at(len(self.prep)))
                    pool.wait_ge(self.v_turned.sem, self.v_turned.at(4))
                    pool.dma_start(h[:, :, :], h_kept).then_inc(h_back.sem, 16)

        class Merge(Stage):
            def __init__(self, layer, T, branch):
                self.l, self.T, self.branch = layer, T, branch
                self.high = signals.new("merged_high_made", KT)
                self.low = signals.new("merged_low_made", KT)

            def tensor(self, pe):
                pe.wait_ge(self.branch.y_ready.sem, self.branch.y_ready.at(self.branch.y_count))
                for c in range(BT):
                    self.branch.mix_unit(pe, c)

            def scalar(self, act):
                for c in range(BT):
                    n = self.branch.n_mix + c
                    split_next(act, split_high, n, n)
                    if c == 0:
                        act.wait_ge(self.branch.o_low.sem, self.branch.o_low.at(self.branch.J))
                    for m in (2 * c, 2 * c + 1):
                        act.wait_ge(self.branch.merged.sem, self.branch.merged.at(m + 1))
                        act.activation(a_high[:, m, 0:self.T], acc[:, m, 0:self.T], ACT.Copy, scale=0.5).then_inc(self.high.sem, 1)

            def vector(self, dve):
                for c in range(BT):
                    n = self.branch.n_mix + c
                    split_next(dve, split_low, n, n)
                    self.branch.merge(dve, c)
                    for m in (2 * c, 2 * c + 1):
                        dve.wait_ge(self.high.sem, self.high.at(m + 1))
                        dve.scalar_tensor_tensor(out=a_low[:, m, 0:self.T], in0=acc[:, m, 0:self.T], scalar=0.5, in1=a_high[:, m, 0:self.T],
                                                 op0=ALU.mult, op1=ALU.subtract).then_inc(self.low.sem, 1)

        class Out(Result):
            def __init__(self, layer, T, merge):
                self.n0, self.T, self.merge = STARTS[layer, "out"], T, merge
                self.result_signals()

            def tensor(self, pe):
                for m in range(KT):
                    if past(m - 1):
                        pe.wait_ge(self.copied.sem, self.copied.at(m - 1))
                    n = self.n0 + m
                    product(pe, n, n, [(ps[:, m % 2, 0:self.T], [(k, k) for k in range(KT)])],
                            lambda k: a_high[:, k, 0:self.T], lambda k: a_low[:, k, 0:self.T],
                            before=(lambda k: pe.wait_ge(self.merge.low.sem, self.merge.low.at(k + 1))) if m == 0 else None)

            def scalar(self, act):
                for m in range(KT):
                    n = self.n0 + m
                    split_next(act, split_high, n, n)
                    act.wait_ge(used.sem, n + 1)
                    self.take(act, m, m % 2)

            def vector(self, dve):
                for m in range(KT):
                    n = self.n0 + m
                    split_next(dve, split_low, n, n)
                    self.add(dve, m, m % 2)

        h_ready = None
        stages.append(Modulation())
        for layer in range(DEPTH):
            last = layer == DEPTH - 1
            for j in range(3):
                T = S_ALL if j < 2 or not last else S_X
                norm = Norm(layer, j, T, h_ready)
                stages.append(norm)
                if j == 1:
                    T = S_X if last else S_ALL
                    branches = []
                    for i in range(len(BRANCHES)):
                        branches.append(Branch(layer, i, T, norm, branches[-1] if branches else None))
                    stages += branches
                    merge = Merge(layer, T, branches[-1])
                    stages.append(merge)
                    result = Out(layer, T, merge)
                else:
                    hidden = Hidden(layer, j, T, norm)
                    stages.append(hidden)
                    result = Down(layer, j, T, hidden)
                stages.append(result)
                residual = Residual(layer, j, T, result)
                stages.append(residual)
                h_ready = residual.h_ready
        if stop:
            del stages[stop:]

        block = ctx.enter_context(nc.Block())

        @block.sync
        def _(sp):
            sp.dma_start(smalls[:, :], small).then_inc(loaded.sem, 16)
            sp.dma_start(h[:, :, :], tokens).then_inc(loaded.sem, 16)
            for i in range(MOD_FIRST):
                for n in range(MOD_GROUP * i, MOD_GROUP * (i + 1)):
                    sp.dma_start(first_raw[n][:, :, :].rearrange("p a b -> p (a b)"), weights[n]).then_inc(first_landed[i].sem, 16)
            for layer in range(DEPTH):
                units = layer_units(layer)
                for stretch in STRETCHES:
                    names = [name for name, _ in units if name in stretch]
                    n, count = STARTS[layer, names[0]], sum(u for name, u in units if name in stretch)
                    widths = [UNIT] * SLOTS
                    if names[0].startswith("down"):
                        widths = [DOWN_WIDTH if narrow(u) else UNIT for u in (DOWN_BESIDE if beside(layer) else DOWN_ALONE)]

                    def step(i, n=n, widths=widths):
                        for c, width in enumerate(widths):
                            fetch(sp, n + c + len(widths) * i, width, c % SLOTS)
                    assert n % SLOTS == 0 and count % len(widths) == 0
                    repeat(sp, count // len(widths), step)
            for k in range(KT):
                sp.wait_ge(h_ready.sem, h_ready.at(k + 1))
                sp.dma_start(out[:, k], h[:, k, 0:S_X]).then_inc(stored.sem, 16)
            sp.wait_ge(stored.sem, 16 * KT)

        @block.gpsimd
        def _(pool):
            pool.memset(ones[:, :], 1.0).then_inc(ones_set.sem, 1)
            pool.memset(eps[:, :], EPS).then_inc(ones_set.sem, 1)
            for st in stages:
                st.pool(pool)

        @block.scalar
        def _(act):
            act.wait_ge(ones_set.sem, ones_set.at(2))
            act.wait_ge(loaded.sem, loaded.at(32))
            stages[1].statistics(act)
            for n in range(AHEAD):
                split_high(act, n, n)
            for st in stages:
                st.scalar(act)

        @block.vector
        def _(dve):
            for n in range(AHEAD):
                split_low(dve, n, n)
            dve.wait_ge(loaded.sem, loaded.at(32))
            for st in stages:
                st.vector(dve)

        @block.tensor
        def _(pe):
            pe.wait_ge(ones_set.sem, ones_set.at(2))
            pe.wait_ge(loaded.sem, loaded.at(32))
            stages[1].sums(pe)
            for st in stages:
                st.tensor(pe)


def segments_of_w_in():
    widths = [("a_q", BW), ("a_k", BW), ("a_v", BW), ("b_q", BW), ("b_k", BW), ("b_v", BW),
              ("c_q", BW), ("c_k", P), ("c_v", P), ("d_q", BW), ("d_k", P), ("d_v", P)] + [(f"gate{i}", D) for i in range(4)]
    seg, at = {}, 0
    for name, w in widths:
        seg[name] = slice(at, at + w)
        at += w
    return seg


GQA_ORDER = np.concatenate([np.arange(HD) + HD * hh for t in range(4) for hh in (t, 4 + t)])


def k8(w):
    n = w.shape[1] // P
    return w.reshape(KT, P, n, P).transpose(2, 1, 0, 3).reshape(n, P, UNIT)


def lay_out(inp):
    a = {k: np.asarray(v) for k, v in inp.items()}
    f = np.float32
    tokens = np.concatenate([a["x"][0], a["ctx"][0]]).T.reshape(KT, P, S_ALL).transpose(1, 0, 2)
    _, total = unit_starts()
    weights = np.zeros((total, P, UNIT), f)
    n = 0
    seg = segments_of_w_in()

    def put(units):
        nonlocal n
        for unit in units:
            weights[n, :, :unit.shape[-1]] = unit
            n += 1
    w_mod = a["w_mod"].reshape(DEPTH, 4, 2, P, -1, MOD_GROUP * P).transpose(0, 4, 1, 3, 2, 5).reshape(-1, P, UNIT)
    mods = iter(w_mod)

    def put_beside(units, pattern):
        own = iter(units)
        for _ in range(len(units) // sum(e is not None for e in pattern)):
            put(next(own) if e is not None else next(mods) for e in pattern)
    put(next(mods) for _ in range(MOD_GROUP * MOD_FIRST))
    for l in range(DEPTH):
        def ffn(j):
            both = np.stack([k8(a["ffn_w_gate"][l, j]), k8(a["ffn_w_up"][l, j])], 1)
            put_beside(both.reshape(2 * FT, P, UNIT), UP_BESIDE if beside(l) else UP_ALONE)
            w = a["ffn_w_down"][l, j].reshape(FT, P, KT, P)
            units = []
            for m in range(KT):
                k0 = 0
                for nk in DOWN_K:
                    units.append(w[k0:k0 + nk, :, m].transpose(1, 0, 2).reshape(P, nk * P))
                    k0 += nk
            put_beside(units, DOWN_BESIDE if beside(l) else DOWN_ALONE)
        ffn(0)
        w_in = a["w_in"][l]
        projections, gates, mixes = [], [], []
        for i, b in enumerate(BRANCHES.lower()):
            q, wb = w_in[:, seg[b + "_q"]], a["w_branch"][l, i]
            if b in "cd":
                q, wb = q[:, GQA_ORDER], wb[GQA_ORDER]
            projections.append(np.concatenate([k8(q), k8(w_in[:, seg[b + "_k"]]), k8(w_in[:, seg[b + "_v"]])]))
            gates.append(k8(w_in[:, seg[f"gate{i}"]]))
            mixes.append(wb.reshape(BT, P, 4, 2, P).transpose(2, 1, 3, 0, 4).reshape(4, P, UNIT))
        put(projections[0])
        for i in range(4):
            put(gates[i])
            if i < 3:
                put(projections[i + 1])
            put(mixes[i])
        put(k8(a["w_out"][l]))
        ffn(1)
    assert n == total
    s = {}
    s["c"] = np.stack([a["c"][0].reshape(KT, P), a["c_ctx"].reshape(KT, P)], -1).transpose(1, 0, 2)
    s["b_mod"] = np.broadcast_to(a["b_mod"].reshape(DEPTH * MODT, P).T[:, :, None], (P, DEPTH * MODT, 2))
    s["gain"] = a["norm_gain"].reshape(DEPTH, 6, KT, P).transpose(3, 0, 1, 2)
    s["lam"] = np.broadcast_to(a["diff_lambda"].reshape(1, -1), (P, DEPTH * 4 * HD))
    s["subln"] = a["diff_subln"].T
    s["qk_gain"] = np.concatenate([a["qk_norm"]] * 2, -1).transpose(2, 0, 1)
    s["sink"] = np.broadcast_to(a["sink"].reshape(1, DEPTH, 2, 4).transpose(0, 1, 3, 2).reshape(1, -1), (P, DEPTH * 8))
    t = np.arange(S_X)
    inv = (f(10000.0) ** (-np.arange(HD // 4, dtype=f) / f(HD // 4))).astype(f)
    ang = np.stack([(t // GRID_W).astype(f)[:, None] * inv, (t % GRID_W).astype(f)[:, None] * inv], 1)
    cos, sin = np.cos(ang), np.sin(ang)
    row = np.arange(P) % HD
    part, half, fr = row // 32, row % 32 // 16, row % 16
    s["cos"] = cos[:, part, fr].T
    s["sin"] = (sin[:, part, fr] * np.where(half, 1, -1)).T
    s["ident"] = np.eye(P)
    s["pairs"] = np.kron(np.eye(2), np.ones((HD, HD)))
    pick = np.zeros((P, 2))
    pick[[0, 2], 0] = pick[[1, 3], 1] = 1
    s["pick"] = pick
    q, k = np.arange(P)[:, None], np.arange(P)[None]
    m = np.stack([np.where(k + P - q <= SWA_WINDOW, 0, MASKED), np.where(q + P - k <= SWA_WINDOW, 0, MASKED)], 1)
    s["mask"] = np.stack([m, m], 2)
    small = np.concatenate([np.asarray(s[name]).reshape(P, w).astype(f) for name, (_, w) in SMALL.items()], 1)
    rows = S_X // GRID_W
    kh = min(NA_KH, rows)
    r, c = t // GRID_W, t % GRID_W
    r0, c0 = np.clip(r - kh // 2, 0, rows - kh), np.clip(c - NA_KW // 2, 0, GRID_W - NA_KW)
    inside = ((r[None] >= r0[:, None]) & (r[None] < r0[:, None] + kh) & (c[None] >= c0[:, None]) & (c[None] < c0[:, None] + NA_KW))
    dr = np.where(inside, r[None] - r[:, None] + NA_KH - 1, 0)
    dc = np.where(inside, c[None] - c[:, None] + NA_KW - 1, 0)
    na = np.where(inside, a["na_bias"][:, :, dr, dc], f(MASKED))
    na = na.reshape(DEPTH, 4, 2, 2, P, S_X).transpose(0, 1, 3, 4, 2, 5).reshape(DEPTH, 8, P, 2, S_X)
    return {"tokens": tokens, "small": small, "weights": weights, "na_rows": na}


def kernel(**inputs):
    import concourse.bacc as bacc
    from concourse.bass_utils import run_bass_kernel_spmd

    nc = bacc.Bacc("TRN2", target_bir_lowering=False, num_devices=1)
    arrays, args = {}, []
    for name, v in lay_out(inputs).items():
        v = np.ascontiguousarray(v, dtype=np.float32)
        arrays[f"in_{name}"] = v
        args.append(nc.dram_tensor(f"in_{name}", v.shape, F32, kind="ExternalInput").ap())
    args.append(nc.dram_tensor("h_kept", (P, KT, S_ALL), F32, kind="Internal").ap())
    args.append(nc.dram_tensor("out_tokens", (P, KT, S_X), F32, kind="ExternalOutput").ap())
    build(nc, *args)
    r = run_bass_kernel_spmd(nc, [arrays], core_ids=[0])
    got = r.results[0]["out_tokens"]
    return got.transpose(1, 0, 2).reshape(D, S_X).T.reshape(1, S_X, D)
```
